# Optimizing a Trainium2 kernel written in Bass

```python
import math
import jax, jax.numpy as jnp
from jax import lax
import numpy as np

D_MODEL = 1024
BATCH = 1
SEQ = 1024
DEPTH = 2

ATTN_WIDTH = D_MODEL // 2
CONV_CHANNELS = D_MODEL - ATTN_WIDTH
V_HEAD_DIM = 64
N_HEADS = ATTN_WIDTH // V_HEAD_DIM
QK_NOPE_DIM = 64
QK_ROPE_DIM = 32
QK_HEAD_DIM = QK_NOPE_DIM + QK_ROPE_DIM
Q_LORA_RANK = 384
KV_LORA_RANK = 256
CONV_GROUPS = 8
CONV_KERNEL = 3
D_FF = 4 * D_MODEL
PLE_DIM = 256
ROPE_THETA = 10000.0
Q_BLOCK = 128
EPS = 1e-6
IN_SPLITS = (Q_LORA_RANK, KV_LORA_RANK, QK_ROPE_DIM, CONV_CHANNELS, CONV_CHANNELS, CONV_CHANNELS)
IN_WIDTH = sum(IN_SPLITS)

kernel_name = "hybrid_mla_shortconv_sandwich_encoder"

def rms_norm(x, g):
    xf = x.astype(jnp.float32)
    y = xf * lax.rsqrt(jnp.mean(xf * xf, axis=-1, keepdims=True) + EPS)
    return (y * g.astype(jnp.float32)).astype(x.dtype)

def group_rms_norm(x, g, n_groups):
    b, s, w = x.shape
    y = rms_norm(x.reshape(b, s, n_groups, w // n_groups), g.reshape(n_groups, w // n_groups))
    return y.reshape(b, s, w)

def rope_tables(seq):
    inv_freq = 1.0 / (ROPE_THETA ** (jnp.arange(0, QK_ROPE_DIM, 2, dtype=jnp.float32) / QK_ROPE_DIM))
    ang = jnp.arange(seq, dtype=jnp.float32)[:, None] * inv_freq[None, :]
    return jnp.cos(ang), jnp.sin(ang)

def apply_rope(x, cos, sin):
    half = QK_ROPE_DIM // 2
    c = cos.astype(x.dtype)
    s = sin.astype(x.dtype)
    x1, x2 = x[..., :half], x[..., half:]
    return jnp.concatenate([x1 * c - x2 * s, x2 * c + x1 * s], axis=-1)

def latent_attention(q_nope, q_rope, k_nope, k_rope, v):
    b, s, h, _ = q_nope.shape
    nb = s // Q_BLOCK
    qn = q_nope.reshape(b, nb, Q_BLOCK, h, QK_NOPE_DIM).transpose(1, 0, 2, 3, 4)
    qr = q_rope.reshape(b, nb, Q_BLOCK, h, QK_ROPE_DIM).transpose(1, 0, 2, 3, 4)
    scale = 1.0 / math.sqrt(QK_HEAD_DIM)

    def one_block(args):
        qn_b, qr_b = args
        sc = (jnp.einsum('bqhd,bkhd->bhqk', qn_b, k_nope, preferred_element_type=jnp.float32)
              + jnp.einsum('bqhr,bkr->bhqk', qr_b, k_rope, preferred_element_type=jnp.float32))
        w = jax.nn.softmax(sc * scale, axis=-1)
        return jnp.einsum('bhqk,bkhd->bqhd', w.astype(v.dtype), v)

    o = lax.map(one_block, (qn, qr))
    return o.transpose(1, 0, 2, 3, 4).reshape(b, s, h * V_HEAD_DIM)

def short_conv(u, w):
    return lax.conv_general_dilated(
        u, w[:, None, :].astype(u.dtype), window_strides=(1,), padding=((1, 1),),
        dimension_numbers=('NWC', 'WIO', 'NWC'), feature_group_count=u.shape[-1])

def setup_inputs(seed: int = 0) -> dict:
    key = jax.random.key(seed)
    ks = jax.random.split(key, 24)
    f32 = jnp.float32

    def w(k, shape, fan_in):
        return jax.random.normal(k, shape, f32) * (fan_in ** -0.5)

    def gain(k, dim):
        return 1.0 + 0.02 * jax.random.normal(k, (DEPTH, dim), f32)

    return {
        "x": jax.random.normal(ks[0], (BATCH, SEQ, D_MODEL), f32),
        "p": jax.random.normal(ks[1], (DEPTH, BATCH, SEQ, PLE_DIM), f32),
        "g_pre_mix": gain(ks[2], D_MODEL),
        "w_in": w(ks[3], (DEPTH, D_MODEL, IN_WIDTH), D_MODEL),
        "g_q_a": gain(ks[4], Q_LORA_RANK),
        "w_q_b": w(ks[5], (DEPTH, Q_LORA_RANK, N_HEADS * QK_HEAD_DIM), Q_LORA_RANK),
        "g_kv_a": gain(ks[6], KV_LORA_RANK),
        "w_kv_b": w(ks[7], (DEPTH, KV_LORA_RANK, N_HEADS * (QK_NOPE_DIM + V_HEAD_DIM)), KV_LORA_RANK),
        "w_conv": w(ks[8], (DEPTH, CONV_KERNEL, CONV_CHANNELS), CONV_KERNEL),
        "g_attn_out": gain(ks[9], ATTN_WIDTH),
        "g_conv_out": gain(ks[10], CONV_CHANNELS),
        "w_out": w(ks[11], (DEPTH, ATTN_WIDTH + CONV_CHANNELS, D_MODEL), ATTN_WIDTH + CONV_CHANNELS),
        "g_post_mix": gain(ks[12], D_MODEL),
        "g_pre_mlp": gain(ks[13], D_MODEL),
        "w_mlp_up": w(ks[14], (DEPTH, D_MODEL, D_FF), D_MODEL),
        "w_mlp_down": w(ks[15], (DEPTH, D_FF, D_MODEL), D_FF),
        "g_post_mlp": gain(ks[16], D_MODEL),
        "g_pre_ple": gain(ks[17], D_MODEL),
        "w_ple_gate": w(ks[18], (DEPTH, D_MODEL, D_MODEL), D_MODEL),
        "w_ple_proj": w(ks[19], (DEPTH, PLE_DIM, D_MODEL), PLE_DIM),
        "g_post_ple": gain(ks[20], D_MODEL),
    }

def reference(x, p, g_pre_mix, w_in, g_q_a, w_q_b, g_kv_a, w_kv_b, w_conv, g_attn_out,
              g_conv_out, w_out, g_post_mix, g_pre_mlp, w_mlp_up, w_mlp_down, g_post_mlp,
              g_pre_ple, w_ple_gate, w_ple_proj, g_post_ple):
    b, s, _ = x.shape
    cos, sin = rope_tables(s)
    split_at = list(np.cumsum(IN_SPLITS)[:-1])

    for i in range(DEPTH):
        h = rms_norm(x, g_pre_mix[i])
        z = h @ w_in[i]
        z_qa, z_kva, z_kr, gate_b, gate_c, conv_in = jnp.split(z, split_at, axis=-1)

        q = (rms_norm(z_qa, g_q_a[i]) @ w_q_b[i]).reshape(b, s, N_HEADS, QK_HEAD_DIM)
        q_nope = q[..., :QK_NOPE_DIM]
        q_rope = apply_rope(q[..., QK_NOPE_DIM:], cos[:, None, :], sin[:, None, :])
        kv = (rms_norm(z_kva, g_kv_a[i]) @ w_kv_b[i]).reshape(b, s, N_HEADS, QK_NOPE_DIM + V_HEAD_DIM)
        k_nope = kv[..., :QK_NOPE_DIM]
        v = kv[..., QK_NOPE_DIM:]
        k_rope = apply_rope(z_kr, cos, sin)
        attn = latent_attention(q_nope, q_rope, k_nope, k_rope, v)

        conv = gate_b * short_conv(gate_c * conv_in, w_conv[i])

        mix = jnp.concatenate([group_rms_norm(attn, g_attn_out[i], N_HEADS),
                               group_rms_norm(conv, g_conv_out[i], CONV_GROUPS)], axis=-1)
        x = x + rms_norm(mix @ w_out[i], g_post_mix[i])

        hm = rms_norm(x, g_pre_mlp[i])
        f = jnp.square(jax.nn.relu(hm @ w_mlp_up[i])) @ w_mlp_down[i]
        x = x + rms_norm(f, g_post_mlp[i])

        gate = jax.nn.sigmoid(rms_norm(x, g_pre_ple[i]) @ w_ple_gate[i])
        e = p[i] @ w_ple_proj[i]
        x = x + rms_norm(gate * e, g_post_ple[i])

    return x


_drawn_inputs = setup_inputs


def setup_inputs(seed=0):
    import zlib

    import numpy as np

    out = dict(_drawn_inputs(seed))
    spreads = {}
    factors = {'g_q_a': 5.512,
     'g_kv_a': 3.125,
     'g_attn_out': 4.783,
     'g_conv_out': 5.129,
     'g_post_mix': 3.526,
     'g_pre_mlp': 3.687,
     'g_post_mlp': 4.165,
     'g_pre_ple': 8.0,
     'g_post_ple': 4.534}
    for name, (base, spread) in spreads.items():
        noise = np.random.default_rng([zlib.crc32(name.encode()), seed]).standard_normal(out[name].shape)
        drawn = base * np.exp(spread * noise) if base else spread * noise
        out[name] = __import__('jax').numpy.asarray(drawn.astype(out[name].dtype))
    for name, factor in factors.items():
        out[name] = (out[name] * factor).astype(out[name].dtype)
    return out
```

```python
import math
from contextlib import ExitStack

import concourse.bass as bass
import numpy as np
from concourse import mybir

DEPTH, SEQ, D = 2, 1024, 1024
P = 128
HALF = 512
DC = D // P
HEADS, NOPE, ROPE, V_DIM = 8, 64, 32, 64
QK = NOPE + ROPE
Q_RANK, KV_RANK = 384, 256
QC, KVC = Q_RANK // P, KV_RANK // P
CONV = 512
D_FF = 4096
PLE = 256
EPS = 1e-6
UNIT = 1024
SLOTS = 4
RAW = 2

PAIRS = HEADS // 2
IN_UNITS = QC + KVC + 1 + 3 * (CONV // P)
OUT_UNITS = DC
GROUPS = D_FF // (2 * P)
MLP_UNITS = 4 * GROUPS
E_UNITS = 2
GATE_UNITS = DC
O_AT = IN_UNITS
M_AT = O_AT + OUT_UNITS
E_AT = M_AT + MLP_UNITS
G_AT = E_AT + E_UNITS
UNITS = G_AT + GATE_UNITS
PAIR_SLOT = (IN_UNITS - 1) % SLOTS

IN_KIND = ([("q", c) for c in range(QC)] + [("kv", c) for c in range(KVC)]
           + [(k, j) for j in range(3) for k in ("C", "u", "B")] + [("kr", 0), ("C", 3), ("u", 3), ("B", 3)])
IN_BLOCKS = [list(range(a, min(a + SLOTS, IN_UNITS))) for a in range(0, IN_UNITS, SLOTS)]
IN_OUTS = [(u, t) for b in IN_BLOCKS for t in range(2) for u in b]
OUT_OUTS = [(m, t) for b in (range(4), range(4, 8)) for t in range(2) for m in b]
GATE_OUTS = [(m, t) for b in ((0, 1), (2, 3, 4, 5), (6, 7)) for t in range(2) for m in b]
BY_ACT = ("C", "B")
BY_DVE = ("q", "kv", "kr")


def outputs_of(kinds, n):
    return sum(IN_KIND[u][0] in kinds for u, _ in IN_OUTS[:n])


CHUNKS = CONV // P
MULT_AT = [15, 22, 29, 35]
CSTAT_AT = [17, 24, 31, 36]
CY_AT = [18, 25, 32, 37]
CLO_AT = [19, 26, 33, 38]
LSQ_AT = [13, 13, 18, 19]
LSTAT_AT = [15, 16, 20, 21]
LF_AT = [16, 17, 21, 22]
LY_AT = [17, 18, 22, 23]
LORA = [range(QC), range(QC, QC + KVC)]

AHEAD = [("pre", -1, t, c) for t in range(2) for c in range(DC)]
OUT_TAIL = [("out", n) for n in range(13)] + [("factor", 0)] + [("pre", 0, 0, c) for c in range(3)]
OUT_TAIL += [("out", 13)] + [("pre", 0, 0, c) for c in range(3, 6)] + [("out", 14)]
OUT_TAIL += [("pre", 0, 0, c) for c in range(6, 8)] + [("out", 15), ("factor", 1)]
OUT_TAIL += [("pre", 0, 1, c) for c in range(8)]
SQUARES = [("lora", i, 0, c) for i in range(4) for c in LORA[i % 2]]
SQUARES += [e if e[0] == "pre" else ("post", 0) + OUT_OUTS[e[1]][::-1] for e in OUT_TAIL if e[0] != "factor"]
SQUARES += [("post", 1, t, c) for t in range(2) for c in range(DC)]
SQUARES += [("pre", 1, t, c) for t in range(2) for c in range(DC)]
SQUARES += [("post", 2, t, m) for m, t in GATE_OUTS]
SQUARES += [("pre", 2, t, c) for t in range(2) for c in range(DC)]


def is_first(e):
    return e[3] == (QC if e[0] == "lora" and e[1] % 2 else 0)


def square_number(e):
    return (AHEAD if e in AHEAD else SQUARES).index(e)


def sum_number(e):
    where = AHEAD if e in AHEAD else SQUARES
    return sum(not is_first(o) for o in where[:where.index(e)])


SUMS = sum(not is_first(e) for e in SQUARES)
SUMS_AHEAD = sum(not is_first(e) for e in AHEAD)
assert SUMS % 2 == 0 and SUMS_AHEAD % 2 == 0

G_Q, G_KV, G_ATT, G_CONV = 0, 3, 5, 9
G_POST = [13, 29, 45]
G_PRE = [21, 37, 53]
G_TAP = 61
G_FIRST = 73
G_ALL = 81


def encoder(nc, x_in, w_units, w_pair, w_v, p_in, gains, table, consts, out):
    f32, f32r = mybir.dt.float32, mybir.dt.float32r
    ALU, ACT, AX = mybir.AluOpType, mybir.ActivationFunctionType, mybir.AxisListType
    SCALE = 1.0 / math.sqrt(QK)
    ctx = ExitStack()

    def sb(name, shape, dt, where=ctx):
        return where.enter_context(nc.sbuf_tensor(name, shape, dt))

    def sem(name):
        return ctx.enter_context(nc.semaphore(name))

    def dram(name, shape, dt):
        return nc.dram_tensor(name, shape, dt, kind="Internal").ap()

    def hs(t):
        return slice(t * HALF, (t + 1) * HALF)

    with ctx:
        raw = sb("raw", [P, RAW, UNIT], f32)
        wh = sb("wh", [P, SLOTS, 8, P], f32r)
        wl = sb("wl", [P, SLOTS, 8, P], f32r)
        stage = sb("stage", [P, UNIT], f32)
        hh = sb("hh", [P, DC, SEQ], f32r)
        hl = sb("hl", [P, DC, SEQ], f32r)
        rpre = sb("rpre", [P, 2, HALF], f32)
        sq = sb("sq", [P, 2, HALF], f32)
        accy = sb("accy", [P, 2, HALF], f32)
        xacc = sb("xacc", [P, HALF], f32)
        tmp = sb("tmp", [P, HALF], f32)
        gv = sb("gv", [P, G_ALL], f32)
        cst = sb("cst", [P, 5, P], f32)
        eps = sb("eps", [P, 1], f32)
        carry = sb("carry", [P, 1], f32)
        mx = sb("mx", [P, 2], f32)
        nm = sb("nm", [P, 2], f32)
        ident, ones, blocks = cst[:, 0, :], cst[:, 1, :], cst[:, 2, :]
        HA, HB = 5, 7

        with ExitStack() as att:
            kh = sb("kh", [QK, 2, SEQ], f32r, att)
            kl = sb("kl", [QK, 2, SEQ], f32r, att)
            tab = sb("tab", [P, SEQ], f32, att)
            with ExitStack() as inp:
                zr = sb("zr", [P, QC + KVC, SEQ], f32, inp)
                cc = sb("cc", [P, SEQ], f32, inp)
                uu = sb("uu", [P, SEQ + 2], f32, inp)
                bb = sb("bb", [P, 2, SEQ], f32, inp)
                cv = sb("cv", [P, SEQ], f32, inp)
                cvs = sb("cvs", [P, 2, HALF], f32, inp)
                cvr = sb("cvr", [P, 2, HALF], f32, inp)
                cyh = sb("cyh", [P, SEQ], f32r, inp)
                cyl = sb("cyl", [P, SEQ], f32r, inp)
                kr = sb("kr", [QK, HALF], f32, inp)
            vh = sb("vh", [P, 8, 3 * V_DIM], f32r, att)
            vl = sb("vl", [P, 8, 3 * V_DIM], f32r, att)
            pr = sb("pr", [P, 2, SEQ], f32, att)
            pth = sb("pth", [P, 2, 8, 256], f32r, att)
            ptl = sb("ptl", [P, 2, 8, 256], f32r, att)
            of = sb("of", [P, HALF], f32, att)
            yh = sb("yh", [P, HALF], f32r, att)
            yl = sb("yl", [P, HALF], f32r, att)
        x = sb("x", [P, DC, SEQ], f32)
        facc = sb("facc", [P, DC, SEQ], f32)
        gh = sb("gh", [P, 2, SEQ], f32r)
        gl = sb("gl", [P, 2, SEQ], f32r)

        ps = ctx.enter_context(nc.psum_tensor("ps", [P, 8, HALF], f32))
        mix_hi = dram("mix_hi", [8, P, SEQ], f32)
        mix_lo = dram("mix_lo", [8, P, SEQ], f32)

        const_in = sem("const_in")
        eps_set = sem("eps_set")
        gains_in = sem("gains_in")
        tab_in = sem("tab_in")
        w_in = [sem(f"w_in{i}") for i in range(RAW)]
        w_hi = sem("w_hi")
        w_lo = sem("w_lo")
        stage_in = sem("stage_in")
        stage_hi = sem("stage_hi")
        stage_lo = sem("stage_lo")
        x_back = sem("x_back")
        x_stored = sem("x_stored")
        squared = sem("squared")
        summed = sem("summed")
        pre_hi = sem("pre_hi")
        pre_lo = sem("pre_lo")
        pre_stat = sem("pre_stat")
        pre_ln = sem("pre_ln")
        pre_r = sem("pre_r")
        post_stat = sem("post_stat")
        post_ln = sem("post_ln")
        post_r = sem("post_r")
        post_mul = sem("post_mul")
        x_new = sem("x_new")
        in_out = sem("in_out")
        in_act = sem("in_act")
        in_dve = sem("in_dve")
        kr_cos = sem("kr_cos")
        kr_sum = sem("kr_sum")
        kr_f = sem("kr_f")
        kr_hi = sem("kr_hi")
        kr_lo = sem("kr_lo")
        u_raw = sem("u_raw")
        u_once = sem("u_once")
        u_done = sem("u_done")
        pads = sem("pads")
        tap = sem("tap")
        cv_raw = sem("cv_raw")
        cv_done = sem("cv_done")
        cv_sq = sem("cv_sq")
        cv_stat = sem("cv_stat")
        cv_ln = sem("cv_ln")
        cv_r = sem("cv_r")
        cv_y = sem("cv_y")
        cv_hi = sem("cv_hi")
        cv_lo = sem("cv_lo")
        mix_stored = sem("mix_stored")
        lr_stat = sem("lr_stat")
        lr_ln = sem("lr_ln")
        lr_r = sem("lr_r")
        lr_y = sem("lr_y")
        lr_hi = sem("lr_hi")
        lr_lo = sem("lr_lo")
        v_ones = sem("v_ones")
        kv_out = sem("kv_out")
        v_hi = sem("v_hi")
        v_lo = sem("v_lo")
        k_f = sem("k_f")
        k_hi = sem("k_hi")
        k_lo = sem("k_lo")
        q_out = sem("q_out")
        q_cos = sem("q_cos")
        q_sin = sem("q_sin")
        q_f = sem("q_f")
        q_hi = sem("q_hi")
        q_lo = sem("q_lo")
        s_out = sem("s_out")
        s_max = sem("s_max")
        s_neg = sem("s_neg")
        s_exp = sem("s_exp")
        t_out = sem("t_out")
        t_hi = sem("t_hi")
        t_lo = sem("t_lo")
        pv_out = sem("pv_out")
        o_sq = sem("o_sq")
        o_copy = sem("o_copy")
        o_var = sem("o_var")
        o_ln = sem("o_ln")
        o_r = sem("o_r")
        o_y = sem("o_y")
        o_hi = sem("o_hi")
        o_lo = sem("o_lo")
        mix_in = sem("mix_in")
        mix_last = sem("mix_last")
        mix_out = sem("mix_out")
        mix_copy = sem("mix_copy")
        up_out = sem("up_out")
        up_v = sem("up_v")
        up_sq = sem("up_sq")
        up_hi = sem("up_hi")
        up_lo = sem("up_lo")
        down_out = sem("down_out")
        down_add = sem("down_add")
        f_zero = sem("f_zero")
        e_out = sem("e_out")
        e_copy = sem("e_copy")
        gate_out = sem("gate_out")
        gate_z = sem("gate_z")
        gate_s = sem("gate_s")
        gate_y = sem("gate_y")

        NORMS = 3

        def pre_at(L, k):
            return L * NORMS + (k + 1)

        def post_at(L, k):
            return L * NORMS + k

        def last_read(L, w, g=0):
            if w < O_AT:
                return in_out, L * len(IN_OUTS) + IN_OUTS.index((w, 1)) + 1
            if w < M_AT:
                return mix_out, L * 16 + OUT_OUTS.index((w - O_AT, 1)) + 1
            if w < M_AT + 2:
                return up_out, (L * GROUPS + g) * 4 + 3 + (w - M_AT)
            if w < M_AT + 4:
                return down_out, (L * GROUPS + g) * 16 + 12 + 4 * (w - M_AT - 2)
            if w < G_AT:
                return e_out, L * 16 + 12 + 4 * (w - E_AT)
            return gate_out, L * 16 + GATE_OUTS.index((w - G_AT, 1)) + 1

        def slot_free(L, w, g=0):
            if w == O_AT + 3:
                return q_out, (L + 1) * 4 * PAIRS
            if not isinstance(g, int):
                return last_read(L, w, g - 1)
            if M_AT <= w < E_AT:
                return last_read(L, w, g - 1) if g > 0 else last_read(L, w - SLOTS)
            if E_AT <= w < E_AT + SLOTS:
                return last_read(L, M_AT + w - E_AT, GROUPS - 1)
            return last_read(L, w - SLOTS)

        gatt = gv[:, G_ATT:G_ATT + PAIRS]

        def pair_of(v, b):
            return v[:, 4 * b:4 * b + 4, :].rearrange("p c (a d) -> p c a d", a=3)[:, :, 0:3:2, :]

        def square_at(L, e):
            return square_number(e) + 1 + (0 if L is None else L * len(SQUARES) + len(AHEAD))

        def sum_at(L, e):
            return sum_number(e) + 1 + (0 if L is None else L * SUMS + SUMS_AHEAD)

        def sum_of(e):
            kind, k, t, c = e
            if kind == "pre":
                return (xacc, tmp)[t][:, :]
            return accy[:, k % 2 if kind == "lora" else t, :]

        def last_of(kind, k, t):
            if kind == "lora":
                return (kind, k, 0, LORA[k % 2][-1])
            return (kind, k, t, DC - 1)

        block = ctx.enter_context(nc.Block())

        @block.sync
        def _(sp):
            def load(L, w, g=0):
                sp.wait_ge(w_lo, L * UNITS + g * 4 + w + 1)
                sp.dma_start(raw[:, w % RAW, :],
                             w_units[bass.ds(L, 1), bass.ds(g * 4 + w, 1), :, :].rearrange("a b p n -> p (a b n)")
                             ).then_inc(w_in[w % RAW], 16)

            def load_stage(L, k, src):
                sp.wait_ge(stage_lo, L * 7 + k + 1)
                sp.dma_start(stage[:, :], src).then_inc(stage_in, 16)

            sp.dma_start(cst[:, :, :], consts).then_inc(const_in, 16)
            sp.dma_start(gv[:, :], gains[0]).then_inc(const_in, 16)
            for t in range(2):
                sp.dma_start(x[:, :, hs(t)], x_in[:, :, hs(t)]).then_inc(const_in, 16)
            sp.wait_ge(const_in, 64)
            for t in range(2):
                sp.dma_start(out[:, :, hs(t)], x[:, :, hs(t)]).then_inc(x_stored, 16)

            with sp.Fori(0, DEPTH) as L:
                load(L, 0)
                load(L, 1)
                sp.wait_ge(pre_lo, pre_at(L, -1) * 16 + 16)
                sp.dma_start(gv[:, :], gains[bass.ds(L, 1), :, :].rearrange("a p n -> p (a n)")).then_inc(gains_in, 16)
                sp.wait_ge(squared, square_at(L, SQUARES[0]) - 1)
                sp.wait_ge(x_stored, L * 32 + 32)
                sp.dma_start(tab[:, :], table).then_inc(tab_in, 16)
                load_stage(L, 0, w_v[bass.ds(L, 1), :, :].rearrange("a p n -> p (a n)"))

                def store_conv(j):
                    sp.wait_ge(cv_lo, L * 8 + 2 * j + 2)
                    sp.dma_start(mix_hi[4 + j], cyh[:, :].bitcast(f32)).then_inc(mix_stored, 16)
                    sp.dma_start(mix_lo[4 + j], cyl[:, :].bitcast(f32)).then_inc(mix_stored, 16)

                stores_before = {15: 0, 18: 1, 22: 2}
                for w in range(2, O_AT + 5):
                    if w in stores_before:
                        store_conv(stores_before[w])
                    load(L, w)

                def pair_unit(j):
                    load_stage(L, j + 1, w_pair[bass.ds(L, 1), bass.ds(j, 1), :, :].rearrange("a b p n -> p (a b n)"))

                def store_attention(j):
                    for t in range(2):
                        sp.wait_ge(o_lo, L * 8 + j * 2 + t + 2)
                        for src, dst in ((yh, mix_hi), (yl, mix_lo)):
                            sp.dma_start(dst[bass.ds(j, 1), :, hs(t)].rearrange("a p n -> p (a n)"), src[:, :].bitcast(f32)).then_inc(mix_stored, 16)

                pair_unit(0)
                store_conv(3)
                with sp.Fori(0, PAIRS - 1) as j:
                    pair_unit(j + 1)
                    store_attention(j)

                def load_mix(c, done):
                    sp.dma_start(hh[:, c, :].bitcast(f32), mix_hi[c]).then_inc(done, 16)
                    sp.dma_start(hl[:, c, :].bitcast(f32), mix_lo[c]).then_inc(done, 16)

                sp.wait_ge(q_out, L * 16 + 16)
                sp.wait_ge(mix_stored, L * 384 + 320)
                for c in (4, 7, 0, 1, 2):
                    load_mix(c, mix_in)
                sp.wait_ge(s_out, L * 64 + 64)
                for c in (5, 6):
                    load_mix(c, mix_in)
                store_attention(PAIRS - 1)
                sp.wait_ge(mix_stored, L * 384 + 384)
                load_mix(3, mix_last)
                sp.wait_ge(mix_copy, L * 16 + 1)
                sp.dma_start(x[:, :, :], out[:, :, :]).then_inc(x_back, 16)
                for w in range(O_AT + 5, M_AT):
                    load(L, w)
                with sp.Fori(0, GROUPS) as g:
                    for i in range(4):
                        load(L, M_AT + i, g)
                load_stage(L, 5, p_in[bass.ds(L, 1), 0, :, :].rearrange("a p n -> p (a n)"))
                for w in range(E_AT, G_AT + 2):
                    load(L, w)
                load_stage(L, 6, p_in[bass.ds(L, 1), 1, :, :].rearrange("a p n -> p (a n)"))
                for w in range(G_AT + 2, UNITS):
                    load(L, w)
                for t in range(2):
                    sp.wait_ge(x_new, post_at(L, 2) * 16 + t * 8 + 8)
                    sp.dma_start(out[:, :, hs(t)], x[:, :, hs(t)]).then_inc(x_stored, 16)
            sp.wait_ge(x_stored, 32 * (DEPTH + 1))
            sp.wait_ge(mix_stored, 384 * DEPTH)

        @block.tensor
        def _(pe):
            def split_product(dst, ah, al, bh, bl, start, stop):
                nc.tensor.matmul(dst, ah, bh, start=start, stop=False)
                nc.tensor.matmul(dst, ah, bl, start=False, stop=False)
                return nc.tensor.matmul(dst, al, bh, start=False, stop=stop)

            def unit_output(bank, slot, t, ready=None, order=range(DC)):
                for n, k in enumerate(order):
                    if ready is not None:
                        ready(k)
                    last = split_product(ps[:, bank, :], wh[:, slot, k, :], wl[:, slot, k, :],
                                         hh[:, k, hs(t)], hl[:, k, hs(t)], n == 0, n == DC - 1)
                return last

            def two_tiles(bank, slot, m, t):
                for k in range(2):
                    tile = 2 * (m % 4) + k
                    last = split_product(ps[:, bank, :], wh[:, slot, tile, :], wl[:, slot, tile, :],
                                         gh[:, k, hs(t)], gl[:, k, hs(t)], k == 0, k == 1)
                return last

            def unit_ready(L, w, g=0):
                pe.wait_ge(w_lo, L * UNITS + g * 4 + w + 1 + RAW)

            def pre_stats(L, k, t):
                if k == -1:
                    pe.wait_ge(summed, L * SUMS + SUMS_AHEAD - (1 - t) * (DC - 1))
                else:
                    pe.wait_ge(summed, sum_at(L, last_of("pre", k, t)))
                if t == 1:
                    pe.wait_ge(pre_ln, pre_at(L, k) * 2 + 1)
                nc.tensor.matmul(ps[:, 7, :], ones, (xacc, tmp)[t][:, :], start=True, stop=True).then_inc(pre_stat, 1)

            def post_stats(L, k, t):
                pe.wait_ge(summed, sum_at(L, last_of("post", k, t)))
                if t == 1:
                    pe.wait_ge(post_ln, post_at(L, k) * 2 + 1)
                nc.tensor.matmul(ps[:, 6, :], ones, accy[:, t, :], start=True, stop=True).then_inc(post_stat, 1)

            def pre_ready(R, t):
                return lambda k: pe.wait_ge(pre_lo, R * 16 + t * 8 + k + 1)

            pe.wait_ge(const_in, 64)
            with pe.Fori(0, DEPTH) as L:
                R = pre_at(L, -1)

                def conv_stat(j, t):
                    pe.wait_ge(cv_sq, L * 8 + 2 * j + t + 1)
                    if j:
                        pe.wait_ge(cv_ln, L * 8 + 2 * j + t - 1)
                    nc.tensor.matmul(ps[:, 4 + t, :], blocks, cvs[:, t, :], start=True, stop=True).then_inc(cv_stat, 1)

                def lora_stat(i):
                    pe.wait_ge(summed, sum_at(L, last_of("lora", i, 0)))
                    if i:
                        pe.wait_ge(lr_ln, L * 4 + i)
                    nc.tensor.matmul(ps[:, 6, :], ones, accy[:, i % 2, :], start=True, stop=True).then_inc(lr_stat, 1)

                for n in range(len(IN_OUTS) + 1):
                    if n < len(IN_OUTS):
                        u, t = IN_OUTS[n]
                        if t == 0:
                            unit_ready(L, u)
                        if n >= 4:
                            kind = IN_KIND[IN_OUTS[n - 4][0]][0]
                            if kind in BY_ACT:
                                pe.wait_ge(in_act, L * 16 + outputs_of(BY_ACT, n - 3))
                            elif kind == "u":
                                pe.wait_ge(u_raw, L * 8 + outputs_of("u", n - 3))
                            else:
                                pe.wait_ge(in_dve, L * 12 + outputs_of(BY_DVE, n - 3))
                        ready = pre_ready(R, t) if n in (0, 4) else None
                        unit_output(n % 4, u % SLOTS, t, ready).then_inc(in_out, 1)
                        if n in (0, 4):
                            pre_stats(L, -1, t)
                    for i in range(4):
                        if LSTAT_AT[i] == n:
                            lora_stat(i)
                    for j in range(CHUNKS):
                        if CSTAT_AT[j] == n:
                            conv_stat(j, 0)
                            conv_stat(j, 1)

                with pe.Fori(0, PAIRS) as j:
                    J = L * PAIRS + j
                    pe.wait_ge(v_ones, L * 2 + 2)
                    pe.wait_ge(cv_ln, L * 8 + 8)
                    pe.wait_ge(lr_lo, L * 5 + 5)
                    pe.wait_ge(stage_lo, L * 7 + 2)
                    for b in range(2):
                        for c4 in range(4):
                            tok = slice((4 * b + c4) * P, (4 * b + c4 + 1) * P)
                            dst = ps[:, 6 + b, c4 * P:(c4 + 1) * P]
                            for k in range(KVC):
                                cols = bass.ds(j * P + k * HALF, P)
                                last = split_product(dst, hh[:, QC + k, tok], hl[:, QC + k, tok],
                                                     hh[:, HB, cols], hl[:, HB, cols], k == 0, k == KVC - 1)
                        last.then_inc(kv_out, 1)
                    pe.wait_ge(stage_lo, L * 7 + j + 3)
                    for t in range(2):
                        for k in range(KVC):
                            last = split_product(ps[:, 4 + t, :], wh[:, PAIR_SLOT, 6 + k, :], wl[:, PAIR_SLOT, 6 + k, :],
                                                 hh[:, QC + k, hs(t)], hl[:, QC + k, hs(t)], k == 0, k == KVC - 1)
                        last.then_inc(kv_out, 1)
                    for n in range(4):
                        t, a = n // 2, n % 2
                        if n < 2:
                            pe.wait_ge(v_lo, J * 2 + n + 1)
                        else:
                            pe.wait_ge(k_f, J * 4 + 2 * (n - 2) + 2)
                        for k in range(QC):
                            last = split_product(ps[:, (6, 7, 4, 5)[n], :], wh[:, PAIR_SLOT, 3 * a + k, :], wl[:, PAIR_SLOT, 3 * a + k, :],
                                                 hh[:, k, hs(t)], hl[:, k, hs(t)], k == 0, k == QC - 1)
                        last.then_inc(q_out, 1)

                    def scores(s):
                        t, a, i = s // 8, (s // 4) % 2, s % 4
                        if s % 4 == 0:
                            pe.wait_ge(q_lo, J * 4 + 2 * t + a + 1)
                        if s == 0:
                            pe.wait_ge(k_lo, J * 4 + 4)
                        if s >= 2:
                            pe.wait_ge(s_exp, J * 16 + s - 1)
                        tok = slice(t * HALF + i * P, t * HALF + (i + 1) * P)
                        for kb in range(2):
                            last = split_product(ps[:, 2 * (s % 2) + kb, :], hh[0:QK, HA + a, tok], hl[0:QK, HA + a, tok],
                                                 kh[:, a, hs(kb)], kl[:, a, hs(kb)], True, True)
                        last.then_inc(s_out, 1)

                    def transposes(s):
                        pe.wait_ge(s_exp, J * 16 + s + 1)
                        if s == 0:
                            pe.wait_ge(q_sin, J * 4 + 4)
                        for b in range(2):
                            if s >= 1:
                                pe.wait_ge(t_lo, J * 32 + 2 * (s - 1) + b + 1)
                            for c in range(4):
                                last = nc.tensor.transpose(ps[:, 4 + b, c * P:(c + 1) * P],
                                                           pr[:, s % 2, (4 * b + c) * P:(4 * b + c + 1) * P], ident)
                            last.then_inc(t_out, 1)

                    def values(G, part):
                        a, half = (G // 2) % 2, G % 2
                        if part == 0:
                            pe.wait_ge(t_lo, J * 32 + 4 * G + 4)
                            if G == 4:
                                pe.wait_ge(o_copy, J * 4 + 1)
                            if G == 6:
                                pe.wait_ge(o_ln, J * 2 + 1)
                        dst = ps[:, 6 + a, half * 256:(half + 1) * 256]
                        for c in range(4 * part, 4 * part + 4):
                            last = split_product(dst, vh[:, c, a * V_DIM:a * V_DIM + P], vl[:, c, a * V_DIM:a * V_DIM + P],
                                                 pth[:, G % 2, c, :], ptl[:, G % 2, c, :], c == 0, c == 7)
                        if part == 1:
                            last.then_inc(pv_out, 1)

                    def variances(t):
                        pe.wait_ge(o_copy, J * 4 + 2 * t + 2)
                        nc.tensor.matmul(ps[:, 7, :], cst[:, 3, :], sq[:, 0, :], start=True, stop=False)
                        nc.tensor.matmul(ps[:, 7, :], cst[:, 4, :], sq[:, 1, :], start=False, stop=True).then_inc(o_var, 1)

                    scores(0)
                    scores(1)
                    for s in range(16):
                        transposes(s)
                        if s + 2 < 16:
                            scores(s + 2)
                        if s == 10:
                            variances(0)
                        if s >= 2:
                            values((s - 2) // 2, s % 2)
                    values(7, 0)
                    values(7, 1)
                    variances(1)
                    pe.wait_ge(o_ln, J * 2 + 2)

                for n, (m, t) in enumerate(OUT_OUTS):
                    if t == 0:
                        unit_ready(L, O_AT + m)
                    if n >= 4:
                        pe.wait_ge(mix_copy, L * 16 + n - 3)

                    def mix_ready(k, n=n):
                        if n == 0 and k == 4:
                            pe.wait_ge(mix_in, (L + 1) * 224)
                        if n == 0 and k == 3:
                            pe.wait_ge(mix_last, (L + 1) * 32)
                    unit_output(n % 4, (O_AT + m) % SLOTS, t, mix_ready, (4, 7, 0, 1, 2, 5, 6, 3)).then_inc(mix_out, 1)
                    if n == 12:
                        post_stats(L, 0, 0)
                post_stats(L, 0, 1)

                def up(g, t, ready=None, after=None):
                    for i in range(2):
                        n = 2 * t + i
                        if t == 0:
                            unit_ready(L, M_AT + i, g)
                        if not isinstance(g, int):
                            pe.wait_ge(up_v, L * 4 * GROUPS + (g - 1) * 4 + n + 1)
                        unit_output(n, (M_AT + i) % SLOTS, t, ready).then_inc(up_out, 1)
                        if i == 0 and after:
                            after()
                        ready = None

                def down(g, t, banks=4, first=False, between={}):
                    pe.wait_ge(up_lo, L * 4 * GROUPS + g * 4 + 2 * t + 2)
                    for m in range(DC):
                        if t == 0 and m % 4 == 0:
                            unit_ready(L, M_AT + 2 + m // 4, g)
                        before = L * 16 * GROUPS + g * 16 + t * 8 + m
                        if m >= banks or (banks == 4 and not first):
                            pe.wait_ge(down_add, before - banks + 1)
                        elif not first:
                            pe.wait_ge(down_add, before - m)
                        two_tiles(4 + m % banks, (M_AT + 2 + m // 4) % SLOTS, m, t).then_inc(down_out, 1)
                        if m in between:
                            between[m]()

                R = pre_at(L, 0)
                up(0, 0, pre_ready(R, 0), lambda: pre_stats(L, 0, 0))
                up(0, 1, pre_ready(R, 1))
                pre_stats(L, 0, 1)
                pe.wait_ge(pre_ln, R * 2 + 2)
                down(0, 0, first=True)
                with pe.Fori(1, GROUPS) as g:
                    up(g, 0)
                    down(g - 1, 1)
                    up(g, 1)
                    down(g, 0)
                down(GROUPS - 1, 1, banks=2, between={4: lambda: post_stats(L, 1, 0)})

                def embed(t, ms):
                    for m in ms:
                        if t == 0 and m % 4 == 0:
                            unit_ready(L, E_AT + m // 4)
                        n = t * 8 + m
                        if n in (8, 9):
                            pe.wait_ge(gate_z, L * 16 + n - 7)
                        elif n >= 4:
                            pe.wait_ge(e_copy, L * 16 + n - 3)
                        two_tiles(m % 4, (E_AT + m // 4) % SLOTS, m, t).then_inc(e_out, 1)

                def gate(n):
                    m, t = GATE_OUTS[n]
                    if t == 0:
                        unit_ready(L, G_AT + m)
                    bank = n % 4 if n >= 4 else n % 2
                    if n < 2:
                        pe.wait_ge(e_copy, L * 16 + 5 + n)
                    elif n < 4:
                        pe.wait_ge(e_copy, L * 16 + 13 + n - 2)
                    elif n < 6:
                        pe.wait_ge(gate_z, L * 16 + n - 1)
                    elif n < 8:
                        pe.wait_ge(e_copy, L * 16 + 9 + n)
                    else:
                        pe.wait_ge(gate_z, L * 16 + n - 3)
                    ready = pre_ready(pre_at(L, 1), t) if n in (0, 2) else None
                    unit_output(bank, (G_AT + m) % SLOTS, t, ready).then_inc(gate_out, 1)

                pe.wait_ge(stage_lo, L * 7 + 8)
                embed(0, range(4))
                post_stats(L, 1, 1)
                embed(0, range(4, 8))
                gate(0)
                pre_stats(L, 1, 0)
                gate(1)
                embed(1, range(8))
                gate(2)
                pre_stats(L, 1, 1)
                for n in range(3, 16):
                    gate(n)
                    if n == 14:
                        post_stats(L, 2, 0)
                post_stats(L, 2, 1)

        @block.scalar
        def _(act):
            def table_of_exp_and_ln():
                nc.scalar.add_instruction(mybir.InstLoadActFuncSet(
                    name=nc.get_next_instruction_name(), act_func_set_id=6, ins=[], outs=[],
                    engine=mybir.EngineType.Activation))

            def copy(dst, src, **more):
                return nc.scalar.activation(dst, src, ACT.Copy, **more)

            def split_unit(L, w, g=0):
                act.wait_ge(w_in[w % RAW], (L * (UNITS // RAW) + g * (4 // RAW) + w // RAW) * 16 + 16)
                if w >= SLOTS:
                    act.wait_ge(*slot_free(L, w, g))
                copy(wh[:, w % SLOTS, :, :].rearrange("p k m -> p (k m)"), raw[:, w % RAW, :]).then_inc(w_hi, 1)

            def split_stage(L, k, dst):
                act.wait_ge(stage_in, (L * 7 + k) * 16 + 16)
                copy(dst, stage[:, :]).then_inc(stage_hi, 1)

            def square(L, e, src):
                k = sum_number(e)
                if is_first(e):
                    dst = sum_of(e)
                else:
                    if L is not None or k >= 2:
                        act.wait_ge(summed, sum_at(L, e) - 2)
                    dst = sq[:, k % 2, :]
                nc.scalar.activation(dst, src, ACT.Square).then_inc(squared, 1)

            def factor(dst, bank, width, stat, ln, r, count, bias=eps):
                act.wait_ge(stat, count)
                more = {} if bias is None else {"bias": bias[:, :]}
                nc.scalar.activation(dst, ps[:, bank, :], ACT.Ln, scale=1.0 / width, **more).then_inc(ln, 1)
                act.wait_ge(ln, count)
                nc.scalar.activation(dst, dst, ACT.Exp, scale=-0.5).then_inc(r, 1)

            def pre_factor(L, k, t):
                factor(rpre[:, t, :], 7, D, pre_stat, pre_ln, pre_r, pre_at(L, k) * 2 + t + 1)

            def post_factor(L, k, t):
                factor(accy[:, t, :], 6, D, post_stat, post_ln, post_r, post_at(L, k) * 2 + t + 1)

            def pre_chunk(L, k, t, c):
                g_at = G_FIRST if L is None else G_PRE[k]
                if L is not None:
                    act.wait_ge(x_new, post_at(L, k) * 16 + t * 8 + c + 1)
                copy(hh[:, c, hs(t)], x[:, c, hs(t)], scale=gv[:, g_at + c:g_at + c + 1]).then_inc(pre_hi, 1)
                square(L, ("pre", k, t, c), x[:, c, hs(t)])

            table_of_exp_and_ln()
            act.wait_ge(const_in, 64)
            act.wait_ge(eps_set, 1)
            for t in range(2):
                for c in range(DC):
                    pre_chunk(None, -1, t, c)
            with act.Fori(0, DEPTH) as L:
                for w in range(SLOTS):
                    split_unit(L, w)
                factor(rpre[:, 0, :], 7, D, pre_stat, pre_ln, pre_r, pre_at(L, -1) * 2 + 1)
                act.wait_ge(x_stored, L * 32 + 32)
                act.wait_ge(pre_lo, pre_at(L, -1) * 16 + 16)

                for n in range(len(IN_OUTS) + 4):
                    u, t = IN_OUTS[n] if n < len(IN_OUTS) else (None, None)
                    kind, j = IN_KIND[u] if u is not None else (None, None)
                    if kind == "C":
                        act.wait_ge(in_out, L * 36 + n + 1)
                        if j:
                            act.wait_ge(u_raw, L * 8 + 2 * (j - 1) + t + 1)
                        copy(cc[:, hs(t)], ps[:, n % 4, :]).then_inc(in_act, 1)
                    if kind == "B":
                        act.wait_ge(in_out, L * 36 + n + 1)
                        if j >= 2:
                            act.wait_ge(cv_raw, L * 4 + j - 1)
                        copy(bb[:, j % 2, hs(t)], ps[:, n % 4, :]).then_inc(in_act, 1)
                    if n == 4:
                        factor(rpre[:, 1, :], 7, D, pre_stat, pre_ln, pre_r, pre_at(L, -1) * 2 + 2)
                    if kind == "kr":
                        act.wait_ge(kr_f, L * 2 + t + 1)
                        for a in range(2):
                            copy(kh[NOPE:QK, a, hs(t)], kr[NOPE:QK, :]).then_inc(kr_hi, 1)
                    for i in range(4):
                        if LF_AT[i] == n:
                            rank = KV_RANK if i % 2 else Q_RANK
                            factor(accy[:, i % 2, :], 6, rank, lr_stat, lr_ln, lr_r, L * 4 + i + 1)
                    for i in range(4):
                        if LSQ_AT[i] == n:
                            if i == 0:
                                act.wait_ge(in_dve, L * 12 + outputs_of(BY_DVE, 13))
                            if i >= 2:
                                act.wait_ge(lr_y, L * 10 + (3, 5)[i - 2])
                            for c in LORA[i % 2]:
                                square(L, ("lora", i, 0, c), zr[:, c, hs(i // 2)])
                    for j in range(CHUNKS):
                        if MULT_AT[j] + 1 == n:
                            for t2 in range(2):
                                act.wait_ge(cv_done, L * 8 + 2 * j + t2 + 1)
                                nc.scalar.activation(cvs[:, t2, :], cv[:, hs(t2)], ACT.Square).then_inc(cv_sq, 1)
                        if CSTAT_AT[j] + 1 == n:
                            for t2 in range(2):
                                factor(cvr[:, t2, :], 4 + t2, 64, cv_stat, cv_ln, cv_r, L * 8 + 2 * j + t2 + 1)
                        if CY_AT[j] + 1 == n:
                            if j:
                                act.wait_ge(mix_stored, L * 384 + 32 * j)
                            for t2 in range(2):
                                act.wait_ge(cv_y, L * 8 + 2 * j + t2 + 1)
                                copy(cyh[:, hs(t2)], cv[:, hs(t2)]).then_inc(cv_hi, 1)
                    if t == 1 and u + SLOTS < O_AT + 3:
                        split_unit(L, u + SLOTS)
                    if n == len(IN_OUTS) - 1:
                        act.wait_ge(in_out, L * 36 + 36)
                        act.wait_ge(lr_y, L * 10 + 10)
                        for c in (3, 4, 0, 1, 2):
                            copy(hh[:, c, :], zr[:, c, :]).then_inc(lr_hi, 1)
                            if c == 4:
                                split_stage(L, 0, hh[:, HB, :])

                with act.Fori(0, PAIRS) as j:
                    J = L * PAIRS + j
                    act.wait_ge(*last_read(L, IN_UNITS - 1))

                    split_stage(L, j + 1, wh[:, PAIR_SLOT, :, :].rearrange("p k m -> p (k m)"))
                    for b in range(2):
                        act.wait_ge(kv_out, J * 4 + b + 1)
                        copy(pair_of(vh, b), ps[:, 6 + b, :].rearrange("p (c a d) -> p c a d", c=4, a=2)).then_inc(v_hi, 1)
                    for t in range(2):
                        act.wait_ge(kv_out, J * 4 + t + 3)
                        for a in range(2):
                            if t == 1:
                                act.wait_ge(k_lo, J * 4 + a + 1)
                            copy(accy[0:NOPE, a, :], ps[a * NOPE:(a + 1) * NOPE, 4 + t, :]).then_inc(k_f, 1)
                            act.wait_ge(k_f, J * 4 + 2 * t + a + 1)
                            copy(kh[0:NOPE, a, hs(t)], accy[0:NOPE, a, :]).then_inc(k_hi, 1)
                    for n in range(4):
                        t, a = n // 2, n % 2
                        act.wait_ge(q_f, J * 4 + n + 1)
                        copy(hh[0:QK, HA + a, hs(t)], (tmp, xacc)[n % 2][0:QK, :]).then_inc(q_hi, 1)

                    def exponentials(s):
                        act.wait_ge(s_neg, J * 16 + s + 1)
                        if s >= 2:
                            act.wait_ge(t_out, J * 32 + 2 * (s - 2) + 2)
                        nc.scalar.activation(pr[:, s % 2, :], ps[:, 2 * (s % 2):2 * (s % 2) + 2, :].rearrange("p b n -> p (b n)"),
                                             ACT.Exp, bias=nm[:, s % 2:s % 2 + 1], scale=SCALE).then_inc(s_exp, 1)

                    def high_of_transposed(s):
                        G = s // 2
                        for b in range(2):
                            act.wait_ge(t_out, J * 32 + 2 * s + b + 1)
                            if s == 0:
                                act.wait_ge(mix_stored, L * 384 + 128)
                            if G >= 2 and s % 2 == 0 and b == 0:
                                act.wait_ge(pv_out, J * 8 + G - 1)
                            copy(pth[:, G % 2, 4 * b:4 * b + 4, (s % 2) * P:(s % 2 + 1) * P],
                                 ps[:, 4 + b, :].rearrange("p (c q) -> p c q", c=4)).then_inc(t_hi, 1)

                    def outputs(t, a):
                        act.wait_ge(pv_out, J * 8 + 2 * (2 * t + a) + 2)
                        if t == 1:
                            act.wait_ge(o_var, J * 2 + 1)
                        if a == 0:
                            act.wait_ge(o_lo, J * 2 + t + 1)
                        nc.scalar.activation(sq[:, a, :], ps[:, 6 + a, :], ACT.Square).then_inc(o_sq, 1)
                        copy(of[a * V_DIM:(a + 1) * V_DIM, :], ps[a * V_DIM:(a + 1) * V_DIM, 6 + a, :]).then_inc(o_copy, 1)

                    def high_of_output(t):
                        act.wait_ge(o_y, J * 2 + t + 1)
                        act.wait_ge(mix_stored, L * 384 + 128 + j * 64 + 32 * t)
                        copy(yh[:, :], of[:, :]).then_inc(o_hi, 1)

                    exponentials(0)
                    exponentials(1)
                    for s in range(16):
                        high_of_transposed(s)
                        if s + 2 < 16:
                            exponentials(s + 2)
                        if s == 5:
                            outputs(0, 0)
                        if s == 9:
                            outputs(0, 1)
                        if s == 10:
                            factor(tmp[:, :], 7, V_DIM, o_var, o_ln, o_r, J * 2 + 1, None)
                        if s == 11:
                            high_of_output(0)
                        if s == 13:
                            outputs(1, 0)
                    outputs(1, 1)
                    factor(tmp[:, :], 7, V_DIM, o_var, o_ln, o_r, J * 2 + 2, None)
                    high_of_output(1)
                split_unit(L, O_AT + 3)

                for e in OUT_TAIL:
                    if e[0] == "out":
                        m, t = OUT_OUTS[e[1]]
                        act.wait_ge(mix_out, L * 16 + e[1] + 1)
                        if e[1] == 0:
                            act.wait_ge(mix_stored, L * 384 + 384)
                        copy(facc[:, m, hs(t)], ps[:, e[1] % 4, :]).then_inc(mix_copy, 1)
                        act.wait_ge(mix_copy, L * 16 + e[1] + 1)
                        square(L, ("post", 0, t, m), facc[:, m, hs(t)])
                        if t == 1:
                            split_unit(L, O_AT + m + SLOTS)
                    elif e[0] == "factor":
                        post_factor(L, 0, e[1])
                    else:
                        pre_chunk(L, *e[1:])
                        if e == ("pre", 0, 1, 3):
                            pre_factor(L, 0, 0)

                def hidden(g, t):
                    for i in range(2):
                        k = L * 4 * GROUPS + g * 4 + 2 * t + i
                        act.wait_ge(up_v, k + 1)
                        nc.scalar.activation(gh[:, i, hs(t)], accy[:, 1, :], ACT.Square).then_inc(up_hi, 1)
                        nc.scalar.activation(accy[:, 0, :], accy[:, 1, :], ACT.Square).then_inc(up_sq, 1)

                def split_two(g, at):
                    for i in range(2):
                        split_unit(L, M_AT + at + i, g)

                hidden(0, 0)
                pre_factor(L, 0, 1)
                hidden(0, 1)
                split_two(1, 0)
                with act.Fori(1, GROUPS) as g:
                    hidden(g, 0)
                    split_two(g, 2)
                    hidden(g, 1)
                    split_two(g + 1, 0)
                for t in range(2):
                    for c in range(DC):
                        act.wait_ge(down_add, (L + 1) * 16 * GROUPS - 16 + 8 * t + c + 1)
                        square(L, ("post", 1, t, c), facc[:, c, hs(t)])
                split_stage(L, 5, gh[:, 0, :])
                split_unit(L, G_AT)
                split_unit(L, G_AT + 1)
                post_factor(L, 1, 0)
                split_stage(L, 6, gh[:, 1, :])

                def embedding(t, c):
                    act.wait_ge(e_out, L * 16 + t * 8 + c + 1)
                    copy(facc[:, c, hs(t)], ps[:, c % 4, :]).then_inc(e_copy, 1)

                def gates(n):
                    m, t = GATE_OUTS[n]
                    act.wait_ge(gate_z, L * 16 + n + 1)
                    nc.scalar.activation(xacc[:, :], xacc[:, :], ACT.Sigmoid).then_inc(gate_s, 1)
                    act.wait_ge(gate_y, L * 16 + n + 1)
                    square(L, ("post", 2, t, m), facc[:, m, hs(t)])
                    w = G_AT + m + SLOTS
                    if t == 1 and w < UNITS:
                        split_unit(L, w)

                for c in range(DC):
                    pre_chunk(L, 1, 0, c)
                    embedding(0, c)
                post_factor(L, 1, 1)
                for c in range(DC):
                    pre_chunk(L, 1, 1, c)
                pre_factor(L, 1, 0)
                gates(0)
                gates(1)
                for c in range(DC):
                    embedding(1, c)
                split_unit(L, G_AT + 2)
                split_unit(L, G_AT + 3)
                table_of_exp_and_ln()
                pre_factor(L, 1, 1)
                for n in range(2, 16):
                    gates(n)
                table_of_exp_and_ln()
                for t in range(2):
                    post_factor(L, 2, t)
                    for c in range(DC):
                        pre_chunk(L, 2, t, c)

        @block.vector
        def _(dve):
            V = nc.vector

            def low(dst, whole, high):
                return V.tensor_tensor(dst, whole, high.bitcast(f32), ALU.subtract)

            def split_unit(L, w, g=0):
                dve.wait_ge(w_hi, L * UNITS + g * 4 + w + 1)
                low(wl[:, w % SLOTS, :, :].rearrange("p k m -> p (k m)"), raw[:, w % RAW, :],
                    wh[:, w % SLOTS, :, :].rearrange("p k m -> p (k m)")).then_inc(w_lo, 1)

            def split_stage(L, k, dst, high):
                dve.wait_ge(stage_hi, L * 7 + k + 1)
                low(dst, stage[:, :], high).then_inc(stage_lo, 1)

            def pre_low(L, k, t, c):
                g_at = G_FIRST if L is None else G_PRE[k]
                R = 0 if L is None else pre_at(L, k)
                dve.wait_ge(pre_hi, R * 16 + t * 8 + c + 1)
                V.scalar_tensor_tensor(hl[:, c, hs(t)], x[:, c, hs(t)], gv[:, g_at + c:g_at + c + 1],
                                       hh[:, c, hs(t)].bitcast(f32), ALU.mult, ALU.subtract).then_inc(pre_lo, 1)

            def residual(L, k, splits={}):
                R = post_at(L, k)
                for t in range(2):
                    dve.wait_ge(post_r, R * 2 + t + 1)
                    for c in range(DC):
                        i = R * 16 + t * 8 + c + 1
                        f, xc = facc[:, c, hs(t)], x[:, c, hs(t)]
                        V.scalar_tensor_tensor(f, f, gv[:, G_POST[k] + c:G_POST[k] + c + 1], accy[:, t, :],
                                               ALU.mult, ALU.mult).then_inc(post_mul, 1)
                        dve.wait_ge(post_mul, i)
                        V.tensor_tensor(xc, xc, f, ALU.add).then_inc(x_new, 1)
                        if c:
                            pre_low(L, k, t, c - 1)
                        if (t, c) in splits:
                            split_unit(L, splits[t, c])
                    pre_low(L, k, t, DC - 1)

            V.memset(eps[:, :], EPS).then_inc(eps_set, 1)
            V.memset(mx[:, :], 0.0).then_inc(w_lo, RAW)
            V.memset(nm[:, 0:1], 0.0).then_inc(stage_lo, 1)
            V.memset(nm[:, 1:2], 0.0).then_inc(o_lo, 1)
            dve.wait_ge(const_in, 64)
            for t in range(2):
                for c in range(DC):
                    pre_low(None, -1, t, c)
            with dve.Fori(0, DEPTH) as L:
                for w in range(SLOTS):
                    split_unit(L, w)
                dve.wait_ge(x_stored, L * 32 + 32)
                dve.wait_ge(squared, square_at(L, SQUARES[0]) - 1)
                dve.wait_ge(tab_in, L * 16 + 16)
                dve.wait_ge(gains_in, L * 16 + 16)
                dve.wait_ge(pads, L * 2 + 2)
                for n in range(len(IN_OUTS) + 5):
                    u, t = IN_OUTS[n] if n < len(IN_OUTS) else (None, None)
                    kind, j = IN_KIND[u] if u is not None else (None, None)
                    if n in (0, 4):
                        dve.wait_ge(pre_r, pre_at(L, -1) * 2 + t + 1)
                    if kind is not None and kind not in BY_ACT:
                        dve.wait_ge(in_out, L * 36 + n + 1)
                    src = ps[:, n % 4, :]
                    if kind in ("q", "kv"):
                        V.tensor_tensor(zr[:, j + (QC if kind == "kv" else 0), hs(t)], src, rpre[:, t, :], ALU.mult).then_inc(in_dve, 1)
                    if kind == "u":
                        dve.wait_ge(in_act, L * 16 + outputs_of(BY_ACT, n))
                        V.tensor_tensor(uu[:, 1 + t * HALF:1 + (t + 1) * HALF], src, cc[:, hs(t)], ALU.mult).then_inc(u_raw, 1)
                    if kind == "kr":
                        rows = slice(NOPE, QK)
                        if t == 1:
                            dve.wait_ge(kr_lo, L * 4 + 2)
                            dve.wait_ge(kr_hi, L * 4 + 2)
                        V.tensor_tensor(sq[rows, 0, :], ps[QK:P, n % 4, :], tab[QK:P, hs(t)], ALU.mult)
                        V.tensor_tensor(kr[rows, :], ps[rows, n % 4, :], tab[rows, hs(t)], ALU.mult).then_inc(kr_cos, 1)
                        dve.wait_ge(kr_cos, L * 2 + t + 1)
                        V.tensor_tensor(kr[rows, :], kr[rows, :], sq[rows, 0, :], ALU.add).then_inc(in_dve, 1)
                        dve.wait_ge(in_dve, L * 12 + outputs_of(BY_DVE, n + 1))
                        V.tensor_tensor(kr[rows, :], kr[rows, :], rpre[rows, t, :], ALU.mult).then_inc(kr_f, 1)
                        for a in range(2):
                            dve.wait_ge(kr_hi, L * 4 + 2 * t + a + 1)
                            low(kl[rows, a, hs(t)], kr[rows, :], kh[rows, a, hs(t)]).then_inc(kr_lo, 1)
                    for i in range(4):
                        if LY_AT[i] == n:
                            dve.wait_ge(lr_r, L * 4 + i + 1)
                            for c in LORA[i % 2]:
                                z = zr[:, c, hs(i // 2)]
                                V.scalar_tensor_tensor(z, z, gv[:, G_Q + c:G_Q + c + 1], accy[:, i % 2, :],
                                                       ALU.mult, ALU.mult).then_inc(lr_y, 1)
                    for j in range(CHUNKS):
                        if CLO_AT[j] + 1 == n:
                            for t2 in range(2):
                                dve.wait_ge(cv_hi, L * 8 + 2 * j + t2 + 1)
                                low(cyl[:, hs(t2)], cv[:, hs(t2)], cyh[:, hs(t2)]).then_inc(cv_lo, 1)
                        if CY_AT[j] == n:
                            for t2 in range(2):
                                dve.wait_ge(cv_r, L * 8 + 2 * j + t2 + 1)
                                V.scalar_tensor_tensor(cv[:, hs(t2)], cv[:, hs(t2)], gv[:, G_CONV + j:G_CONV + j + 1],
                                                       cvr[:, t2, :], ALU.mult, ALU.mult).then_inc(cv_y, 1)
                    for j in range(CHUNKS):
                        if MULT_AT[j] == n:
                            dve.wait_ge(u_done, L * 8 + 2 * j + 2)
                            if j:
                                dve.wait_ge(cv_lo, L * 8 + 2 * j)
                            w = [gv[:, G_TAP + 3 * j + k:G_TAP + 3 * j + k + 1] for k in range(3)]
                            V.tensor_scalar(cv[:, :], uu[:, 1:SEQ + 1], w[1], None, ALU.mult).then_inc(tap, 1)
                            for i, k in ((1, 0), (2, 2)):
                                dve.wait_ge(tap, L * 12 + 3 * j + i)
                                V.scalar_tensor_tensor(cv[:, :], uu[:, k:SEQ + k], w[k], cv[:, :], ALU.mult, ALU.add).then_inc(tap, 1)
                            dve.wait_ge(tap, L * 12 + 3 * j + 3)
                            dve.wait_ge(in_act, L * 16 + outputs_of(BY_ACT, IN_OUTS.index((IN_KIND.index(("B", j)), 1)) + 1))
                            V.tensor_tensor(cv[:, :], cv[:, :], bb[:, j % 2, :], ALU.mult).then_inc(cv_raw, 1)
                    if t == 1 and u + SLOTS < O_AT + 3:
                        split_unit(L, u + SLOTS)
                    if n == len(IN_OUTS) - 1:
                        for i, c in enumerate((3, 4, 0, 1, 2)):
                            dve.wait_ge(lr_hi, L * 5 + i + 1)
                            low(hl[:, c, :], zr[:, c, :], hh[:, c, :]).then_inc(lr_lo, 1)
                            if c == 4:
                                split_stage(L, 0, hl[:, HB, :], hh[:, HB, :])

                with dve.Fori(0, PAIRS) as j:
                    J = L * PAIRS + j
                    split_stage(L, j + 1, wl[:, PAIR_SLOT, :, :].rearrange("p k m -> p (k m)"),
                                wh[:, PAIR_SLOT, :, :].rearrange("p k m -> p (k m)"))
                    for b in range(2):
                        dve.wait_ge(v_hi, J * 2 + b + 1)
                        low(pair_of(vl, b), ps[:, 6 + b, :].rearrange("p (c a d) -> p c a d", c=4, a=2),
                            pair_of(vh, b)).then_inc(v_lo, 1)
                    for t in range(2):
                        for a in range(2):
                            dve.wait_ge(k_hi, J * 4 + 2 * t + a + 1)
                            low(kl[0:NOPE, a, hs(t)], accy[0:NOPE, a, :], kh[0:NOPE, a, hs(t)]).then_inc(k_lo, 1)
                    for n in range(4):
                        t, a, bank = n // 2, n % 2, (6, 7, 4, 5)[n]
                        q = (tmp, xacc)[n % 2]
                        dve.wait_ge(q_out, J * 4 + n + 1)
                        V.tensor_tensor(q[0:QK, :], ps[0:QK, bank, :], tab[0:QK, hs(t)], ALU.mult).then_inc(q_cos, 1)
                        V.tensor_tensor(sq[NOPE:QK, n % 2, :], ps[QK:P, bank, :], tab[QK:P, hs(t)], ALU.mult).then_inc(q_sin, 1)
                        dve.wait_ge(q_sin, J * 4 + n + 1)
                        V.tensor_tensor(q[NOPE:QK, :], q[NOPE:QK, :], sq[NOPE:QK, n % 2, :], ALU.add).then_inc(q_f, 1)
                        dve.wait_ge(q_hi, J * 4 + n + 1)
                        low(hl[0:QK, HA + a, hs(t)], q[0:QK, :], hh[0:QK, HA + a, hs(t)]).then_inc(q_lo, 1)

                    def maxima(s):
                        dve.wait_ge(s_out, J * 16 + s + 1)
                        V.reduce_max(mx[:, s % 2:s % 2 + 1], ps[:, 2 * (s % 2):2 * (s % 2) + 2, :].rearrange("p b n -> p (b n)"),
                                     AX.X).then_inc(s_max, 1)
                        dve.wait_ge(s_max, J * 16 + s + 1)
                        V.tensor_scalar(nm[:, s % 2:s % 2 + 1], mx[:, s % 2:s % 2 + 1], -SCALE, None, ALU.mult).then_inc(s_neg, 1)

                    def low_of_transposed(s):
                        G = s // 2
                        for b in range(2):
                            dve.wait_ge(t_hi, J * 32 + 2 * s + b + 1)
                            at = (slice(None), G % 2, slice(4 * b, 4 * b + 4), slice((s % 2) * P, (s % 2 + 1) * P))
                            V.tensor_tensor(ptl[at], ps[:, 4 + b, :].rearrange("p (c q) -> p c q", c=4),
                                            pth[at].bitcast(f32), ALU.subtract).then_inc(t_lo, 1)

                    def output(t):
                        dve.wait_ge(o_r, J * 2 + t + 1)
                        V.scalar_tensor_tensor(of[:, :], of[:, :], gatt[:, bass.ds(j, 1)], tmp[:, :], ALU.mult, ALU.mult).then_inc(o_y, 1)
                        dve.wait_ge(o_hi, J * 2 + t + 1)
                        low(yl[:, :], of[:, :], yh[:, :]).then_inc(o_lo, 1)

                    maxima(0)
                    maxima(1)
                    for s in range(16):
                        low_of_transposed(s)
                        if s + 2 < 16:
                            maxima(s + 2)
                        if s == 11:
                            output(0)
                    output(1)
                split_unit(L, O_AT + 3)

                for w in range(O_AT + SLOTS, O_AT + 2 * SLOTS + 1):
                    split_unit(L, w)
                dve.wait_ge(x_back, L * 16 + 16)
                residual(L, 0, {(0, 3): M_AT + 1, (0, 6): M_AT + 2, (1, 0): M_AT + 3})

                def hidden(g, t):
                    for i in range(2):
                        k = L * 4 * GROUPS + g * 4 + 2 * t + i
                        dve.wait_ge(up_out, k + 1)
                        V.scalar_tensor_tensor(accy[:, 1, :], ps[:, 2 * t + i, :], 0.0, rpre[:, t, :], ALU.max, ALU.mult).then_inc(up_v, 1)
                        dve.wait_ge(up_sq, k + 1)
                        low(gl[:, i, hs(t)], accy[:, 0, :], gh[:, i, hs(t)]).then_inc(up_lo, 1)

                def add(g, t, banks=4):
                    for m in range(DC):
                        dve.wait_ge(down_out, L * 16 * GROUPS + g * 16 + t * 8 + m + 1)
                        f = facc[:, m, hs(t)]
                        V.tensor_tensor(f, f, ps[:, 4 + m % banks, :], ALU.add).then_inc(down_add, 1)

                def split_two(g, at):
                    for i in range(2):
                        split_unit(L, M_AT + at + i, g)

                dve.wait_ge(pre_r, pre_at(L, 0) * 2 + 1)
                hidden(0, 0)
                dve.wait_ge(pre_r, pre_at(L, 0) * 2 + 2)
                hidden(0, 1)
                split_two(1, 0)
                dve.wait_ge(f_zero, L * 2 + 2)
                add(0, 0)
                with dve.Fori(1, GROUPS) as g:
                    hidden(g, 0)
                    add(g - 1, 1)
                    split_two(g, 2)
                    hidden(g, 1)
                    split_two(g + 1, 0)
                    add(g, 0)
                add(GROUPS - 1, 1, banks=2)
                split_stage(L, 5, gl[:, 0, :], gh[:, 0, :])
                split_unit(L, G_AT)
                split_unit(L, G_AT + 1)
                split_stage(L, 6, gl[:, 1, :], gh[:, 1, :])
                residual(L, 1)

                def gates(n):
                    m, t = GATE_OUTS[n]
                    if n in (0, 2):
                        dve.wait_ge(pre_r, pre_at(L, 1) * 2 + t + 1)
                    dve.wait_ge(gate_out, L * 16 + n + 1)
                    if n:
                        dve.wait_ge(gate_y, L * 16 + n)
                    V.tensor_tensor(xacc[:, :], ps[:, n % 4 if n >= 4 else n % 2, :], rpre[:, t, :], ALU.mult).then_inc(gate_z, 1)
                    dve.wait_ge(gate_s, L * 16 + n + 1)
                    f = facc[:, m, hs(t)]
                    dve.wait_ge(e_copy, L * 16 + t * 8 + m + 1)
                    V.tensor_tensor(f, f, xacc[:, :], ALU.mult).then_inc(gate_y, 1)
                    w = G_AT + m + SLOTS
                    if t == 1 and w < UNITS:
                        split_unit(L, w)

                gates(0)
                gates(1)
                split_unit(L, G_AT + 2)
                split_unit(L, G_AT + 3)
                for n in range(2, 16):
                    gates(n)
                residual(L, 2)

        @block.gpsimd
        def _(pool):
            def add_square(L, e):
                acc = sum_of(e)
                pool.wait_ge(squared, square_at(L, e))
                if L is not None or sum_number(e):
                    pool.wait_ge(summed, sum_at(L, e) - 1)
                nc.gpsimd.tensor_tensor(acc, acc, sq[:, sum_number(e) % 2, :], ALU.add).then_inc(summed, 1)

            pool.wait_ge(eps_set, 1)
            for e in AHEAD:
                if not is_first(e):
                    add_square(None, e)
            with pool.Fori(0, DEPTH) as L:
                pool.wait_ge(x_stored, L * 32 + 32)
                pool.wait_ge(pre_lo, pre_at(L, -1) * 16 + 16)
                pool.wait_ge(squared, square_at(L, SQUARES[0]) - 1)
                nc.gpsimd.tensor_tensor(uu[:, 0:1], eps[:, :], eps[:, :], ALU.subtract).then_inc(pads, 1)
                nc.gpsimd.tensor_tensor(uu[:, SEQ + 1:SEQ + 2], eps[:, :], eps[:, :], ALU.subtract).then_inc(pads, 1)
                for n in range(len(IN_OUTS)):
                    u, t = IN_OUTS[n]
                    kind, j = IN_KIND[u]
                    if kind == "u":
                        k = L * 8 + 2 * j + t + 1
                        piece = uu[:, 1 + t * HALF:1 + (t + 1) * HALF]
                        pool.wait_ge(u_raw, k)
                        nc.gpsimd.tensor_tensor(piece, piece, rpre[:, t, :], ALU.mult).then_inc(u_once, 1)
                        pool.wait_ge(u_once, k)
                        nc.gpsimd.tensor_tensor(piece, piece, rpre[:, t, :], ALU.mult).then_inc(u_done, 1)
                    for j in range(CHUNKS):
                        if MULT_AT[j] == n:
                            pool.wait_ge(cv_raw, L * 4 + j + 1)
                            for t2 in range(2):
                                nc.gpsimd.tensor_tensor(cv[:, hs(t2)], cv[:, hs(t2)], rpre[:, t2, :], ALU.mult).then_inc(cv_done, 1)
                    for i in range(4):
                        if LSQ_AT[i] == n:
                            for c in LORA[i % 2][1:]:
                                add_square(L, ("lora", i, 0, c))
                pool.wait_ge(lr_lo, L * 5 + 5)
                nc.gpsimd.tensor_tensor(carry[:, :], eps[:, :], eps[:, :], ALU.add)
                nc.gpsimd.memset(vh[:, :, V_DIM:2 * V_DIM].bitcast(f32), 1.0).then_inc(v_ones, 1)
                nc.gpsimd.memset(vl[:, :, V_DIM:2 * V_DIM].bitcast(f32), 0.0).then_inc(v_ones, 1)
                for e in SQUARES:
                    if e[0] == "lora":
                        continue
                    if not is_first(e):
                        add_square(L, e)
                    if e[:2] == ("pre", 0) and e[3] == DC - 1:
                        t = e[2]
                        pool.wait_ge(x_new, post_at(L, 0) * 16 + t * 8 + 8)
                        nc.gpsimd.tensor_tensor(carry[:, :], eps[:, :], eps[:, :], ALU.add)
                        nc.gpsimd.memset(facc[:, :, hs(t)], 0.0).then_inc(f_zero, 1)


def kernel(**inputs):
    import concourse.bacc as _bacc
    from concourse.bass_utils import run_bass_kernel_spmd as _run

    a = {k: np.ascontiguousarray(v) for k, v in inputs.items()}

    def tiles(w, rows, cols):
        return np.stack([w[:, r:r + P][:, :, cols] for r in rows], axis=2)

    k_all = range(0, D, P)
    swap = np.r_[ROPE // 2:ROPE, 0:ROPE // 2]
    at_kr = Q_RANK + KV_RANK
    at_b = at_kr + ROPE
    starts = {"q": 0, "kv": Q_RANK, "B": at_b, "C": at_b + CONV, "u": at_b + 2 * CONV}
    units = []
    for kind, c in IN_KIND:
        if kind == "kr":
            kr = at_kr + np.arange(ROPE)
            cols = np.concatenate([kr, kr, kr, kr[swap]])
        else:
            cols = starts[kind] + c * P + np.arange(P)
        units.append(tiles(a["w_in"], k_all, cols))
    for m in range(DC):
        units.append(tiles(a["w_out"], k_all, m * P + np.arange(P)))
    for g in range(GROUPS):
        for i in range(2):
            units.append(tiles(a["w_mlp_up"], k_all, (2 * g + i) * P + np.arange(P)))
        for h in range(2):
            units.append(np.concatenate([tiles(a["w_mlp_down"], (2 * g * P, (2 * g + 1) * P), m * P + np.arange(P))
                                         for m in range(4 * h, 4 * h + 4)], axis=2))
    for h in range(2):
        units.append(np.concatenate([tiles(a["w_ple_proj"], (0, P), m * P + np.arange(P))
                                     for m in range(4 * h, 4 * h + 4)], axis=2))
    for m in range(DC):
        units.append(tiles(a["w_ple_gate"], k_all, m * P + np.arange(P)))
    w_units = np.ascontiguousarray(np.stack(units, axis=1).reshape(DEPTH, UNITS, P, UNIT))

    pairs = []
    for j in range(PAIRS):
        parts = []
        for h in (2 * j, 2 * j + 1):
            nope = h * QK + np.arange(NOPE)
            rope = h * QK + NOPE + np.arange(ROPE)
            parts.append(tiles(a["w_q_b"], range(0, Q_RANK, P), np.concatenate([nope, rope, rope[swap]])))
        cols = np.concatenate([h * (NOPE + V_DIM) + np.arange(NOPE) for h in (2 * j, 2 * j + 1)])
        parts.append(tiles(a["w_kv_b"], range(0, KV_RANK, P), cols))
        pairs.append(np.concatenate(parts, axis=2))
    w_pair = np.ascontiguousarray(np.stack(pairs, axis=1).reshape(DEPTH, PAIRS, P, UNIT))
    v_cols = np.concatenate([h * (NOPE + V_DIM) + NOPE + np.arange(V_DIM) for h in range(HEADS)])
    w_v = np.ascontiguousarray(tiles(a["w_kv_b"], range(0, KV_RANK, P), v_cols).reshape(DEPTH, P, UNIT))

    def columns(v):
        return v.reshape(DEPTH, -1, P).transpose(0, 2, 1)

    following = [(i + 1) % DEPTH for i in range(DEPTH)]
    taps = a["w_conv"].reshape(DEPTH, 3, CHUNKS, P).transpose(0, 3, 2, 1).reshape(DEPTH, P, 3 * CHUNKS)
    gains = np.ascontiguousarray(np.concatenate(
        [columns(a["g_q_a"]), columns(a["g_kv_a"]), columns(a["g_attn_out"]), columns(a["g_conv_out"]),
         columns(a["g_post_mix"]), columns(a["g_pre_mlp"]), columns(a["g_post_mlp"]), columns(a["g_pre_ple"]),
         columns(a["g_post_ple"]), columns(a["g_pre_mix"][following]), taps, columns(a["g_pre_mix"])], axis=2))
    assert gains.shape[2] == G_ALL

    inv_freq = 1.0 / (np.float32(10000.0) ** (np.arange(0, ROPE, 2, dtype=np.float32) / np.float32(ROPE)))
    angle = inv_freq.astype(np.float32)[:, None] * np.arange(SEQ, dtype=np.float32)[None, :]
    cos, sin = np.cos(angle).astype(np.float32), np.sin(angle).astype(np.float32)
    table = np.concatenate([np.ones((NOPE, SEQ), np.float32), cos, cos, -sin, sin], axis=0)
    consts = np.zeros((P, 5, P), np.float32)
    consts[:, 0] = np.eye(P)
    consts[:, 1] = 1.0
    for i in range(2):
        consts[64 * i:64 * i + 64, 2, 64 * i:64 * i + 64] = 1.0
        consts[64 * i:64 * i + 64, 3 + i, 64 * i:64 * i + 64] = 1.0
        consts[64 * (1 - i), 3 + i, 64 * i:64 * i + 64] = V_DIM * EPS

    arrays = {
        "x_in": np.ascontiguousarray(a["x"].reshape(SEQ, DC, P).transpose(2, 1, 0)),
        "w_units": w_units, "w_pair": w_pair, "w_v": w_v,
        "p_in": np.ascontiguousarray(a["p"].reshape(DEPTH, SEQ, PLE // P, P).transpose(0, 2, 3, 1)),
        "gains": gains, "table": table, "consts": consts,
    }
    nc = _bacc.Bacc("TRN2", target_bir_lowering=False, num_devices=1)
    args = [nc.dram_tensor(k, v.shape, mybir.dt.from_np(v.dtype), kind="ExternalInput").ap() for k, v in arrays.items()]
    args.append(nc.dram_tensor("out", [P, DC, SEQ], mybir.dt.float32, kind="ExternalOutput").ap())
    encoder(nc, *args)
    r = _run(nc, [arrays], core_ids=[0])
    got = r.results[0]["out"]
    return np.ascontiguousarray(got.transpose(2, 1, 0)).reshape(1, SEQ, D)
```

```python
import math
from contextlib import ExitStack

import concourse.bass as bass
import numpy as np
from concourse import mybir

DEPTH, SEQ, D = 2, 1024, 1024
P = 128
HALF = 512
DC = D // P
HEADS, NOPE, ROPE, V_DIM = 8, 64, 32, 64
QK = NOPE + ROPE
Q_RANK, KV_RANK = 384, 256
QC, KVC = Q_RANK // P, KV_RANK // P
CONV = 512
D_FF = 4096
PLE = 256
EPS = 1e-6
UNIT = 1024
SLOTS = 4
RAW = 2

PAIRS = HEADS // 2
IN_UNITS = QC + KVC + 1 + 3 * (CONV // P)
OUT_UNITS = DC
GROUPS = D_FF // (2 * P)
MLP_UNITS = 4 * GROUPS
E_UNITS = 2
GATE_UNITS = DC
O_AT = IN_UNITS
M_AT = O_AT + OUT_UNITS
E_AT = M_AT + MLP_UNITS
G_AT = E_AT + E_UNITS
UNITS = G_AT + GATE_UNITS
HEAD_UNIT = 5 * P
HEAD_SLOT = IN_UNITS % SLOTS
STAGES = HEADS + PLE // P
STEPS = SEQ // P
MIX_STORED = 16 * 2 * (CONV // P + 2 * HEADS)

IN_KIND = ([("q", c) for c in range(QC)] + [("kv", c) for c in range(KVC)]
           + [(k, j) for j in range(3) for k in ("C", "u", "B")] + [("kr", 0), ("C", 3), ("u", 3), ("B", 3)])
IN_BLOCKS = [list(range(a, min(a + SLOTS, IN_UNITS))) for a in range(0, IN_UNITS, SLOTS)]
IN_OUTS = [(u, t) for b in IN_BLOCKS for t in range(2) for u in b]
OUT_OUTS = [(m, t) for b in (range(4), range(4, 8)) for t in range(2) for m in b]
GATE_OUTS = [(m, t) for b in ((0, 1), (2, 3, 4, 5), (6, 7)) for t in range(2) for m in b]
BY_ACT = ("C", "B")
BY_DVE = ("q", "kv", "kr")


def outputs_of(kinds, n):
    return sum(IN_KIND[u][0] in kinds for u, _ in IN_OUTS[:n])


CHUNKS = CONV // P
MULT_AT = [15, 22, 29, 35]
CSTAT_AT = [17, 24, 31, 36]
CY_AT = [18, 25, 32, 37]
CLO_AT = [19, 26, 33, 38]
LSQ_AT = [13, 13, 18, 19]
LSTAT_AT = [15, 16, 20, 21]
LF_AT = [16, 17, 21, 22]
LY_AT = [17, 18, 22, 23]
LORA = [range(QC), range(QC, QC + KVC)]

AHEAD = [("pre", -1, t, c) for t in range(2) for c in range(DC)]
OUT_TAIL = [("out", n) for n in range(13)] + [("factor", 0)] + [("pre", 0, 0, c) for c in range(3)]
OUT_TAIL += [("out", 13)] + [("pre", 0, 0, c) for c in range(3, 6)] + [("out", 14)]
OUT_TAIL += [("pre", 0, 0, c) for c in range(6, 8)] + [("out", 15), ("factor", 1)]
OUT_TAIL += [("pre", 0, 1, c) for c in range(8)]
SQUARES = [("lora", i, 0, c) for i in range(4) for c in LORA[i % 2]]
SQUARES += [e if e[0] == "pre" else ("post", 0) + OUT_OUTS[e[1]][::-1] for e in OUT_TAIL if e[0] != "factor"]
SQUARES += [("post", 1, t, c) for t in range(2) for c in range(DC)]
SQUARES += [("pre", 1, t, c) for t in range(2) for c in range(DC)]
SQUARES += [("post", 2, t, m) for m, t in GATE_OUTS]
SQUARES += [("pre", 2, t, c) for t in range(2) for c in range(DC)]


def is_first(e):
    return e[3] == (QC if e[0] == "lora" and e[1] % 2 else 0)


def square_number(e):
    return (AHEAD if e in AHEAD else SQUARES).index(e)


def sum_number(e):
    where = AHEAD if e in AHEAD else SQUARES
    return sum(not is_first(o) for o in where[:where.index(e)])


SUMS = sum(not is_first(e) for e in SQUARES)
SUMS_AHEAD = sum(not is_first(e) for e in AHEAD)
assert SUMS % 2 == 0 and SUMS_AHEAD % 2 == 0

G_Q, G_KV, G_ATT, G_CONV = 0, 3, 5, 9
G_POST = [13, 29, 45]
G_PRE = [21, 37, 53]
G_TAP = 61
G_FIRST = 73
G_ALL = 81


def encoder(nc, x_in, w_units, w_head, p_in, gains, table, consts, out):
    f32, f32r = mybir.dt.float32, mybir.dt.float32r
    ALU, ACT, AX = mybir.AluOpType, mybir.ActivationFunctionType, mybir.AxisListType
    SCALE = 1.0 / math.sqrt(QK)
    ctx = ExitStack()

    def sb(name, shape, dt, where=ctx):
        return where.enter_context(nc.sbuf_tensor(name, shape, dt))

    def sem(name):
        return ctx.enter_context(nc.semaphore(name))

    def dram(name, shape, dt):
        return nc.dram_tensor(name, shape, dt, kind="Internal").ap()

    def hs(t):
        return slice(t * HALF, (t + 1) * HALF)

    with ctx:
        raw = sb("raw", [P, RAW, UNIT], f32)
        wh = sb("wh", [P, SLOTS, 8, P], f32r)
        wl = sb("wl", [P, SLOTS, 8, P], f32r)
        stage = sb("stage", [P, UNIT], f32)
        hh = sb("hh", [P, DC, SEQ], f32r)
        hl = sb("hl", [P, DC, SEQ], f32r)
        rpre = sb("rpre", [P, 2, HALF], f32)
        sq = sb("sq", [P, 2, HALF], f32)
        accy = sb("accy", [P, 2, HALF], f32)
        xacc = sb("xacc", [P, HALF], f32)
        tmp = sb("tmp", [P, HALF], f32)
        gv = sb("gv", [P, G_ALL], f32)
        cst = sb("cst", [P, 5, P], f32)
        eps = sb("eps", [P, 1], f32)
        carry = sb("carry", [P, 1], f32)
        mx = sb("mx", [P, 2], f32)
        nm = sb("nm", [P, 2], f32)
        ident, ones, blocks = cst[:, 0, :], cst[:, 1, :], cst[:, 2, :]
        HA, HB = 5, 7

        with ExitStack() as att:
            kh = sb("kh", [P, 2, SEQ], f32r, att)
            kl = sb("kl", [P, 2, SEQ], f32r, att)
            tab = sb("tab", [P, SEQ], f32, att)
            with ExitStack() as inp:
                zr = sb("zr", [P, QC + KVC, SEQ], f32, inp)
                cc = sb("cc", [P, SEQ], f32, inp)
                uu = sb("uu", [P, SEQ + 2], f32, inp)
                bb = sb("bb", [P, 2, SEQ], f32, inp)
                cv = sb("cv", [P, SEQ], f32, inp)
                cvs = sb("cvs", [P, 2, HALF], f32, inp)
                cvr = sb("cvr", [P, 2, HALF], f32, inp)
                cyh = sb("cyh", [P, SEQ], f32r, inp)
                cyl = sb("cyl", [P, SEQ], f32r, inp)
                kr = sb("kr", [P, HALF], f32, inp)
            vh = sb("vh", [P, 8, 3 * V_DIM], f32r, att)
            vl = sb("vl", [P, 8, 3 * V_DIM], f32r, att)
            pr = sb("pr", [P, 2, SEQ], f32, att)
            pth = sb("pth", [P, 2, 8, 256], f32r, att)
            ptl = sb("ptl", [P, 2, 8, 256], f32r, att)
            of = sb("of", [P, HALF], f32, att)
            yh = sb("yh", [P, HALF], f32r, att)
            yl = sb("yl", [P, HALF], f32r, att)
        x = sb("x", [P, DC, SEQ], f32)
        facc = sb("facc", [P, DC, SEQ], f32)
        gh = sb("gh", [P, 2, SEQ], f32r)
        gl = sb("gl", [P, 2, SEQ], f32r)

        ps = ctx.enter_context(nc.psum_tensor("ps", [P, 8, HALF], f32))
        mix_hi = dram("mix_hi", [8, P, SEQ], f32)
        mix_lo = dram("mix_lo", [8, P, SEQ], f32)

        const_in = sem("const_in")
        eps_set = sem("eps_set")
        gains_in = sem("gains_in")
        tab_in = sem("tab_in")
        w_in = [sem(f"w_in{i}") for i in range(RAW)]
        w_hi = sem("w_hi")
        w_lo = sem("w_lo")
        stage_in = sem("stage_in")
        stage_hi = sem("stage_hi")
        stage_lo = sem("stage_lo")
        x_back = sem("x_back")
        x_stored = sem("x_stored")
        squared = sem("squared")
        summed = sem("summed")
        pre_hi = sem("pre_hi")
        pre_lo = sem("pre_lo")
        pre_stat = sem("pre_stat")
        pre_ln = sem("pre_ln")
        pre_r = sem("pre_r")
        post_stat = sem("post_stat")
        post_ln = sem("post_ln")
        post_r = sem("post_r")
        post_mul = sem("post_mul")
        x_new = sem("x_new")
        in_out = sem("in_out")
        in_act = sem("in_act")
        in_dve = sem("in_dve")
        kr_cos = sem("kr_cos")
        kr_sum = sem("kr_sum")
        kr_f = sem("kr_f")
        kr_hi = sem("kr_hi")
        kr_lo = sem("kr_lo")
        u_raw = sem("u_raw")
        u_once = sem("u_once")
        u_done = sem("u_done")
        pads = sem("pads")
        tap = sem("tap")
        cv_raw = sem("cv_raw")
        cv_done = sem("cv_done")
        cv_sq = sem("cv_sq")
        cv_stat = sem("cv_stat")
        cv_ln = sem("cv_ln")
        cv_r = sem("cv_r")
        cv_y = sem("cv_y")
        cv_hi = sem("cv_hi")
        cv_lo = sem("cv_lo")
        mix_stored = sem("mix_stored")
        lr_stat = sem("lr_stat")
        lr_ln = sem("lr_ln")
        lr_r = sem("lr_r")
        lr_y = sem("lr_y")
        lr_hi = sem("lr_hi")
        lr_lo = sem("lr_lo")
        v_ones = sem("v_ones")
        kv_out = sem("kv_out")
        k_hi = sem("k_hi")
        k_lo = sem("k_lo")
        v_f = sem("v_f")
        v_out = sem("v_out")
        v_hi = sem("v_hi")
        v_lo = sem("v_lo")
        q_out = sem("q_out")
        q_f = sem("q_f")
        q_hi = sem("q_hi")
        q_lo = sem("q_lo")
        s_out = sem("s_out")
        s_max = sem("s_max")
        s_neg = sem("s_neg")
        s_exp = sem("s_exp")
        t_out = sem("t_out")
        t_hi = sem("t_hi")
        t_lo = sem("t_lo")
        pv_out = sem("pv_out")
        o_sq = sem("o_sq")
        o_copy = sem("o_copy")
        o_var = sem("o_var")
        o_ln = sem("o_ln")
        o_r = sem("o_r")
        o_y = sem("o_y")
        o_hi = sem("o_hi")
        o_lo = sem("o_lo")
        mix_in = sem("mix_in")
        mix_last = sem("mix_last")
        mix_out = sem("mix_out")
        mix_copy = sem("mix_copy")
        up_out = sem("up_out")
        up_v = sem("up_v")
        up_sq = sem("up_sq")
        up_hi = sem("up_hi")
        up_lo = sem("up_lo")
        down_out = sem("down_out")
        down_add = sem("down_add")
        f_zero = sem("f_zero")
        e_out = sem("e_out")
        e_copy = sem("e_copy")
        gate_out = sem("gate_out")
        gate_z = sem("gate_z")
        gate_s = sem("gate_s")
        gate_y = sem("gate_y")

        NORMS = 3

        def pre_at(L, k):
            return L * NORMS + (k + 1)

        def post_at(L, k):
            return L * NORMS + k

        def last_read(L, w, g=0):
            if w < O_AT:
                return in_out, L * len(IN_OUTS) + IN_OUTS.index((w, 1)) + 1
            if w < M_AT:
                return mix_out, L * 16 + OUT_OUTS.index((w - O_AT, 1)) + 1
            if w < M_AT + 2:
                return up_out, (L * GROUPS + g) * 4 + 3 + (w - M_AT)
            if w < M_AT + 4:
                return down_out, (L * GROUPS + g) * 16 + 12 + 4 * (w - M_AT - 2)
            if w < G_AT:
                return e_out, L * 16 + 12 + 4 * (w - E_AT)
            return gate_out, L * 16 + GATE_OUTS.index((w - G_AT, 1)) + 1

        def slot_free(L, w, g=0):
            if w == O_AT:
                return q_out, (L + 1) * 2 * HEADS - 2
            if not isinstance(g, int):
                return last_read(L, w, g - 1)
            if M_AT <= w < E_AT:
                return last_read(L, w, g - 1) if g > 0 else last_read(L, w - SLOTS)
            if E_AT <= w < E_AT + SLOTS:
                return last_read(L, M_AT + w - E_AT, GROUPS - 1)
            return last_read(L, w - SLOTS)

        gatt = gv[:, G_ATT:G_ATT + PAIRS]

        def head_unit(a, h_or_l):
            ring, held = ((wh, hh), (wl, hl))[h_or_l]
            return held[:, HB, 0:HEAD_UNIT].rearrange("p (k m) -> p k m", k=5) if a else ring[:, HEAD_SLOT, 0:5, :]

        def rows(a):
            return slice(a * V_DIM, (a + 1) * V_DIM)

        def step(L, h, s):
            return (L * HEADS + h) * STEPS + s

        def square_at(L, e):
            return square_number(e) + 1 + (0 if L is None else L * len(SQUARES) + len(AHEAD))

        def sum_at(L, e):
            return sum_number(e) + 1 + (0 if L is None else L * SUMS + SUMS_AHEAD)

        def sum_of(e):
            kind, k, t, c = e
            if kind == "pre":
                return (xacc, tmp)[t][:, :]
            return accy[:, k % 2 if kind == "lora" else t, :]

        def last_of(kind, k, t):
            if kind == "lora":
                return (kind, k, 0, LORA[k % 2][-1])
            return (kind, k, t, DC - 1)

        block = ctx.enter_context(nc.Block())

        @block.sync
        def _(sp):
            def load(L, w, g=0):
                sp.wait_ge(w_lo, L * UNITS + g * 4 + w + 1)
                sp.dma_start(raw[:, w % RAW, :],
                             w_units[bass.ds(L, 1), bass.ds(g * 4 + w, 1), :, :].rearrange("a b p n -> p (a b n)")
                             ).then_inc(w_in[w % RAW], 16)

            def load_stage(L, k, src):
                sp.wait_ge(stage_lo, L * STAGES + k + 1)
                sp.dma_start(stage[:, 0:src.shape[1]], src).then_inc(stage_in, 16)

            sp.dma_start(cst[:, :, :], consts).then_inc(const_in, 16)
            sp.dma_start(gv[:, :], gains[0]).then_inc(const_in, 16)
            for t in range(2):
                sp.dma_start(x[:, :, hs(t)], x_in[:, :, hs(t)]).then_inc(const_in, 16)
            sp.wait_ge(const_in, 64)
            for t in range(2):
                sp.dma_start(out[:, :, hs(t)], x[:, :, hs(t)]).then_inc(x_stored, 16)

            with sp.Fori(0, DEPTH) as L:
                load(L, 0)
                load(L, 1)
                sp.wait_ge(pre_lo, pre_at(L, -1) * 16 + 16)
                sp.dma_start(gv[:, :], gains[bass.ds(L, 1), :, :].rearrange("a p n -> p (a n)")).then_inc(gains_in, 16)
                sp.wait_ge(squared, square_at(L, SQUARES[0]) - 1)
                sp.wait_ge(x_stored, L * 32 + 32)
                sp.dma_start(tab[:, :], table).then_inc(tab_in, 16)

                def load_head(h):
                    load_stage(L, h, w_head[bass.ds(L, 1), bass.ds(h, 1), :, :].rearrange("a b p n -> p (a b n)"))

                load_head(0)

                def store_conv(j):
                    sp.wait_ge(cv_lo, L * 8 + 2 * j + 2)
                    sp.dma_start(mix_hi[4 + j], cyh[:, :].bitcast(f32)).then_inc(mix_stored, 16)
                    sp.dma_start(mix_lo[4 + j], cyl[:, :].bitcast(f32)).then_inc(mix_stored, 16)

                stores_before = {15: 0, 18: 1}
                for w in range(2, O_AT + RAW):
                    if w in stores_before:
                        store_conv(stores_before[w])
                    load(L, w)

                load_head(1)
                store_conv(2)
                store_conv(3)

                def store_attention(j, a, t):
                    sp.wait_ge(o_lo, L * 2 * HEADS + j * 4 + a * 2 + t + 2)
                    for src, dst in ((yh, mix_hi), (yl, mix_lo)):
                        sp.dma_start(dst[bass.ds(j, 1), rows(a), hs(t)].rearrange("a p n -> p (a n)"),
                                     src[rows(a), :].bitcast(f32)).then_inc(mix_stored, 16)

                load_head(2)
                store_attention(0, 0, 0)
                load_head(3)
                store_attention(0, 0, 1)
                store_attention(0, 1, 0)
                with sp.Fori(1, PAIRS - 1) as j:
                    load_head(2 * j + 2)
                    store_attention(j - 1, 1, 1)
                    store_attention(j, 0, 0)
                    load_head(2 * j + 3)
                    store_attention(j, 0, 1)
                    store_attention(j, 1, 0)
                store_attention(PAIRS - 2, 1, 1)
                store_attention(PAIRS - 1, 0, 0)

                def load_mix(c, done):
                    sp.dma_start(hh[:, c, :].bitcast(f32), mix_hi[c]).then_inc(done, 16)
                    sp.dma_start(hl[:, c, :].bitcast(f32), mix_lo[c]).then_inc(done, 16)

                sp.wait_ge(q_out, (L + 1) * 2 * HEADS)
                sp.wait_ge(mix_stored, L * MIX_STORED + MIX_STORED - 96)
                for c in (4, 7, 0, 1, 2):
                    load_mix(c, mix_in)
                store_attention(PAIRS - 1, 0, 1)
                for w in range(O_AT + RAW, O_AT + SLOTS):
                    load(L, w)
                sp.wait_ge(s_out, (L + 1) * HEADS * STEPS)
                for c in (5, 6):
                    load_mix(c, mix_in)
                load(L, O_AT + SLOTS)
                store_attention(PAIRS - 1, 1, 0)
                store_attention(PAIRS - 1, 1, 1)
                sp.wait_ge(mix_stored, (L + 1) * MIX_STORED)
                load_mix(3, mix_last)
                sp.wait_ge(mix_copy, L * 16 + 1)
                sp.dma_start(x[:, :, :], out[:, :, :]).then_inc(x_back, 16)
                for w in range(O_AT + 5, M_AT):
                    load(L, w)
                with sp.Fori(0, GROUPS) as g:
                    for i in range(4):
                        load(L, M_AT + i, g)
                load_stage(L, HEADS, p_in[bass.ds(L, 1), 0, :, :].rearrange("a p n -> p (a n)"))
                for w in range(E_AT, G_AT + 2):
                    load(L, w)
                load_stage(L, HEADS + 1, p_in[bass.ds(L, 1), 1, :, :].rearrange("a p n -> p (a n)"))
                for w in range(G_AT + 2, UNITS):
                    load(L, w)
                for t in range(2):
                    sp.wait_ge(x_new, post_at(L, 2) * 16 + t * 8 + 8)
                    sp.dma_start(out[:, :, hs(t)], x[:, :, hs(t)]).then_inc(x_stored, 16)
            sp.wait_ge(x_stored, 32 * (DEPTH + 1))
            sp.wait_ge(mix_stored, MIX_STORED * DEPTH)

        @block.tensor
        def _(pe):
            def split_product(dst, ah, al, bh, bl, start, stop):
                nc.tensor.matmul(dst, ah, bh, start=start, stop=False)
                nc.tensor.matmul(dst, ah, bl, start=False, stop=False)
                return nc.tensor.matmul(dst, al, bh, start=False, stop=stop)

            def unit_output(bank, slot, t, ready=None, order=range(DC)):
                for n, k in enumerate(order):
                    if ready is not None:
                        ready(k)
                    last = split_product(ps[:, bank, :], wh[:, slot, k, :], wl[:, slot, k, :],
                                         hh[:, k, hs(t)], hl[:, k, hs(t)], n == 0, n == DC - 1)
                return last

            def two_tiles(bank, slot, m, t):
                for k in range(2):
                    tile = 2 * (m % 4) + k
                    last = split_product(ps[:, bank, :], wh[:, slot, tile, :], wl[:, slot, tile, :],
                                         gh[:, k, hs(t)], gl[:, k, hs(t)], k == 0, k == 1)
                return last

            def unit_ready(L, w, g=0):
                pe.wait_ge(w_lo, L * UNITS + g * 4 + w + 1 + RAW)

            def pre_stats(L, k, t):
                if k == -1:
                    pe.wait_ge(summed, L * SUMS + SUMS_AHEAD - (1 - t) * (DC - 1))
                else:
                    pe.wait_ge(summed, sum_at(L, last_of("pre", k, t)))
                if t == 1:
                    pe.wait_ge(pre_ln, pre_at(L, k) * 2 + 1)
                nc.tensor.matmul(ps[:, 7, :], ones, (xacc, tmp)[t][:, :], start=True, stop=True).then_inc(pre_stat, 1)

            def post_stats(L, k, t):
                pe.wait_ge(summed, sum_at(L, last_of("post", k, t)))
                if t == 1:
                    pe.wait_ge(post_ln, post_at(L, k) * 2 + 1)
                nc.tensor.matmul(ps[:, 6, :], ones, accy[:, t, :], start=True, stop=True).then_inc(post_stat, 1)

            def pre_ready(R, t):
                return lambda k: pe.wait_ge(pre_lo, R * 16 + t * 8 + k + 1)

            pe.wait_ge(const_in, 64)
            with pe.Fori(0, DEPTH) as L:
                R = pre_at(L, -1)

                def conv_stat(j, t):
                    pe.wait_ge(cv_sq, L * 8 + 2 * j + t + 1)
                    if j:
                        pe.wait_ge(cv_ln, L * 8 + 2 * j + t - 1)
                    nc.tensor.matmul(ps[:, 4 + t, :], blocks, cvs[:, t, :], start=True, stop=True).then_inc(cv_stat, 1)

                def lora_stat(i):
                    pe.wait_ge(summed, sum_at(L, last_of("lora", i, 0)))
                    if i:
                        pe.wait_ge(lr_ln, L * 4 + i)
                    nc.tensor.matmul(ps[:, 6, :], ones, accy[:, i % 2, :], start=True, stop=True).then_inc(lr_stat, 1)

                for n in range(len(IN_OUTS) + 1):
                    if n < len(IN_OUTS):
                        u, t = IN_OUTS[n]
                        if t == 0:
                            unit_ready(L, u)
                        if n >= 4:
                            kind = IN_KIND[IN_OUTS[n - 4][0]][0]
                            if kind in BY_ACT:
                                pe.wait_ge(in_act, L * 16 + outputs_of(BY_ACT, n - 3))
                            elif kind == "u":
                                pe.wait_ge(u_raw, L * 8 + outputs_of("u", n - 3))
                            else:
                                pe.wait_ge(in_dve, L * 12 + outputs_of(BY_DVE, n - 3))
                        ready = pre_ready(R, t) if n in (0, 4) else None
                        unit_output(n % 4, u % SLOTS, t, ready).then_inc(in_out, 1)
                        if n in (0, 4):
                            pre_stats(L, -1, t)
                    for i in range(4):
                        if LSTAT_AT[i] == n:
                            lora_stat(i)
                    for j in range(CHUNKS):
                        if CSTAT_AT[j] == n and j < CHUNKS - 1:
                            conv_stat(j, 0)
                            conv_stat(j, 1)

                def keys_and_values(h, a, t, bank):
                    if t == 0:
                        pe.wait_ge(stage_lo, L * STAGES + h + 2)
                    for k in range(KVC):
                        last = split_product(ps[:, bank, :], head_unit(a, 0)[:, 3 + k, :], head_unit(a, 1)[:, 3 + k, :],
                                             hh[:, QC + k, hs(t)], hl[:, QC + k, hs(t)], k == 0, k == KVC - 1)
                    last.then_inc(kv_out, 1)

                def queries(h, a, t, bank):
                    for k in range(QC):
                        last = split_product(ps[:, bank, :], head_unit(a, 0)[:, k, :], head_unit(a, 1)[:, k, :],
                                             hh[:, k, hs(t)], hl[:, k, hs(t)], k == 0, k == QC - 1)
                    last.then_inc(q_out, 1)

                def values_by_token(h, a, t, bank):
                    pe.wait_ge(v_f, (L * HEADS + h) * 2 + 2)
                    for c in range(STEPS):
                        last = nc.tensor.matmul(ps[:, bank, c * V_DIM:(c + 1) * V_DIM],
                                                accy[:, c // 4, (c % 4) * P:(c % 4 + 1) * P], cst[:, 0, V_DIM:P],
                                                start=True, stop=True)
                    last.then_inc(v_out, 1)

                PIECES = {0: (keys_and_values, 0), 1: (keys_and_values, 1), 2: (queries, 0),
                          3: (values_by_token, 0), 4: (queries, 1)}

                def scores(h, a, s):
                    if s % 4 == 0:
                        pe.wait_ge(q_lo, (L * HEADS + h) * 2 + s // 4 + 1)
                    if s == 0:
                        pe.wait_ge(k_lo, (L * HEADS + h) * 2 + 2)
                    if isinstance(h, int) and h == 0 and s < 2:
                        if s == 0:
                            pe.wait_ge(v_f, L * HEADS * 2 + 2)
                        else:
                            pe.wait_ge(v_lo, L * HEADS + 1)
                    else:
                        pe.wait_ge(s_exp, step(L, h, s) - 1)
                    tok = slice(s * P, (s + 1) * P)
                    for kb in range(2):
                        last = split_product(ps[:, 2 * (s % 2) + kb, :], hh[:, HA + a, tok], hl[:, HA + a, tok],
                                             kh[:, a, hs(kb)], kl[:, a, hs(kb)], True, True)
                    last.then_inc(s_out, 1)

                def transposes(h, s, first, piece):
                    S = step(L, h, s)
                    pe.wait_ge(s_exp, S + 1)
                    for b in range(2):
                        if not (first and s == 0):
                            pe.wait_ge(t_lo, 2 * S + b - 1)
                        elif b == 0:
                            pe.wait_ge(cv_ln, L * 8 + 8)
                        if b == 1 and piece:
                            piece_read(h, s - 1)
                        for c in range(4):
                            last = nc.tensor.transpose(ps[:, 4 + b, c * P:(c + 1) * P],
                                                       pr[:, s % 2, (4 * b + c) * P:(4 * b + c + 1) * P], ident)
                        last.then_inc(t_out, 1)

                def piece_read(h, s):
                    H = L * HEADS + h + 1
                    if s in (0, 1):
                        pe.wait_ge(k_lo, H * 2 + s + 1)
                    elif s in (2, 4):
                        pe.wait_ge(q_f, H * 2 + s // 2)
                    elif s == 3:
                        pe.wait_ge(v_lo, H + 1)

                def values(h, a, G, part):
                    if part == 0:
                        pe.wait_ge(t_lo, 2 * step(L, h, 2 * G + 2))
                    dst = ps[:, 6 + G // 2, (G % 2) * 256:(G % 2 + 1) * 256]
                    for c in range(4 * part, 4 * part + 4):
                        last = split_product(dst, vh[:, c, a * V_DIM:a * V_DIM + P], vl[:, c, a * V_DIM:a * V_DIM + P],
                                             pth[:, G % 2, c, :], ptl[:, G % 2, c, :], c == 0, c == 7)
                    if part == 1:
                        last.then_inc(pv_out, 1)

                def variances(h, a, t):
                    pe.wait_ge(o_copy, (L * HEADS + h) * 2 + t + 1)
                    nc.tensor.matmul(ps[:, 6 + t, :], cst[:, 3 + a, :], sq[:, 0, :], start=True, stop=True).then_inc(o_var, 1)

                def head(h, a, first=False, last=False):
                    for s in range(STEPS):
                        transposes(h, s, first, s - 1 in PIECES and not last)
                        if s + 2 < STEPS:
                            scores(h, a, s + 2)
                        elif not last:
                            scores(h + 1, 1 - a, s + 2 - STEPS)
                        if s in PIECES and not last:
                            make, t = PIECES[s]
                            pe.wait_ge(t_lo, 2 * step(L, h, s) + 2)
                            make(h + 1, 1 - a, t, 5)
                        if s == 3 and not first:
                            variances(h - 1, 1 - a, 1)
                        if s == 7:
                            variances(h, a, 0)
                        if s >= 2:
                            if s == 2 and not first:
                                pe.wait_ge(o_ln, (L * HEADS + h) * 2 - 1)
                            if s == 6 and not first:
                                pe.wait_ge(o_ln, (L * HEADS + h) * 2)
                            values(h, a, (s - 2) // 2, s % 2)
                        elif not first:
                            values(h - 1, 1 - a, 3, s)

                pe.wait_ge(lr_lo, L * 5 + 2)
                keys_and_values(0, 0, 0, 0)
                keys_and_values(0, 0, 1, 1)
                pe.wait_ge(lr_lo, L * 5 + 5)
                queries(0, 0, 0, 2)
                conv_stat(CHUNKS - 1, 0)
                conv_stat(CHUNKS - 1, 1)
                values_by_token(0, 0, 0, 3)
                queries(0, 0, 1, 6)
                pe.wait_ge(v_ones, L * 2 + 2)
                scores(0, 0, 0)
                scores(0, 0, 1)
                head(0, 0, first=True)
                head(1, 1)
                with pe.Fori(1, PAIRS - 1) as j:
                    head(2 * j, 0)
                    head(2 * j + 1, 1)
                head(HEADS - 2, 0)
                head(HEADS - 1, 1, last=True)
                values(HEADS - 1, 1, 3, 0)
                values(HEADS - 1, 1, 3, 1)

                def mix_part(n, order, start, stop):
                    m, t = OUT_OUTS[n]
                    for i, k in enumerate(order):
                        slot = (O_AT + m) % SLOTS
                        last = split_product(ps[:, n % 4, :], wh[:, slot, k, :], wl[:, slot, k, :],
                                             hh[:, k, hs(t)], hl[:, k, hs(t)], start and i == 0, stop and i == len(order) - 1)
                    return last

                for n in range(4):
                    unit_ready(L, O_AT + n)
                    if n == 0:
                        pe.wait_ge(mix_in, (L + 1) * 224)
                    mix_part(n, (4, 7, 0, 1, 2, 5, 6), True, False)
                    if n == 0:
                        variances(HEADS - 1, 1, 1)
                pe.wait_ge(mix_last, (L + 1) * 32)
                for n in range(4):
                    mix_part(n, (3,), False, True).then_inc(mix_out, 1)
                for n in range(4, len(OUT_OUTS)):
                    m, t = OUT_OUTS[n]
                    if t == 0:
                        unit_ready(L, O_AT + m)
                    pe.wait_ge(mix_copy, L * 16 + n - 3)
                    mix_part(n, range(DC), True, True).then_inc(mix_out, 1)
                    if n == 12:
                        post_stats(L, 0, 0)
                post_stats(L, 0, 1)

                def up(g, t, ready=None, after=None):
                    for i in range(2):
                        n = 2 * t + i
                        if t == 0:
                            unit_ready(L, M_AT + i, g)
                        if not isinstance(g, int):
                            pe.wait_ge(up_v, L * 4 * GROUPS + (g - 1) * 4 + n + 1)
                        unit_output(n, (M_AT + i) % SLOTS, t, ready).then_inc(up_out, 1)
                        if i == 0 and after:
                            after()
                        ready = None

                def down(g, t, banks=4, first=False, between={}):
                    pe.wait_ge(up_lo, L * 4 * GROUPS + g * 4 + 2 * t + 2)
                    for m in range(DC):
                        if t == 0 and m % 4 == 0:
                            unit_ready(L, M_AT + 2 + m // 4, g)
                        before = L * 16 * GROUPS + g * 16 + t * 8 + m
                        if m >= banks or (banks == 4 and not first):
                            pe.wait_ge(down_add, before - banks + 1)
                        elif not first:
                            pe.wait_ge(down_add, before - m)
                        two_tiles(4 + m % banks, (M_AT + 2 + m // 4) % SLOTS, m, t).then_inc(down_out, 1)
                        if m in between:
                            between[m]()

                R = pre_at(L, 0)
                up(0, 0, pre_ready(R, 0), lambda: pre_stats(L, 0, 0))
                up(0, 1, pre_ready(R, 1))
                pre_stats(L, 0, 1)
                pe.wait_ge(pre_ln, R * 2 + 2)
                down(0, 0, first=True)
                with pe.Fori(1, GROUPS) as g:
                    up(g, 0)
                    down(g - 1, 1)
                    up(g, 1)
                    down(g, 0)
                down(GROUPS - 1, 1, banks=2, between={4: lambda: post_stats(L, 1, 0)})

                def embed(t, ms):
                    for m in ms:
                        if t == 0 and m % 4 == 0:
                            unit_ready(L, E_AT + m // 4)
                        n = t * 8 + m
                        if n in (8, 9):
                            pe.wait_ge(gate_z, L * 16 + n - 7)
                        elif n >= 4:
                            pe.wait_ge(e_copy, L * 16 + n - 3)
                        two_tiles(m % 4, (E_AT + m // 4) % SLOTS, m, t).then_inc(e_out, 1)

                def gate(n):
                    m, t = GATE_OUTS[n]
                    if t == 0:
                        unit_ready(L, G_AT + m)
                    bank = n % 4 if n >= 4 else n % 2
                    if n < 2:
                        pe.wait_ge(e_copy, L * 16 + 5 + n)
                    elif n < 4:
                        pe.wait_ge(e_copy, L * 16 + 13 + n - 2)
                    elif n < 6:
                        pe.wait_ge(gate_z, L * 16 + n - 1)
                    elif n < 8:
                        pe.wait_ge(e_copy, L * 16 + 9 + n)
                    else:
                        pe.wait_ge(gate_z, L * 16 + n - 3)
                    ready = pre_ready(pre_at(L, 1), t) if n in (0, 2) else None
                    unit_output(bank, (G_AT + m) % SLOTS, t, ready).then_inc(gate_out, 1)

                pe.wait_ge(stage_lo, (L + 1) * STAGES + 1)
                embed(0, range(4))
                post_stats(L, 1, 1)
                embed(0, range(4, 8))
                gate(0)
                pre_stats(L, 1, 0)
                gate(1)
                embed(1, range(8))
                gate(2)
                pre_stats(L, 1, 1)
                for n in range(3, 16):
                    gate(n)
                    if n == 14:
                        post_stats(L, 2, 0)
                post_stats(L, 2, 1)

        @block.scalar
        def _(act):
            def table_of_exp_and_ln():
                nc.scalar.add_instruction(mybir.InstLoadActFuncSet(
                    name=nc.get_next_instruction_name(), act_func_set_id=6, ins=[], outs=[],
                    engine=mybir.EngineType.Activation))

            def copy(dst, src, **more):
                return nc.scalar.activation(dst, src, ACT.Copy, **more)

            def split_unit(L, w, g=0):
                act.wait_ge(w_in[w % RAW], (L * (UNITS // RAW) + g * (4 // RAW) + w // RAW) * 16 + 16)
                if w >= SLOTS:
                    act.wait_ge(*slot_free(L, w, g))
                copy(wh[:, w % SLOTS, :, :].rearrange("p k m -> p (k m)"), raw[:, w % RAW, :]).then_inc(w_hi, 1)

            def split_stage(L, k, dst):
                act.wait_ge(stage_in, (L * STAGES + k) * 16 + 16)
                copy(dst, stage[:, 0:dst.shape[1]]).then_inc(stage_hi, 1)

            def square(L, e, src):
                k = sum_number(e)
                if is_first(e):
                    dst = sum_of(e)
                else:
                    if L is not None or k >= 2:
                        act.wait_ge(summed, sum_at(L, e) - 2)
                    dst = sq[:, k % 2, :]
                nc.scalar.activation(dst, src, ACT.Square).then_inc(squared, 1)

            def split_head(L, h, a):
                split_stage(L, h, head_unit(a, 0).rearrange("p k m -> p (k m)"))

            def factor(dst, bank, width, stat, ln, r, count, bias=eps, part=slice(None)):
                act.wait_ge(stat, count)
                more = {} if bias is None else {"bias": bias[:, :]}
                nc.scalar.activation(dst, ps[part, bank, :], ACT.Ln, scale=1.0 / width, **more).then_inc(ln, 1)
                act.wait_ge(ln, count)
                nc.scalar.activation(dst, dst, ACT.Exp, scale=-0.5).then_inc(r, 1)

            def pre_factor(L, k, t):
                factor(rpre[:, t, :], 7, D, pre_stat, pre_ln, pre_r, pre_at(L, k) * 2 + t + 1)

            def post_factor(L, k, t):
                factor(accy[:, t, :], 6, D, post_stat, post_ln, post_r, post_at(L, k) * 2 + t + 1)

            def pre_chunk(L, k, t, c):
                g_at = G_FIRST if L is None else G_PRE[k]
                if L is not None:
                    act.wait_ge(x_new, post_at(L, k) * 16 + t * 8 + c + 1)
                copy(hh[:, c, hs(t)], x[:, c, hs(t)], scale=gv[:, g_at + c:g_at + c + 1]).then_inc(pre_hi, 1)
                square(L, ("pre", k, t, c), x[:, c, hs(t)])

            table_of_exp_and_ln()
            act.wait_ge(const_in, 64)
            act.wait_ge(eps_set, 1)
            for t in range(2):
                for c in range(DC):
                    pre_chunk(None, -1, t, c)
            with act.Fori(0, DEPTH) as L:
                for w in range(SLOTS):
                    split_unit(L, w)
                factor(rpre[:, 0, :], 7, D, pre_stat, pre_ln, pre_r, pre_at(L, -1) * 2 + 1)
                act.wait_ge(x_stored, L * 32 + 32)
                act.wait_ge(pre_lo, pre_at(L, -1) * 16 + 16)

                for n in range(len(IN_OUTS)):
                    u, t = IN_OUTS[n] if n < len(IN_OUTS) else (None, None)
                    kind, j = IN_KIND[u] if u is not None else (None, None)
                    if kind == "C":
                        act.wait_ge(in_out, L * 36 + n + 1)
                        if j:
                            act.wait_ge(u_raw, L * 8 + 2 * (j - 1) + t + 1)
                        copy(cc[:, hs(t)], ps[:, n % 4, :]).then_inc(in_act, 1)
                    if kind == "B":
                        act.wait_ge(in_out, L * 36 + n + 1)
                        if j >= 2:
                            act.wait_ge(cv_raw, L * 4 + j - 1)
                        copy(bb[:, j % 2, hs(t)], ps[:, n % 4, :]).then_inc(in_act, 1)
                    if n == 4:
                        factor(rpre[:, 1, :], 7, D, pre_stat, pre_ln, pre_r, pre_at(L, -1) * 2 + 2)
                    if kind == "kr":
                        act.wait_ge(kr_f, L * 2 + t + 1)
                        for a in range(2):
                            copy(kh[NOPE:P, a, hs(t)], kr[NOPE:P, :]).then_inc(kr_hi, 1)
                    for i in range(4):
                        if LF_AT[i] == n:
                            rank = KV_RANK if i % 2 else Q_RANK
                            factor(accy[:, i % 2, :], 6, rank, lr_stat, lr_ln, lr_r, L * 4 + i + 1)
                    for i in range(4):
                        if LSQ_AT[i] == n:
                            if i == 0:
                                act.wait_ge(in_dve, L * 12 + outputs_of(BY_DVE, 13))
                            if i >= 2:
                                act.wait_ge(lr_y, L * 10 + (3, 5)[i - 2])
                            for c in LORA[i % 2]:
                                square(L, ("lora", i, 0, c), zr[:, c, hs(i // 2)])
                    for j in range(CHUNKS):
                        if MULT_AT[j] + 1 == n and j < CHUNKS - 1:
                            for t2 in range(2):
                                act.wait_ge(cv_done, L * 8 + 2 * j + t2 + 1)
                                nc.scalar.activation(cvs[:, t2, :], cv[:, hs(t2)], ACT.Square).then_inc(cv_sq, 1)
                        if CSTAT_AT[j] + 1 == n and j < CHUNKS - 1:
                            for t2 in range(2):
                                factor(cvr[:, t2, :], 4 + t2, 64, cv_stat, cv_ln, cv_r, L * 8 + 2 * j + t2 + 1)
                        if CY_AT[j] + 1 == n and j < CHUNKS - 1:
                            if j:
                                act.wait_ge(mix_stored, L * MIX_STORED + 32 * j)
                            for t2 in range(2):
                                act.wait_ge(cv_y, L * 8 + 2 * j + t2 + 1)
                                copy(cyh[:, hs(t2)], cv[:, hs(t2)]).then_inc(cv_hi, 1)
                    if t == 1 and u + SLOTS < IN_UNITS:
                        split_unit(L, u + SLOTS)
                    if n == 31:
                        act.wait_ge(*last_read(L, IN_UNITS - SLOTS))
                        split_head(L, 0, 0)

                def latents(cs):
                    for c in cs:
                        copy(hh[:, c, :], zr[:, c, :]).then_inc(lr_hi, 1)

                def keys_and_values(h, a, t, bank):
                    H = L * HEADS + h
                    act.wait_ge(kv_out, H * 2 + t + 1)
                    copy(accy[:, t, :], ps[:, bank, :]).then_inc(v_f, 1)
                    copy(kh[0:NOPE, a, hs(t)], ps[0:NOPE, bank, :]).then_inc(k_hi, 1)

                def queries(h, a, t, bank):
                    act.wait_ge(q_f, (L * HEADS + h) * 2 + t + 1)
                    copy(hh[:, HA + a, hs(t)], (tmp, xacc)[t][:, :]).then_inc(q_hi, 1)

                def values_by_token(h, a, t, bank):
                    act.wait_ge(v_out, L * HEADS + h + 1)
                    copy(vh[:, :, 2 * a * V_DIM:(2 * a + 1) * V_DIM],
                         ps[:, bank, :].rearrange("p (c d) -> p c d", c=STEPS)).then_inc(v_hi, 1)

                PIECES = {0: (keys_and_values, 0), 1: (keys_and_values, 1), 2: (queries, 0),
                          3: (values_by_token, 0), 4: (queries, 1)}

                def exponentials(h, s):
                    act.wait_ge(s_neg, step(L, h, s) + 1)
                    nc.scalar.activation(pr[:, s % 2, :], ps[:, 2 * (s % 2):2 * (s % 2) + 2, :].rearrange("p b n -> p (b n)"),
                                         ACT.Exp, bias=nm[:, s % 2:s % 2 + 1], scale=SCALE).then_inc(s_exp, 1)

                def high_of_transposed(h, s, first):
                    G = s // 2
                    for b in range(2):
                        act.wait_ge(t_out, 2 * step(L, h, s) + b + 1)
                        if first and s == 0:
                            act.wait_ge(mix_stored, L * MIX_STORED + 128)
                        if s % 2 == 0 and b == 0 and (G >= 2 or not first):
                            act.wait_ge(pv_out, (L * HEADS + h) * 4 + G - 1)
                        copy(pth[:, G % 2, 4 * b:4 * b + 4, (s % 2) * P:(s % 2 + 1) * P],
                             ps[:, 4 + b, :].rearrange("p (c q) -> p c q", c=4)).then_inc(t_hi, 1)

                def outputs(h, a, t):
                    O = (L * HEADS + h) * 2 + t
                    act.wait_ge(pv_out, 2 * O + 2)
                    act.wait_ge(o_lo, O + 1)
                    nc.scalar.activation(sq[:, 0, :], ps[:, 6 + t, :], ACT.Square).then_inc(o_sq, 1)
                    copy(of[rows(a), :], ps[rows(a), 6 + t, :]).then_inc(o_copy, 1)

                def output_factor(h, a, t):
                    factor(sq[rows(a), 1, :], 6 + t, V_DIM, o_var, o_ln, o_r, (L * HEADS + h) * 2 + t + 1, None, rows(a))

                def high_of_output(h, a, t):
                    O = (L * HEADS + h) * 2 + t
                    act.wait_ge(o_y, O + 1)
                    act.wait_ge(mix_stored, L * MIX_STORED + 128 + (h * 2 + t) * 32)
                    copy(yh[rows(a), :], of[rows(a), :]).then_inc(o_hi, 1)

                def head(h, a, first=False, last=False):
                    for s in range(STEPS):
                        high_of_transposed(h, s, first)
                        if s + 1 < STEPS:
                            exponentials(h, s + 1)
                        elif not last:
                            exponentials(h + 1, 0)
                        if s in PIECES and not last:
                            make, t = PIECES[s]
                            make(h + 1, 1 - a, t, 5)
                        if not first:
                            if s == 0:
                                high_of_output(h - 1, 1 - a, 0)
                            if s == 2:
                                outputs(h - 1, 1 - a, 1)
                            if s == 3:
                                output_factor(h - 1, 1 - a, 1)
                            if s == 4:
                                high_of_output(h - 1, 1 - a, 1)
                        if s == 6:
                            outputs(h, a, 0)
                            if a == 0 and not (isinstance(h, int) and h == HEADS - 2):
                                split_head(L, h + 2, a)
                            elif a == 1 and not last:
                                split_head(L, h + 2, a)
                            if last:
                                split_unit(L, O_AT + 1)
                        if s == 7:
                            output_factor(h, a, 0)
                            if last:
                                split_unit(L, O_AT + 2)
                                split_unit(L, O_AT + 3)
                        if last and s == 5:
                            split_unit(L, O_AT)

                act.wait_ge(in_out, L * 36 + 36)
                act.wait_ge(lr_y, L * 10 + 10)
                latents((3, 4, 0))
                for t in range(2):
                    act.wait_ge(cv_done, L * 8 + 6 + t + 1)
                    nc.scalar.activation(cvs[:, t, :], cv[:, hs(t)], ACT.Square).then_inc(cv_sq, 1)
                latents((1, 2))
                keys_and_values(0, 0, 0, 0)
                keys_and_values(0, 0, 1, 1)
                queries(0, 0, 0, 2)
                for t in range(2):
                    factor(cvr[:, t, :], 4 + t, 64, cv_stat, cv_ln, cv_r, L * 8 + 6 + t + 1)
                act.wait_ge(mix_stored, L * MIX_STORED + 96)
                for t in range(2):
                    act.wait_ge(cv_y, L * 8 + 6 + t + 1)
                    copy(cyh[:, hs(t)], cv[:, hs(t)]).then_inc(cv_hi, 1)
                values_by_token(0, 0, 0, 3)
                queries(0, 0, 1, 6)
                split_head(L, 1, 1)
                exponentials(0, 0)
                head(0, 0, first=True)
                head(1, 1)
                with act.Fori(1, PAIRS - 1) as j:
                    head(2 * j, 0)
                    head(2 * j + 1, 1)
                head(HEADS - 2, 0)
                head(HEADS - 1, 1, last=True)
                high_of_output(HEADS - 1, 1, 0)
                outputs(HEADS - 1, 1, 1)
                output_factor(HEADS - 1, 1, 1)
                high_of_output(HEADS - 1, 1, 1)

                for e in OUT_TAIL:
                    if e[0] == "out":
                        m, t = OUT_OUTS[e[1]]
                        act.wait_ge(mix_out, L * 16 + e[1] + 1)
                        if e[1] == 0:
                            act.wait_ge(mix_stored, (L + 1) * MIX_STORED)
                        copy(facc[:, m, hs(t)], ps[:, e[1] % 4, :]).then_inc(mix_copy, 1)
                        act.wait_ge(mix_copy, L * 16 + e[1] + 1)
                        square(L, ("post", 0, t, m), facc[:, m, hs(t)])
                        if t == 1:
                            split_unit(L, O_AT + m + SLOTS)
                    elif e[0] == "factor":
                        post_factor(L, 0, e[1])
                    else:
                        pre_chunk(L, *e[1:])
                        if e == ("pre", 0, 1, 3):
                            pre_factor(L, 0, 0)

                def hidden(g, t):
                    for i in range(2):
                        k = L * 4 * GROUPS + g * 4 + 2 * t + i
                        act.wait_ge(up_v, k + 1)
                        nc.scalar.activation(gh[:, i, hs(t)], accy[:, 1, :], ACT.Square).then_inc(up_hi, 1)
                        nc.scalar.activation(accy[:, 0, :], accy[:, 1, :], ACT.Square).then_inc(up_sq, 1)

                def split_two(g, at):
                    for i in range(2):
                        split_unit(L, M_AT + at + i, g)

                hidden(0, 0)
                pre_factor(L, 0, 1)
                hidden(0, 1)
                split_two(1, 0)
                with act.Fori(1, GROUPS) as g:
                    hidden(g, 0)
                    split_two(g, 2)
                    hidden(g, 1)
                    split_two(g + 1, 0)
                for t in range(2):
                    for c in range(DC):
                        act.wait_ge(down_add, (L + 1) * 16 * GROUPS - 16 + 8 * t + c + 1)
                        square(L, ("post", 1, t, c), facc[:, c, hs(t)])
                split_stage(L, HEADS, gh[:, 0, :])
                split_unit(L, G_AT)
                split_unit(L, G_AT + 1)
                post_factor(L, 1, 0)
                split_stage(L, HEADS + 1, gh[:, 1, :])

                def embedding(t, c):
                    act.wait_ge(e_out, L * 16 + t * 8 + c + 1)
                    copy(facc[:, c, hs(t)], ps[:, c % 4, :]).then_inc(e_copy, 1)

                def gates(n):
                    m, t = GATE_OUTS[n]
                    act.wait_ge(gate_z, L * 16 + n + 1)
                    nc.scalar.activation(xacc[:, :], xacc[:, :], ACT.Sigmoid).then_inc(gate_s, 1)
                    act.wait_ge(gate_y, L * 16 + n + 1)
                    square(L, ("post", 2, t, m), facc[:, m, hs(t)])
                    w = G_AT + m + SLOTS
                    if t == 1 and w < UNITS:
                        split_unit(L, w)

                for c in range(DC):
                    pre_chunk(L, 1, 0, c)
                    embedding(0, c)
                post_factor(L, 1, 1)
                for c in range(DC):
                    pre_chunk(L, 1, 1, c)
                pre_factor(L, 1, 0)
                gates(0)
                gates(1)
                for c in range(DC):
                    embedding(1, c)
                split_unit(L, G_AT + 2)
                split_unit(L, G_AT + 3)
                table_of_exp_and_ln()
                pre_factor(L, 1, 1)
                for n in range(2, 16):
                    gates(n)
                table_of_exp_and_ln()
                for t in range(2):
                    post_factor(L, 2, t)
                    for c in range(DC):
                        pre_chunk(L, 2, t, c)

        @block.vector
        def _(dve):
            V = nc.vector

            def low(dst, whole, high):
                return V.tensor_tensor(dst, whole, high.bitcast(f32), ALU.subtract)

            def split_unit(L, w, g=0):
                dve.wait_ge(w_hi, L * UNITS + g * 4 + w + 1)
                low(wl[:, w % SLOTS, :, :].rearrange("p k m -> p (k m)"), raw[:, w % RAW, :],
                    wh[:, w % SLOTS, :, :].rearrange("p k m -> p (k m)")).then_inc(w_lo, 1)

            def split_stage(L, k, dst, high):
                dve.wait_ge(stage_hi, L * STAGES + k + 1)
                low(dst, stage[:, 0:dst.shape[1]], high).then_inc(stage_lo, 1)

            def split_head(L, h, a):
                split_stage(L, h, head_unit(a, 1).rearrange("p k m -> p (k m)"), head_unit(a, 0).rearrange("p k m -> p (k m)"))

            def pre_low(L, k, t, c):
                g_at = G_FIRST if L is None else G_PRE[k]
                R = 0 if L is None else pre_at(L, k)
                dve.wait_ge(pre_hi, R * 16 + t * 8 + c + 1)
                V.scalar_tensor_tensor(hl[:, c, hs(t)], x[:, c, hs(t)], gv[:, g_at + c:g_at + c + 1],
                                       hh[:, c, hs(t)].bitcast(f32), ALU.mult, ALU.subtract).then_inc(pre_lo, 1)

            def residual(L, k, splits={}):
                R = post_at(L, k)
                for t in range(2):
                    dve.wait_ge(post_r, R * 2 + t + 1)
                    for c in range(DC):
                        i = R * 16 + t * 8 + c + 1
                        f, xc = facc[:, c, hs(t)], x[:, c, hs(t)]
                        V.scalar_tensor_tensor(f, f, gv[:, G_POST[k] + c:G_POST[k] + c + 1], accy[:, t, :],
                                               ALU.mult, ALU.mult).then_inc(post_mul, 1)
                        dve.wait_ge(post_mul, i)
                        V.tensor_tensor(xc, xc, f, ALU.add).then_inc(x_new, 1)
                        if c:
                            pre_low(L, k, t, c - 1)
                        if (t, c) in splits:
                            split_unit(L, splits[t, c])
                    pre_low(L, k, t, DC - 1)

            V.memset(eps[:, :], EPS).then_inc(eps_set, 1)
            V.memset(mx[:, :], 0.0).then_inc(w_lo, RAW)
            V.memset(nm[:, 0:1], 0.0).then_inc(stage_lo, 1)
            V.memset(nm[:, 1:2], 0.0).then_inc(o_lo, 1)
            dve.wait_ge(const_in, 64)
            for t in range(2):
                for c in range(DC):
                    pre_low(None, -1, t, c)
            with dve.Fori(0, DEPTH) as L:
                for w in range(SLOTS):
                    split_unit(L, w)
                dve.wait_ge(x_stored, L * 32 + 32)
                dve.wait_ge(squared, square_at(L, SQUARES[0]) - 1)
                dve.wait_ge(tab_in, L * 16 + 16)
                dve.wait_ge(gains_in, L * 16 + 16)
                dve.wait_ge(pads, L * 2 + 2)

                def conv_taps(j):
                    dve.wait_ge(u_done, L * 8 + 2 * j + 2)
                    if j:
                        dve.wait_ge(cv_lo, L * 8 + 2 * j)
                    w = [gv[:, G_TAP + 3 * j + k:G_TAP + 3 * j + k + 1] for k in range(3)]
                    V.tensor_scalar(cv[:, :], uu[:, 1:SEQ + 1], w[1], None, ALU.mult).then_inc(tap, 1)
                    for i, k in ((1, 0), (2, 2)):
                        dve.wait_ge(tap, L * 12 + 3 * j + i)
                        V.scalar_tensor_tensor(cv[:, :], uu[:, k:SEQ + k], w[k], cv[:, :], ALU.mult, ALU.add).then_inc(tap, 1)

                def conv_gate(j):
                    dve.wait_ge(tap, L * 12 + 3 * j + 3)
                    dve.wait_ge(in_act, L * 16 + outputs_of(BY_ACT, IN_OUTS.index((IN_KIND.index(("B", j)), 1)) + 1))
                    V.tensor_tensor(cv[:, :], cv[:, :], bb[:, j % 2, :], ALU.mult).then_inc(cv_raw, 1)

                def conv_norm(j):
                    for t in range(2):
                        dve.wait_ge(cv_r, L * 8 + 2 * j + t + 1)
                        V.scalar_tensor_tensor(cv[:, hs(t)], cv[:, hs(t)], gv[:, G_CONV + j:G_CONV + j + 1],
                                               cvr[:, t, :], ALU.mult, ALU.mult).then_inc(cv_y, 1)

                def conv_low(j):
                    for t in range(2):
                        dve.wait_ge(cv_hi, L * 8 + 2 * j + t + 1)
                        low(cyl[:, hs(t)], cv[:, hs(t)], cyh[:, hs(t)]).then_inc(cv_lo, 1)

                for n in range(len(IN_OUTS)):
                    u, t = IN_OUTS[n]
                    kind, j = IN_KIND[u]
                    if n in (0, 4):
                        dve.wait_ge(pre_r, pre_at(L, -1) * 2 + t + 1)
                    if kind is not None and kind not in BY_ACT:
                        dve.wait_ge(in_out, L * 36 + n + 1)
                    src = ps[:, n % 4, :]
                    if kind in ("q", "kv"):
                        V.tensor_tensor(zr[:, j + (QC if kind == "kv" else 0), hs(t)], src, rpre[:, t, :], ALU.mult).then_inc(in_dve, 1)
                    if kind == "u":
                        dve.wait_ge(in_act, L * 16 + outputs_of(BY_ACT, n))
                        V.tensor_tensor(uu[:, 1 + t * HALF:1 + (t + 1) * HALF], src, cc[:, hs(t)], ALU.mult).then_inc(u_raw, 1)
                    if kind == "kr":
                        one, both = slice(NOPE, QK), slice(NOPE, P)
                        if t == 1:
                            dve.wait_ge(kr_lo, L * 4 + 2)
                            dve.wait_ge(kr_hi, L * 4 + 2)
                        V.tensor_tensor(sq[one, 0, :], ps[QK:P, n % 4, :], tab[QK:P, hs(t)], ALU.mult)
                        V.tensor_tensor(kr[one, :], ps[one, n % 4, :], tab[one, hs(t)], ALU.mult).then_inc(kr_cos, 1)
                        dve.wait_ge(kr_cos, L * 2 + t + 1)
                        V.tensor_tensor(kr[QK:P, :], kr[one, :], sq[one, 0, :], ALU.add).then_inc(kr_sum, 1)
                        dve.wait_ge(kr_sum, L * 2 + t + 1)
                        V.tensor_tensor(kr[one, :], kr[one, :], sq[one, 0, :], ALU.add).then_inc(in_dve, 1)
                        dve.wait_ge(in_dve, L * 12 + outputs_of(BY_DVE, n + 1))
                        V.tensor_tensor(kr[both, :], kr[both, :], rpre[both, t, :], ALU.mult).then_inc(kr_f, 1)
                        for a in range(2):
                            dve.wait_ge(kr_hi, L * 4 + 2 * t + a + 1)
                            low(kl[both, a, hs(t)], kr[both, :], kh[both, a, hs(t)]).then_inc(kr_lo, 1)
                    for i in range(4):
                        if LY_AT[i] == n:
                            dve.wait_ge(lr_r, L * 4 + i + 1)
                            for c in LORA[i % 2]:
                                z = zr[:, c, hs(i // 2)]
                                V.scalar_tensor_tensor(z, z, gv[:, G_Q + c:G_Q + c + 1], accy[:, i % 2, :],
                                                       ALU.mult, ALU.mult).then_inc(lr_y, 1)
                    for j in range(CHUNKS - 1):
                        if CLO_AT[j] + 1 == n:
                            conv_low(j)
                        if CY_AT[j] == n:
                            conv_norm(j)
                    for j in range(CHUNKS - 1):
                        if MULT_AT[j] == n:
                            conv_taps(j)
                            conv_gate(j)
                    if t == 1 and u + SLOTS < IN_UNITS:
                        split_unit(L, u + SLOTS)
                    if n == 31:
                        split_head(L, 0, 0)

                def latents(cs):
                    for c in cs:
                        dve.wait_ge(lr_hi, L * 5 + (3, 4, 0, 1, 2).index(c) + 1)
                        low(hl[:, c, :], zr[:, c, :], hh[:, c, :]).then_inc(lr_lo, 1)

                def keys_and_values(h, a, t, bank):
                    dve.wait_ge(k_hi, (L * HEADS + h) * 2 + t + 1)
                    low(kl[0:NOPE, a, hs(t)], ps[0:NOPE, bank, :], kh[0:NOPE, a, hs(t)]).then_inc(k_lo, 1)

                def queries(h, a, t, bank):
                    dve.wait_ge(q_out, (L * HEADS + h) * 2 + t + 1)
                    V.tensor_tensor((tmp, xacc)[t][:, :], ps[:, bank, :], tab[:, hs(t)], ALU.mult).then_inc(q_f, 1)

                def low_of_queries(h, a, t):
                    dve.wait_ge(q_hi, (L * HEADS + h) * 2 + t + 1)
                    low(hl[:, HA + a, hs(t)], (tmp, xacc)[t][:, :], hh[:, HA + a, hs(t)]).then_inc(q_lo, 1)

                def values_by_token(h, a, t, bank):
                    at = (slice(None), slice(None), slice(2 * a * V_DIM, (2 * a + 1) * V_DIM))
                    dve.wait_ge(v_hi, L * HEADS + h + 1)
                    low(vl[at], ps[:, bank, :].rearrange("p (c d) -> p c d", c=STEPS), vh[at]).then_inc(v_lo, 1)

                PIECES = {0: (keys_and_values, 0), 1: (keys_and_values, 1), 2: (queries, 0),
                          3: (values_by_token, 0), 4: (queries, 1)}

                def maxima(h, s):
                    S = step(L, h, s)
                    dve.wait_ge(s_out, S + 1)
                    V.reduce_max(mx[:, s % 2:s % 2 + 1], ps[:, 2 * (s % 2):2 * (s % 2) + 2, :].rearrange("p b n -> p (b n)"),
                                 AX.X).then_inc(s_max, 1)
                    dve.wait_ge(s_max, S + 1)
                    V.tensor_scalar(nm[:, s % 2:s % 2 + 1], mx[:, s % 2:s % 2 + 1], -SCALE, None, ALU.mult).then_inc(s_neg, 1)

                def low_of_transposed(h, s):
                    G = s // 2
                    for b in range(2):
                        dve.wait_ge(t_hi, 2 * step(L, h, s) + b + 1)
                        at = (slice(None), G % 2, slice(4 * b, 4 * b + 4), slice((s % 2) * P, (s % 2 + 1) * P))
                        V.tensor_tensor(ptl[at], ps[:, 4 + b, :].rearrange("p (c q) -> p c q", c=4),
                                        pth[at].bitcast(f32), ALU.subtract).then_inc(t_lo, 1)

                def output(h, a, t, j):
                    dve.wait_ge(o_r, (L * HEADS + h) * 2 + t + 1)
                    V.scalar_tensor_tensor(of[rows(a), :], of[rows(a), :], gatt[rows(a), bass.ds(j, 1)],
                                           sq[rows(a), 1, :], ALU.mult, ALU.mult).then_inc(o_y, 1)

                def low_of_output(h, a, t):
                    dve.wait_ge(o_hi, (L * HEADS + h) * 2 + t + 1)
                    low(yl[rows(a), :], of[rows(a), :], yh[rows(a), :]).then_inc(o_lo, 1)

                def head(j, a, first=False, last=False):
                    h = 2 * j + a
                    before = j if a else j - 1
                    for s in range(STEPS):
                        low_of_transposed(h, s)
                        if s + 2 < STEPS:
                            maxima(h, s + 2)
                        elif not last:
                            maxima(h + 1, s + 2 - STEPS)
                        if s in PIECES and not last:
                            make, t = PIECES[s]
                            make(h + 1, 1 - a, t, 5)
                        if s in (3, 5) and not last:
                            low_of_queries(h + 1, 1 - a, s // 4)
                        if not first:
                            if s == 0:
                                output(h - 1, 1 - a, 0, before)
                            if s == 1:
                                low_of_output(h - 1, 1 - a, 0)
                            if s == 4:
                                output(h - 1, 1 - a, 1, before)
                            if s == 5:
                                low_of_output(h - 1, 1 - a, 1)
                        if s == 6 and not last and not (isinstance(h, int) and h == HEADS - 2):
                            split_head(L, h + 2, a)
                        if last and s == 5:
                            split_unit(L, O_AT)
                        if last and s == 6:
                            split_unit(L, O_AT + 1)
                        if last and s == 7:
                            split_unit(L, O_AT + 2)
                            split_unit(L, O_AT + 3)

                conv_taps(CHUNKS - 1)
                latents((3, 4))
                conv_gate(CHUNKS - 1)
                latents((0, 1, 2))
                keys_and_values(0, 0, 0, 0)
                keys_and_values(0, 0, 1, 1)
                queries(0, 0, 0, 2)
                low_of_queries(0, 0, 0)
                conv_norm(CHUNKS - 1)
                conv_low(CHUNKS - 1)
                values_by_token(0, 0, 0, 3)
                queries(0, 0, 1, 6)
                low_of_queries(0, 0, 1)
                maxima(0, 0)
                maxima(0, 1)
                split_head(L, 1, 1)
                head(0, 0, first=True)
                head(0, 1)
                with dve.Fori(1, PAIRS - 1) as j:
                    head(j, 0)
                    head(j, 1)
                head(PAIRS - 1, 0)
                head(PAIRS - 1, 1, last=True)
                output(HEADS - 1, 1, 0, PAIRS - 1)
                low_of_output(HEADS - 1, 1, 0)
                output(HEADS - 1, 1, 1, PAIRS - 1)
                low_of_output(HEADS - 1, 1, 1)

                for w in range(O_AT + SLOTS, O_AT + 2 * SLOTS + 1):
                    split_unit(L, w)
                dve.wait_ge(x_back, L * 16 + 16)
                residual(L, 0, {(0, 3): M_AT + 1, (0, 6): M_AT + 2, (1, 0): M_AT + 3})

                def hidden(g, t):
                    for i in range(2):
                        k = L * 4 * GROUPS + g * 4 + 2 * t + i
                        dve.wait_ge(up_out, k + 1)
                        V.scalar_tensor_tensor(accy[:, 1, :], ps[:, 2 * t + i, :], 0.0, rpre[:, t, :], ALU.max, ALU.mult).then_inc(up_v, 1)
                        dve.wait_ge(up_sq, k + 1)
                        low(gl[:, i, hs(t)], accy[:, 0, :], gh[:, i, hs(t)]).then_inc(up_lo, 1)

                def add(g, t, banks=4):
                    for m in range(DC):
                        dve.wait_ge(down_out, L * 16 * GROUPS + g * 16 + t * 8 + m + 1)
                        f = facc[:, m, hs(t)]
                        V.tensor_tensor(f, f, ps[:, 4 + m % banks, :], ALU.add).then_inc(down_add, 1)

                def split_two(g, at):
                    for i in range(2):
                        split_unit(L, M_AT + at + i, g)

                dve.wait_ge(pre_r, pre_at(L, 0) * 2 + 1)
                hidden(0, 0)
                dve.wait_ge(pre_r, pre_at(L, 0) * 2 + 2)
                hidden(0, 1)
                split_two(1, 0)
                dve.wait_ge(f_zero, L * 2 + 2)
                add(0, 0)
                with dve.Fori(1, GROUPS) as g:
                    hidden(g, 0)
                    add(g - 1, 1)
                    split_two(g, 2)
                    hidden(g, 1)
                    split_two(g + 1, 0)
                    add(g, 0)
                add(GROUPS - 1, 1, banks=2)
                split_stage(L, HEADS, gl[:, 0, :], gh[:, 0, :])
                split_unit(L, G_AT)
                split_unit(L, G_AT + 1)
                split_stage(L, HEADS + 1, gl[:, 1, :], gh[:, 1, :])
                residual(L, 1)

                def gates(n):
                    m, t = GATE_OUTS[n]
                    if n in (0, 2):
                        dve.wait_ge(pre_r, pre_at(L, 1) * 2 + t + 1)
                    dve.wait_ge(gate_out, L * 16 + n + 1)
                    if n:
                        dve.wait_ge(gate_y, L * 16 + n)
                    V.tensor_tensor(xacc[:, :], ps[:, n % 4 if n >= 4 else n % 2, :], rpre[:, t, :], ALU.mult).then_inc(gate_z, 1)
                    dve.wait_ge(gate_s, L * 16 + n + 1)
                    f = facc[:, m, hs(t)]
                    dve.wait_ge(e_copy, L * 16 + t * 8 + m + 1)
                    V.tensor_tensor(f, f, xacc[:, :], ALU.mult).then_inc(gate_y, 1)
                    w = G_AT + m + SLOTS
                    if t == 1 and w < UNITS:
                        split_unit(L, w)

                gates(0)
                gates(1)
                split_unit(L, G_AT + 2)
                split_unit(L, G_AT + 3)
                for n in range(2, 16):
                    gates(n)
                residual(L, 2)

        @block.gpsimd
        def _(pool):
            def add_square(L, e):
                acc = sum_of(e)
                pool.wait_ge(squared, square_at(L, e))
                if L is not None or sum_number(e):
                    pool.wait_ge(summed, sum_at(L, e) - 1)
                nc.gpsimd.tensor_tensor(acc, acc, sq[:, sum_number(e) % 2, :], ALU.add).then_inc(summed, 1)

            pool.wait_ge(eps_set, 1)
            for e in AHEAD:
                if not is_first(e):
                    add_square(None, e)
            with pool.Fori(0, DEPTH) as L:
                pool.wait_ge(x_stored, L * 32 + 32)
                pool.wait_ge(pre_lo, pre_at(L, -1) * 16 + 16)
                pool.wait_ge(squared, square_at(L, SQUARES[0]) - 1)
                nc.gpsimd.tensor_tensor(uu[:, 0:1], eps[:, :], eps[:, :], ALU.subtract).then_inc(pads, 1)
                nc.gpsimd.tensor_tensor(uu[:, SEQ + 1:SEQ + 2], eps[:, :], eps[:, :], ALU.subtract).then_inc(pads, 1)
                for n in range(len(IN_OUTS)):
                    u, t = IN_OUTS[n]
                    kind, j = IN_KIND[u]
                    if kind == "u":
                        k = L * 8 + 2 * j + t + 1
                        piece = uu[:, 1 + t * HALF:1 + (t + 1) * HALF]
                        pool.wait_ge(u_raw, k)
                        nc.gpsimd.tensor_tensor(piece, piece, rpre[:, t, :], ALU.mult).then_inc(u_once, 1)
                        pool.wait_ge(u_once, k)
                        nc.gpsimd.tensor_tensor(piece, piece, rpre[:, t, :], ALU.mult).then_inc(u_done, 1)
                    for j in range(CHUNKS):
                        if MULT_AT[j] == n:
                            pool.wait_ge(cv_raw, L * 4 + j + 1)
                            for t2 in range(2):
                                nc.gpsimd.tensor_tensor(cv[:, hs(t2)], cv[:, hs(t2)], rpre[:, t2, :], ALU.mult).then_inc(cv_done, 1)
                    for i in range(4):
                        if LSQ_AT[i] == n:
                            for c in LORA[i % 2][1:]:
                                add_square(L, ("lora", i, 0, c))
                pool.wait_ge(lr_lo, L * 5 + 5)
                nc.gpsimd.tensor_tensor(carry[:, :], eps[:, :], eps[:, :], ALU.add)
                nc.gpsimd.memset(vh[:, :, V_DIM:2 * V_DIM].bitcast(f32), 1.0).then_inc(v_ones, 1)
                nc.gpsimd.memset(vl[:, :, V_DIM:2 * V_DIM].bitcast(f32), 0.0).then_inc(v_ones, 1)
                for e in SQUARES:
                    if e[0] == "lora":
                        continue
                    if not is_first(e):
                        add_square(L, e)
                    if e[:2] == ("pre", 0) and e[3] == DC - 1:
                        t = e[2]
                        pool.wait_ge(x_new, post_at(L, 0) * 16 + t * 8 + 8)
                        nc.gpsimd.tensor_tensor(carry[:, :], eps[:, :], eps[:, :], ALU.add)
                        nc.gpsimd.memset(facc[:, :, hs(t)], 0.0).then_inc(f_zero, 1)


def kernel(**inputs):
    import concourse.bacc as _bacc
    from concourse.bass_utils import run_bass_kernel_spmd as _run

    a = {k: np.ascontiguousarray(v) for k, v in inputs.items()}

    def tiles(w, rows, cols):
        return np.stack([w[:, r:r + P][:, :, cols] for r in rows], axis=2)

    k_all = range(0, D, P)
    swap = np.r_[ROPE // 2:ROPE, 0:ROPE // 2]
    at_kr = Q_RANK + KV_RANK
    at_b = at_kr + ROPE
    starts = {"q": 0, "kv": Q_RANK, "B": at_b, "C": at_b + CONV, "u": at_b + 2 * CONV}
    units = []
    for kind, c in IN_KIND:
        if kind == "kr":
            kr = at_kr + np.arange(ROPE)
            cols = np.concatenate([kr, kr, kr, kr[swap]])
        else:
            cols = starts[kind] + c * P + np.arange(P)
        units.append(tiles(a["w_in"], k_all, cols))
    for m in range(DC):
        units.append(tiles(a["w_out"], k_all, m * P + np.arange(P)))
    for g in range(GROUPS):
        for i in range(2):
            units.append(tiles(a["w_mlp_up"], k_all, (2 * g + i) * P + np.arange(P)))
        for h in range(2):
            units.append(np.concatenate([tiles(a["w_mlp_down"], (2 * g * P, (2 * g + 1) * P), m * P + np.arange(P))
                                         for m in range(4 * h, 4 * h + 4)], axis=2))
    for h in range(2):
        units.append(np.concatenate([tiles(a["w_ple_proj"], (0, P), m * P + np.arange(P))
                                     for m in range(4 * h, 4 * h + 4)], axis=2))
    for m in range(DC):
        units.append(tiles(a["w_ple_gate"], k_all, m * P + np.arange(P)))
    w_units = np.ascontiguousarray(np.stack(units, axis=1).reshape(DEPTH, UNITS, P, UNIT))

    heads = []
    for h in range(HEADS):
        nope = h * QK + np.arange(NOPE)
        rope = h * QK + NOPE + np.arange(ROPE)
        q = tiles(a["w_q_b"], range(0, Q_RANK, P), np.concatenate([nope, rope, rope[swap]]))
        kv = tiles(a["w_kv_b"], range(0, KV_RANK, P), h * (NOPE + V_DIM) + np.arange(NOPE + V_DIM))
        heads.append(np.concatenate([q, kv], axis=2))
    w_head = np.ascontiguousarray(np.stack(heads, axis=1).reshape(DEPTH, HEADS, P, HEAD_UNIT))

    def columns(v):
        return v.reshape(DEPTH, -1, P).transpose(0, 2, 1)

    following = [(i + 1) % DEPTH for i in range(DEPTH)]
    taps = a["w_conv"].reshape(DEPTH, 3, CHUNKS, P).transpose(0, 3, 2, 1).reshape(DEPTH, P, 3 * CHUNKS)
    gains = np.ascontiguousarray(np.concatenate(
        [columns(a["g_q_a"]), columns(a["g_kv_a"]), columns(a["g_attn_out"]), columns(a["g_conv_out"]),
         columns(a["g_post_mix"]), columns(a["g_pre_mlp"]), columns(a["g_post_mlp"]), columns(a["g_pre_ple"]),
         columns(a["g_post_ple"]), columns(a["g_pre_mix"][following]), taps, columns(a["g_pre_mix"])], axis=2))
    assert gains.shape[2] == G_ALL

    inv_freq = 1.0 / (np.float32(10000.0) ** (np.arange(0, ROPE, 2, dtype=np.float32) / np.float32(ROPE)))
    angle = inv_freq.astype(np.float32)[:, None] * np.arange(SEQ, dtype=np.float32)[None, :]
    cos, sin = np.cos(angle).astype(np.float32), np.sin(angle).astype(np.float32)
    table = np.concatenate([np.ones((NOPE, SEQ), np.float32), cos, cos, -sin, sin], axis=0)
    consts = np.zeros((P, 5, P), np.float32)
    consts[:, 0] = np.eye(P)
    consts[:, 1] = 1.0
    for i in range(2):
        consts[64 * i:64 * i + 64, 2, 64 * i:64 * i + 64] = 1.0
        consts[64 * i:64 * i + 64, 3 + i, 64 * i:64 * i + 64] = 1.0
        consts[64 * (1 - i), 3 + i, 64 * i:64 * i + 64] = V_DIM * EPS

    arrays = {
        "x_in": np.ascontiguousarray(a["x"].reshape(SEQ, DC, P).transpose(2, 1, 0)),
        "w_units": w_units, "w_head": w_head,
        "p_in": np.ascontiguousarray(a["p"].reshape(DEPTH, SEQ, PLE // P, P).transpose(0, 2, 3, 1)),
        "gains": gains, "table": table, "consts": consts,
    }
    nc = _bacc.Bacc("TRN2", target_bir_lowering=False, num_devices=1)
    args = [nc.dram_tensor(k, v.shape, mybir.dt.from_np(v.dtype), kind="ExternalInput").ap() for k, v in arrays.items()]
    args.append(nc.dram_tensor("out", [P, DC, SEQ], mybir.dt.float32, kind="ExternalOutput").ap())
    encoder(nc, *args)
    r = _run(nc, [arrays], core_ids=[0])
    got = r.results[0]["out"]
    return np.ascontiguousarray(got.transpose(2, 1, 0)).reshape(1, SEQ, D)
```

```python
import math
from contextlib import ExitStack

import concourse.bass as bass
import numpy as np
from concourse import mybir

DEPTH, SEQ, D = 2, 1024, 1024
P = 128
HALF = 512
DC = D // P
HEADS, NOPE, ROPE, V_DIM = 8, 64, 32, 64
QK = NOPE + ROPE
Q_RANK, KV_RANK = 384, 256
QC, KVC = Q_RANK // P, KV_RANK // P
CONV = 512
D_FF = 4096
PLE = 256
EPS = 1e-6
UNIT = 1024
SLOTS = 4
RAW = 2

PAIRS = HEADS // 2
IN_UNITS = QC + KVC + 1 + 3 * (CONV // P)
OUT_UNITS = DC
GROUPS = D_FF // (2 * P)
MLP_UNITS = 4 * GROUPS
E_UNITS = 2
GATE_UNITS = DC
O_AT = IN_UNITS
M_AT = O_AT + OUT_UNITS
E_AT = M_AT + MLP_UNITS
G_AT = E_AT + E_UNITS
UNITS = G_AT + GATE_UNITS
HEAD_UNIT = 5 * P
HEAD_SLOT = IN_UNITS % SLOTS
STAGES = HEADS + PLE // P
STEPS = SEQ // P
MIX_STORED = 16 * 2 * (CONV // P + 2 * HEADS)

IN_KIND = ([("q", c) for c in range(QC)] + [("kv", c) for c in range(KVC)]
           + [(k, j) for j in range(3) for k in ("C", "u", "B")] + [("kr", 0), ("C", 3), ("u", 3), ("B", 3)])
IN_BLOCKS = [list(range(a, min(a + SLOTS, IN_UNITS))) for a in range(0, IN_UNITS, SLOTS)]
IN_OUTS = [(u, t) for b in IN_BLOCKS for t in range(2) for u in b]
OUT_OUTS = [(m, t) for b in (range(4), range(4, 8)) for t in range(2) for m in b]
GATE_OUTS = [(m, t) for b in ((0, 1), (2, 3), (4, 5, 6, 7)) for t in range(2) for m in b]
BY_ACT = ("C", "B")
BY_DVE = ("q", "kv", "kr")


def outputs_of(kinds, n):
    return sum(IN_KIND[u][0] in kinds for u, _ in IN_OUTS[:n])


CHUNKS = CONV // P
MULT_AT = [15, 22, 29, 35]
CSTAT_AT = [17, 24, 31]
CY_AT = [18, 25, 32]
CLO_AT = [19, 26, 33]
HEAD_AT = 31
LSQ_AT = [13, 13, 18, 19]
LSTAT_AT = [15, 16, 20, 21]
LF_AT = [16, 17, 21, 22]
LY_AT = [17, 18, 22, 23]
LATENTS = [(c, t) for t in range(2) for c in (3, 4)] + [(c, t) for t in range(2) for c in (0, 1, 2)]
LORA = [range(QC), range(QC, QC + KVC)]

AHEAD = [("pre", -1, t, c) for t in range(2) for c in range(DC)]
def residual_chunks(k, t, cs):
    return [("pre", k, t, c) for c in cs]


OUT_TAIL = [("out", n) for n in range(13)] + [("factor", 0)] + residual_chunks(0, 0, range(1)) + [("out", 13)]
OUT_TAIL += residual_chunks(0, 0, range(1, 4)) + [("out", 14)] + residual_chunks(0, 0, range(4, 6)) + [("out", 15)]
OUT_TAIL += residual_chunks(0, 0, range(6, 8)) + [("factor", 1)] + residual_chunks(0, 1, range(DC))
OUT_TAIL_DVE = [("out", n) for n in range(13)] + [("factor", 0)] + residual_chunks(0, 0, range(3)) + [("out", 13)]
OUT_TAIL_DVE += residual_chunks(0, 0, range(3, 6)) + [("out", 14)] + residual_chunks(0, 0, range(6, 8)) + [("out", 15)]
OUT_TAIL_DVE += [("factor", 1)] + residual_chunks(0, 1, range(DC))
MLP_TAIL = [("sum", 0, c) for c in range(DC)] + [("p", 0), ("unit", 0), ("factor", 0)]
MLP_TAIL += [("sum", 1, c) for c in range(4)]
for c in range(DC):
    MLP_TAIL += residual_chunks(1, 0, (c,)) + [("embed", 0, c)]
    MLP_TAIL += [("sum", 1, 4 + c)] if c < 4 else []
    MLP_TAIL += [("p", 1)] if c == 2 else [("unit", 1)] if c == 3 else []
MLP_TAIL += [("factor", 1)] + residual_chunks(1, 1, (0, 1)) + [("pre_factor", 0), ("gate", 0)] + residual_chunks(1, 1, (2,))
MLP_TAIL += [("use", 0), ("gate", 1)] + residual_chunks(1, 1, (3,)) + [("use", 1)]
for c in range(DC):
    MLP_TAIL += [("embed", 1, c)] + (residual_chunks(1, 1, (4 + c,)) if c < 4 else [])
    MLP_TAIL += [("unit", 2)] if c == 4 else []
MLP_TAIL += [("unit", 3), ("pre_factor", 1)]
MLP_TAIL_DVE = [("add", c) for c in range(2)] + [("p", 0)] + [("add", c) for c in range(2, 6)] + [("unit", 0), ("factor", 0)] + residual_chunks(1, 0, (0,))
MLP_TAIL_DVE += [("add", 6)] + residual_chunks(1, 0, (1,)) + [("add", 7)] + residual_chunks(1, 0, (2, 3)) + [("p", 1)]
MLP_TAIL_DVE += residual_chunks(1, 0, (4,)) + [("unit", 1)] + residual_chunks(1, 0, (5, 6, 7)) + [("factor", 1)]
MLP_TAIL_DVE += residual_chunks(1, 1, (0, 1)) + [("gate", 0)] + residual_chunks(1, 1, (2,)) + [("use", 0), ("gate", 1)]
MLP_TAIL_DVE += residual_chunks(1, 1, (3,)) + [("use", 1)] + residual_chunks(1, 1, range(4, 8)) + [("unit", 2), ("unit", 3)]
GATE_TAIL = [(e, n) for n in range(2, 13) for e in ("gate", "use", "split")] + [("factor", 0)]
GATE_TAIL_DVE = list(GATE_TAIL)
GATE_TAIL += [("gate", 13)] + residual_chunks(2, 0, (0,)) + [("use", 13), ("split", 13)] + residual_chunks(2, 0, (1,))
GATE_TAIL += [("gate", 14)] + residual_chunks(2, 0, (2,)) + [("use", 14), ("gate", 15)] + residual_chunks(2, 0, (3,))
GATE_TAIL += [("use", 15), ("split", 14)] + residual_chunks(2, 0, (4,)) + [("split", 15)] + residual_chunks(2, 0, (5, 6, 7))
GATE_TAIL += [("factor", 1)] + residual_chunks(2, 1, range(DC))
GATE_TAIL_DVE += [("gate", 13)] + residual_chunks(2, 0, (0,)) + [("use", 13)] + residual_chunks(2, 0, (1,)) + [("gate", 14), ("split", 13)]
GATE_TAIL_DVE += residual_chunks(2, 0, (2,)) + [("use", 14), ("gate", 15)] + residual_chunks(2, 0, (3,)) + [("use", 15), ("split", 14)]
GATE_TAIL_DVE += residual_chunks(2, 0, (4, 5)) + [("split", 15)] + residual_chunks(2, 0, (6, 7))
GATE_TAIL_DVE += [("factor", 1)] + residual_chunks(2, 1, range(DC))
SQUARES = [("lora", i, 0, c) for i in range(4) for c in LORA[i % 2]]
SQUARES += [e if e[0] == "pre" else ("post", 0) + OUT_OUTS[e[1]][::-1] for e in OUT_TAIL if e[0] != "factor"]
SQUARES += [e if e[0] == "pre" else ("post", 1) + e[1:] if e[0] == "sum" else ("post", 2) + GATE_OUTS[e[1]][::-1]
            for e in MLP_TAIL if e[0] in ("pre", "sum", "use")]
SQUARES += [e if e[0] == "pre" else ("post", 2) + GATE_OUTS[e[1]][::-1] for e in GATE_TAIL if e[0] in ("pre", "use")]


def is_first(e):
    return e[3] == (QC if e[0] == "lora" and e[1] % 2 else 0)


def square_number(e):
    return (AHEAD if e in AHEAD else SQUARES).index(e)


def sum_number(e):
    where = AHEAD if e in AHEAD else SQUARES
    return sum(not is_first(o) for o in where[:where.index(e)])


SUMS = sum(not is_first(e) for e in SQUARES)
SUMS_AHEAD = sum(not is_first(e) for e in AHEAD)
assert SUMS % 2 == 0 and SUMS_AHEAD % 2 == 0

G_Q, G_KV, G_ATT, G_CONV = 0, 3, 5, 9
G_POST = [13, 29, 45]
G_PRE = [21, 37, 53]
G_TAP = 61
G_FIRST = 73
G_ALL = 81


def encoder(nc, x_in, w_units, w_head, p_in, gains, table, consts, out):
    f32, f32r = mybir.dt.float32, mybir.dt.float32r
    ALU, ACT, AX = mybir.AluOpType, mybir.ActivationFunctionType, mybir.AxisListType
    SCALE = 1.0 / math.sqrt(QK)
    ctx = ExitStack()

    def sb(name, shape, dt, where=ctx):
        return where.enter_context(nc.sbuf_tensor(name, shape, dt))

    def sem(name):
        return ctx.enter_context(nc.semaphore(name))

    def dram(name, shape, dt):
        return nc.dram_tensor(name, shape, dt, kind="Internal").ap()

    def hs(t):
        return slice(t * HALF, (t + 1) * HALF)

    with ctx:
        raw = sb("raw", [P, RAW, UNIT], f32)
        wh = sb("wh", [P, SLOTS, 8, P], f32r)
        wl = sb("wl", [P, SLOTS, 8, P], f32r)
        stage = sb("stage", [P, UNIT], f32)
        hh = sb("hh", [P, DC, SEQ], f32r)
        hl = sb("hl", [P, DC, SEQ], f32r)
        rpre = sb("rpre", [P, 2, HALF], f32)
        sq = sb("sq", [P, 2, HALF], f32)
        accy = sb("accy", [P, 2, HALF], f32)
        xacc = sb("xacc", [P, HALF], f32)
        tmp = sb("tmp", [P, HALF], f32)
        gv = sb("gv", [P, G_ALL], f32)
        cst = sb("cst", [P, 5, P], f32)
        eps = sb("eps", [P, 1], f32)
        carry = sb("carry", [P, 1], f32)
        mx = sb("mx", [P, 2], f32)
        nm = sb("nm", [P, 2], f32)
        ident, ones, blocks = cst[:, 0, :], cst[:, 1, :], cst[:, 2, :]
        HA, HB = 5, 7

        with ExitStack() as att:
            with ExitStack() as inp:
                zr = sb("zr", [P, QC + KVC, SEQ], f32, inp)
                cc = sb("cc", [P, SEQ], f32, inp)
                uu = sb("uu", [P, SEQ + 2], f32, inp)
                bb = sb("bb", [P, 2, SEQ], f32, inp)
                cv = sb("cv", [P, SEQ], f32, inp)
                cvs = sb("cvs", [P, 2, HALF], f32, inp)
                cvr = sb("cvr", [P, 2, HALF], f32, inp)
                cyh = sb("cyh", [P, SEQ], f32r, inp)
                cyl = sb("cyl", [P, SEQ], f32r, inp)
                kr = sb("kr", [P, HALF], f32, inp)
            vh = sb("vh", [P, 8, 3 * V_DIM], f32r, att)
            vl = sb("vl", [P, 8, 3 * V_DIM], f32r, att)
            pr = sb("pr", [P, 2, SEQ], f32, att)
            pth = sb("pth", [P, 2, 8, 256], f32r, att)
            ptl = sb("ptl", [P, 2, 8, 256], f32r, att)
            of = sb("of", [P, HALF], f32, att)
            yh = sb("yh", [P, HALF], f32r, att)
            yl = sb("yl", [P, HALF], f32r, att)
            sb("gap", [P, 16], f32, att)
            kh = sb("kh", [P, 2, SEQ], f32r, att)
            kl = sb("kl", [P, 2, SEQ], f32r, att)
            tab = sb("tab", [P, SEQ], f32, att)
        gh = sb("gh", [P, 2, SEQ], f32r)
        gl = sb("gl", [P, 2, SEQ], f32r)
        xf = sb("xf", [P, 2, 2, DC, HALF], f32)
        x, facc = xf[:, :, 0, :, :], xf[:, :, 1, :, :]

        ps = ctx.enter_context(nc.psum_tensor("ps", [P, 8, HALF], f32))
        mix_hi = dram("mix_hi", [8, P, SEQ], f32)
        mix_lo = dram("mix_lo", [8, P, SEQ], f32)

        const_in = sem("const_in")
        eps_set = sem("eps_set")
        gains_in = sem("gains_in")
        tab_in = sem("tab_in")
        w_in = [sem(f"w_in{i}") for i in range(RAW)]
        w_hi = sem("w_hi")
        w_lo = sem("w_lo")
        stage_in = sem("stage_in")
        stage_hi = sem("stage_hi")
        stage_lo = sem("stage_lo")
        x_first = [sem(f"x_first{i}") for i in range(4)]
        x_back = [sem(f"x_back{t}") for t in range(2)]
        x_stored = [sem(f"x_stored{t}") for t in range(2)]
        squared = sem("squared")
        summed = sem("summed")
        pre_hi = sem("pre_hi")
        pre_lo = sem("pre_lo")
        pre_stat = sem("pre_stat")
        pre_ln = sem("pre_ln")
        pre_r = sem("pre_r")
        post_stat = sem("post_stat")
        post_ln = sem("post_ln")
        post_r = sem("post_r")
        post_mul = sem("post_mul")
        x_new = sem("x_new")
        in_out = sem("in_out")
        in_act = sem("in_act")
        in_dve = sem("in_dve")
        kr_cos = sem("kr_cos")
        kr_sum = sem("kr_sum")
        kr_f = sem("kr_f")
        kr_hi = sem("kr_hi")
        kr_lo = sem("kr_lo")
        u_raw = sem("u_raw")
        u_once = sem("u_once")
        u_done = sem("u_done")
        pads = sem("pads")
        tap = sem("tap")
        cv_raw = sem("cv_raw")
        cv_done = sem("cv_done")
        cv_sq = sem("cv_sq")
        cv_stat = sem("cv_stat")
        cv_ln = sem("cv_ln")
        cv_r = sem("cv_r")
        cv_y = sem("cv_y")
        cv_hi = sem("cv_hi")
        cv_lo = sem("cv_lo")
        mix_stored = sem("mix_stored")
        lr_stat = sem("lr_stat")
        lr_ln = sem("lr_ln")
        lr_r = sem("lr_r")
        lr_y = sem("lr_y")
        lr_hi = sem("lr_hi")
        lr_lo = sem("lr_lo")
        v_ones = sem("v_ones")
        kv_out = sem("kv_out")
        k_hi = sem("k_hi")
        k_lo = sem("k_lo")
        v_f = sem("v_f")
        v_out = sem("v_out")
        v_hi = sem("v_hi")
        v_lo = sem("v_lo")
        q_out = sem("q_out")
        q_f = sem("q_f")
        q_hi = sem("q_hi")
        q_lo = sem("q_lo")
        s_out = sem("s_out")
        s_max = sem("s_max")
        s_neg = sem("s_neg")
        s_exp = sem("s_exp")
        t_out = sem("t_out")
        t_hi = sem("t_hi")
        t_lo = sem("t_lo")
        pv_out = sem("pv_out")
        o_sq = sem("o_sq")
        o_copy = sem("o_copy")
        o_var = sem("o_var")
        o_ln = sem("o_ln")
        o_r = sem("o_r")
        o_y = sem("o_y")
        o_hi = sem("o_hi")
        o_lo = sem("o_lo")
        mix_in = sem("mix_in")
        mix_56 = sem("mix_56")
        mix_last = sem("mix_last")
        mix_out = sem("mix_out")
        mix_copy = sem("mix_copy")
        up_out = sem("up_out")
        up_v = sem("up_v")
        up_sq = sem("up_sq")
        up_hi = sem("up_hi")
        up_lo = sem("up_lo")
        down_out = sem("down_out")
        down_add = sem("down_add")
        f_zero = sem("f_zero")
        e_out = sem("e_out")
        e_copy = sem("e_copy")
        gate_out = sem("gate_out")
        gate_z = sem("gate_z")
        gate_s = sem("gate_s")
        gate_y = sem("gate_y")

        NORMS = 3

        def pre_at(L, k):
            return L * NORMS + (k + 1)

        def post_at(L, k):
            return L * NORMS + k

        def last_read(L, w, g=0):
            if w < O_AT:
                return in_out, L * len(IN_OUTS) + IN_OUTS.index((w, 1)) + 1
            if w < M_AT:
                return mix_out, L * 16 + OUT_OUTS.index((w - O_AT, 1)) + 1
            if w < M_AT + 2:
                return up_out, (L * GROUPS + g) * 4 + 3 + (w - M_AT)
            if w < M_AT + 4:
                return down_out, (L * GROUPS + g) * 16 + 12 + 4 * (w - M_AT - 2)
            if w < G_AT:
                return e_out, L * 16 + 12 + 4 * (w - E_AT)
            return gate_out, L * 16 + GATE_OUTS.index((w - G_AT, 1)) + 1

        def slot_free(L, w, g=0):
            if w == O_AT:
                return q_out, (L + 1) * 2 * HEADS - 2
            if not isinstance(g, int):
                return last_read(L, w, g - 1)
            if M_AT <= w < E_AT:
                return last_read(L, w, g - 1) if g > 0 else last_read(L, w - SLOTS)
            if E_AT <= w < E_AT + SLOTS:
                return last_read(L, M_AT + w - E_AT, GROUPS - 1)
            return last_read(L, w - SLOTS)

        gatt = gv[:, G_ATT:G_ATT + PAIRS]

        def head_unit(a, low):
            ring, held = ((wh, hh), (wl, hl))[low]
            return held[:, HB, 0:HEAD_UNIT].rearrange("p (k m) -> p k m", k=5) if a else ring[:, HEAD_SLOT, 0:5, :]

        def rows(a):
            return slice(a * V_DIM, (a + 1) * V_DIM)

        def gate_of(n):
            return (tmp if n >= 12 else xacc)[:, :]

        def step(L, h, s):
            return (L * HEADS + h) * STEPS + s

        def square_at(L, e):
            return square_number(e) + 1 + (0 if L is None else L * len(SQUARES) + len(AHEAD))

        def sum_at(L, e):
            return sum_number(e) + 1 + (0 if L is None else L * SUMS + SUMS_AHEAD)

        def sum_of(e):
            kind, k, t, c = e
            if kind == "pre":
                return (xacc, tmp)[t][:, :]
            return accy[:, k % 2 if kind == "lora" else t, :]

        def last_of(kind, k, t):
            if kind == "lora":
                return (kind, k, 0, LORA[k % 2][-1])
            return (kind, k, t, DC - 1)

        block = ctx.enter_context(nc.Block())

        @block.sync
        def _(sp):
            def load(L, w, g=0):
                sp.wait_ge(w_lo, L * UNITS + g * 4 + w + 1)
                sp.dma_start(raw[:, w % RAW, :],
                             w_units[bass.ds(L, 1), bass.ds(g * 4 + w, 1), :, :].rearrange("a b p n -> p (a b n)")
                             ).then_inc(w_in[w % RAW], 16)

            def load_stage(L, k, src):
                sp.wait_ge(stage_lo, L * STAGES + k + 1)
                sp.dma_start(stage[:, 0:src.shape[1]], src).then_inc(stage_in, 16)

            def load_x(i):
                t, half = i // 2, slice(i % 2 * 4, i % 2 * 4 + 4)
                sp.dma_start(x[:, t, half, :], x_in[:, half, hs(t)]).then_inc(x_first[i], 16)

            sp.dma_start(gv[:, :], gains[0]).then_inc(const_in, 16)
            load(0, 0)
            load(0, 1)
            sp.dma_start(cst[:, :, :], consts).then_inc(const_in, 16)
            load_x(0)
            load(0, 2)
            load(0, 3)
            for i in range(1, 4):
                load_x(i)
            for t in range(2):
                for four in (slice(0, 4), slice(4, 8)):
                    sp.dma_start(out[:, four, hs(t)], x_in[:, four, hs(t)]).then_inc(x_stored[t], 16)

            with sp.Fori(0, DEPTH) as L:
                sp.wait_ge(pre_lo, pre_at(L, -1) * 16 + 16)
                sp.dma_start(gv[:, :], gains[bass.ds(L, 1), :, :].rearrange("a p n -> p (a n)")).then_inc(gains_in, 16)
                sp.wait_ge(squared, square_at(L, SQUARES[0]) - 1)
                sp.wait_ge(x_stored[1], L * 32 + 32)
                sp.dma_start(tab[:, :], table).then_inc(tab_in, 16)

                def load_head(h):
                    load_stage(L, h, w_head[bass.ds(L, 1), bass.ds(h, 1), :, :].rearrange("a b p n -> p (a b n)"))

                load_head(0)

                def store_conv(j):
                    sp.wait_ge(cv_lo, L * 8 + 2 * j + 2)
                    sp.dma_start(mix_hi[4 + j], cyh[:, :].bitcast(f32)).then_inc(mix_stored, 16)
                    sp.dma_start(mix_lo[4 + j], cyl[:, :].bitcast(f32)).then_inc(mix_stored, 16)

                stores_before = {15: 0, 18: 1}
                for w in range(SLOTS, O_AT + RAW):
                    if w in stores_before:
                        store_conv(stores_before[w])
                    load(L, w)

                load_head(1)
                store_conv(2)
                store_conv(3)

                def store_attention(j, a, t):
                    sp.wait_ge(o_lo, L * 2 * HEADS + j * 4 + a * 2 + t + 2)
                    for src, dst in ((yh, mix_hi), (yl, mix_lo)):
                        sp.dma_start(dst[bass.ds(j, 1), rows(a), hs(t)].rearrange("a p n -> p (a n)"),
                                     src[rows(a), :].bitcast(f32)).then_inc(mix_stored, 16)

                load_head(2)
                store_attention(0, 0, 0)
                load_head(3)
                store_attention(0, 0, 1)
                store_attention(0, 1, 0)
                with sp.Fori(1, PAIRS - 1) as j:
                    load_head(2 * j + 2)
                    store_attention(j - 1, 1, 1)
                    store_attention(j, 0, 0)
                    load_head(2 * j + 3)
                    store_attention(j, 0, 1)
                    store_attention(j, 1, 0)
                store_attention(PAIRS - 2, 1, 1)
                store_attention(PAIRS - 1, 0, 0)

                def load_mix(c, done):
                    sp.dma_start(hh[:, c, :].bitcast(f32), mix_hi[c]).then_inc(done, 16)
                    sp.dma_start(hl[:, c, :].bitcast(f32), mix_lo[c]).then_inc(done, 16)

                sp.wait_ge(q_out, (L + 1) * 2 * HEADS)
                sp.wait_ge(mix_stored, L * MIX_STORED + MIX_STORED - 96)
                for c in (4, 7, 0, 1, 2):
                    load_mix(c, mix_in)
                store_attention(PAIRS - 1, 0, 1)
                for w in range(O_AT + RAW, O_AT + SLOTS):
                    load(L, w)
                sp.wait_ge(s_out, (L + 1) * HEADS * STEPS)
                for c in (5, 6):
                    load_mix(c, mix_56)
                load(L, O_AT + SLOTS)
                store_attention(PAIRS - 1, 1, 0)
                store_attention(PAIRS - 1, 1, 1)
                sp.wait_ge(mix_stored, (L + 1) * MIX_STORED)
                load_mix(3, mix_last)
                sp.wait_ge(mix_copy, L * 16 + 1)
                for t in range(2):
                    sp.dma_start(x[:, t, :, :], out[:, :, hs(t)]).then_inc(x_back[t], 16)
                for w in range(O_AT + 5, M_AT):
                    load(L, w)
                load_stage(L, HEADS, p_in[bass.ds(L, 1), 0, :, :].rearrange("a p n -> p (a n)"))
                with sp.Fori(0, GROUPS) as g:
                    for i in range(4):
                        load(L, M_AT + i, g)
                for w in range(E_AT, G_AT + 2):
                    load(L, w)
                load_stage(L, HEADS + 1, p_in[bass.ds(L, 1), 1, :, :].rearrange("a p n -> p (a n)"))
                for w in range(G_AT + 2, UNITS + SLOTS):
                    load(L, w)
                for t in range(2):
                    for i in range(2):
                        four = slice(4 * i, 4 * i + 4)
                        sp.wait_ge(x_new, post_at(L, 2) * 16 + 8 * t + 4 * i + 4)
                        sp.dma_start(out[:, four, hs(t)], x[:, t, four, :]).then_inc(x_stored[t], 16)
            for t in range(2):
                sp.wait_ge(x_stored[t], 32 * (DEPTH + 1))
            for w in range(RAW):
                sp.wait_ge(w_in[w], (DEPTH * UNITS + SLOTS) // RAW * 16)
            sp.wait_ge(mix_stored, MIX_STORED * DEPTH)

        @block.tensor
        def _(pe):
            def split_product(dst, ah, al, bh, bl, start, stop):
                nc.tensor.matmul(dst, ah, bh, start=start, stop=False)
                nc.tensor.matmul(dst, ah, bl, start=False, stop=False)
                return nc.tensor.matmul(dst, al, bh, start=False, stop=stop)

            def unit_output(bank, slot, t, ready=None, order=range(DC)):
                for n, k in enumerate(order):
                    if ready is not None:
                        ready(k)
                    last = split_product(ps[:, bank, :], wh[:, slot, k, :], wl[:, slot, k, :],
                                         hh[:, k, hs(t)], hl[:, k, hs(t)], n == 0, n == DC - 1)
                return last

            def side_by_side(outputs, t, ready, done):
                for k in range(DC):
                    ready(k)
                    for bank, slot in outputs:
                        last = split_product(ps[:, bank, :], wh[:, slot, k, :], wl[:, slot, k, :],
                                             hh[:, k, hs(t)], hl[:, k, hs(t)], k == 0, k == DC - 1)
                        if k == DC - 1:
                            last.then_inc(done, 1)

            def two_tiles(bank, slot, m, t):
                for k in range(2):
                    tile = 2 * (m % 4) + k
                    last = split_product(ps[:, bank, :], wh[:, slot, tile, :], wl[:, slot, tile, :],
                                         gh[:, k, hs(t)], gl[:, k, hs(t)], k == 0, k == 1)
                return last

            def unit_ready(L, w, g=0):
                pe.wait_ge(w_lo, L * UNITS + g * 4 + w + 1 + RAW)

            def pre_stats(L, k, t):
                if k == -1:
                    pe.wait_ge(summed, L * SUMS + SUMS_AHEAD - (1 - t) * (DC - 1))
                else:
                    pe.wait_ge(summed, sum_at(L, last_of("pre", k, t)))
                if t == 1:
                    pe.wait_ge(pre_ln, pre_at(L, k) * 2 + 1)
                nc.tensor.matmul(ps[:, 7, :], ones, (xacc, tmp)[t][:, :], start=True, stop=True).then_inc(pre_stat, 1)

            def post_stats(L, k, t):
                pe.wait_ge(summed, sum_at(L, last_of("post", k, t)))
                if t == 1:
                    pe.wait_ge(post_ln, post_at(L, k) * 2 + 1)
                nc.tensor.matmul(ps[:, 6, :], ones, accy[:, t, :], start=True, stop=True).then_inc(post_stat, 1)

            def pre_ready(R, t):
                return lambda k: pe.wait_ge(pre_lo, R * 16 + t * 8 + k + 1)

            pe.wait_ge(const_in, 32)
            with pe.Fori(0, DEPTH) as L:
                R = pre_at(L, -1)

                def conv_stat(j, t):
                    pe.wait_ge(cv_sq, L * 8 + 2 * j + t + 1)
                    if j:
                        pe.wait_ge(cv_ln, L * 8 + 2 * j + t - 1)
                    nc.tensor.matmul(ps[:, 4 + t, :], blocks, cvs[:, t, :], start=True, stop=True).then_inc(cv_stat, 1)

                def lora_stat(i):
                    pe.wait_ge(summed, sum_at(L, last_of("lora", i, 0)))
                    if i:
                        pe.wait_ge(lr_ln, L * 4 + i)
                    nc.tensor.matmul(ps[:, 6, :], ones, accy[:, i % 2, :], start=True, stop=True).then_inc(lr_stat, 1)

                for n in range(SLOTS):
                    unit_ready(L, n)
                side_by_side([(n, n) for n in range(SLOTS)], 0, pre_ready(R, 0), in_out)
                pre_stats(L, -1, 0)
                for n in range(SLOTS, len(IN_OUTS) + 1):
                    if n < len(IN_OUTS):
                        u, t = IN_OUTS[n]
                        if t == 0:
                            unit_ready(L, u)
                        if n >= 4:
                            kind = IN_KIND[IN_OUTS[n - 4][0]][0]
                            if kind in BY_ACT:
                                pe.wait_ge(in_act, L * 16 + outputs_of(BY_ACT, n - 3))
                            elif kind == "u":
                                pe.wait_ge(u_raw, L * 8 + outputs_of("u", n - 3))
                            else:
                                pe.wait_ge(in_dve, L * 12 + outputs_of(BY_DVE, n - 3))
                        ready = pre_ready(R, t) if n == 4 else None
                        unit_output(n % 4, u % SLOTS, t, ready).then_inc(in_out, 1)
                        if n == 4:
                            pre_stats(L, -1, t)
                    for i in range(4):
                        if LSTAT_AT[i] == n:
                            lora_stat(i)
                    for j in range(CHUNKS - 1):
                        if CSTAT_AT[j] == n:
                            conv_stat(j, 0)
                            conv_stat(j, 1)

                def keys_and_values(h, a, t, bank):
                    if t == 0:
                        pe.wait_ge(stage_lo, L * STAGES + h + 2)
                    for k in range(KVC):
                        last = split_product(ps[:, bank, :], head_unit(a, 0)[:, 3 + k, :], head_unit(a, 1)[:, 3 + k, :],
                                             hh[:, QC + k, hs(t)], hl[:, QC + k, hs(t)], k == 0, k == KVC - 1)
                    last.then_inc(kv_out, 1)

                def queries(h, a, t, bank):
                    for k in range(QC):
                        last = split_product(ps[:, bank, :], head_unit(a, 0)[:, k, :], head_unit(a, 1)[:, k, :],
                                             hh[:, k, hs(t)], hl[:, k, hs(t)], k == 0, k == QC - 1)
                    last.then_inc(q_out, 1)

                def values_by_token(h, a, t, bank):
                    pe.wait_ge(v_f, (L * HEADS + h) * 2 + 2)
                    for c in range(STEPS):
                        last = nc.tensor.matmul(ps[:, bank, c * V_DIM:(c + 1) * V_DIM],
                                                accy[:, c // 4, (c % 4) * P:(c % 4 + 1) * P], cst[:, 0, V_DIM:P],
                                                start=True, stop=True)
                    last.then_inc(v_out, 1)

                PIECES = {0: (keys_and_values, 0, 6), 1: (keys_and_values, 1, 6), 3: (values_by_token, 0, 5),
                          4: (queries, 0, 7), 5: (queries, 1, 7)}

                def scores(h, a, s):
                    if s % 4 == 0:
                        pe.wait_ge(q_lo, (L * HEADS + h) * 2 + s // 4 + 1)
                    if s == 0:
                        pe.wait_ge(k_lo, (L * HEADS + h) * 2 + 2)
                    if isinstance(h, int) and h == 0 and s < 2:
                        if s == 0:
                            pe.wait_ge(v_f, L * HEADS * 2 + 2)
                        else:
                            pe.wait_ge(v_lo, L * HEADS + 1)
                    else:
                        pe.wait_ge(s_exp, step(L, h, s) - 1)
                    tok = slice(s * P, (s + 1) * P)
                    for kb in range(2):
                        last = split_product(ps[:, 2 * (s % 2) + kb, :], hh[:, HA + a, tok], hl[:, HA + a, tok],
                                             kh[:, a, hs(kb)], kl[:, a, hs(kb)], True, True)
                    last.then_inc(s_out, 1)

                def transposes(h, s, first, piece):
                    S = step(L, h, s)
                    pe.wait_ge(s_exp, S + 1)
                    for b in range(2):
                        if not (first and s == 0):
                            pe.wait_ge(t_lo, 2 * S + b - 1)
                        elif b == 0:
                            pe.wait_ge(cv_ln, L * 8 + 8)
                        if b == 1 and piece:
                            pe.wait_ge(v_lo, L * HEADS + h + 2)
                        for c in range(4):
                            last = nc.tensor.transpose(ps[:, 4 + b, c * P:(c + 1) * P],
                                                       pr[:, s % 2, (4 * b + c) * P:(4 * b + c + 1) * P], ident)
                        last.then_inc(t_out, 1)

                def bank_free(h, s, first):
                    H = L * HEADS + h
                    if s == 0:
                        if first:
                            pe.wait_ge(q_f, H * 2 + 2)
                        else:
                            pe.wait_ge(o_ln, H * 2 - 1)
                    if s == 1:
                        pe.wait_ge(k_lo, H * 2 + 3)
                    if s == 3:
                        pe.wait_ge(t_lo, 2 * step(L, h, s) + 2)
                    if s == 4 and not first:
                        pe.wait_ge(o_ln, H * 2)
                    if s == 5:
                        pe.wait_ge(q_f, H * 2 + 3)

                def values(h, a, G, part):
                    if part == 0:
                        pe.wait_ge(t_lo, 2 * step(L, h, 2 * G + 2))
                    dst = ps[:, 6 + G // 2, (G % 2) * 256:(G % 2 + 1) * 256]
                    for c in range(4 * part, 4 * part + 4):
                        last = split_product(dst, vh[:, c, a * V_DIM:a * V_DIM + P], vl[:, c, a * V_DIM:a * V_DIM + P],
                                             pth[:, G % 2, c, :], ptl[:, G % 2, c, :], c == 0, c == 7)
                    if part == 1:
                        last.then_inc(pv_out, 1)

                def variances(h, a, t):
                    pe.wait_ge(o_copy, (L * HEADS + h) * 2 + t + 1)
                    nc.tensor.matmul(ps[:, 6 + t, :], cst[:, 3 + a, :], sq[:, 0, :], start=True, stop=True).then_inc(o_var, 1)

                def head(h, a, first=False, last=False):
                    for s in range(STEPS):
                        transposes(h, s, first, s == 4 and not last)
                        if s + 2 < STEPS:
                            scores(h, a, s + 2)
                        elif not last:
                            scores(h + 1, 1 - a, s + 2 - STEPS)
                        if s in PIECES and not last:
                            make, t, bank = PIECES[s]
                            bank_free(h, s, first)
                            make(h + 1, 1 - a, t, bank)
                        if s == 3 and not first:
                            variances(h - 1, 1 - a, 1)
                        if s == 7:
                            variances(h, a, 0)
                        if s >= 2:
                            H = L * HEADS + h
                            if s == 2 and last:
                                pe.wait_ge(o_ln, H * 2 - 1)
                            if s == 2 and not last:
                                pe.wait_ge(k_lo, H * 2 + 4)
                            if s == 6 and last:
                                pe.wait_ge(o_ln, H * 2)
                            if s == 6 and not last:
                                pe.wait_ge(q_f, H * 2 + 4)
                            values(h, a, (s - 2) // 2, s % 2)
                        elif not first:
                            values(h - 1, 1 - a, 3, s)

                pe.wait_ge(lr_lo, L * 10 + 2)
                keys_and_values(0, 0, 0, 0)
                pe.wait_ge(lr_lo, L * 10 + 4)
                keys_and_values(0, 0, 1, 1)
                pe.wait_ge(lr_lo, L * 10 + 7)
                queries(0, 0, 0, 2)
                conv_stat(CHUNKS - 1, 0)
                conv_stat(CHUNKS - 1, 1)
                values_by_token(0, 0, 0, 3)
                pe.wait_ge(lr_lo, L * 10 + 10)
                queries(0, 0, 1, 6)
                pe.wait_ge(v_ones, L * 2 + 2)
                scores(0, 0, 0)
                scores(0, 0, 1)
                head(0, 0, first=True)
                head(1, 1)
                with pe.Fori(1, PAIRS - 1) as j:
                    head(2 * j, 0)
                    head(2 * j + 1, 1)
                head(HEADS - 2, 0)
                head(HEADS - 1, 1, last=True)
                values(HEADS - 1, 1, 3, 0)
                values(HEADS - 1, 1, 3, 1)

                def mix_part(n, order, start, stop):
                    m, t = OUT_OUTS[n]
                    for i, k in enumerate(order):
                        slot = (O_AT + m) % SLOTS
                        last = split_product(ps[:, n % 4, :], wh[:, slot, k, :], wl[:, slot, k, :],
                                             hh[:, k, hs(t)], hl[:, k, hs(t)], start and i == 0, stop and i == len(order) - 1)
                    return last

                for n in range(4):
                    unit_ready(L, O_AT + n)
                    if n == 0:
                        pe.wait_ge(mix_in, (L + 1) * 160)
                    mix_part(n, (4, 7, 0, 1, 2), True, False)
                    if n == 0:
                        variances(HEADS - 1, 1, 1)
                pe.wait_ge(mix_56, (L + 1) * 64)
                for n in range(4):
                    mix_part(n, (5, 6), False, False)
                pe.wait_ge(mix_last, (L + 1) * 32)
                for n in range(4):
                    mix_part(n, (3,), False, True).then_inc(mix_out, 1)
                for n in range(4, len(OUT_OUTS)):
                    m, t = OUT_OUTS[n]
                    if t == 0:
                        unit_ready(L, O_AT + m)
                    pe.wait_ge(mix_copy, L * 16 + n - 3)
                    mix_part(n, range(DC), True, True).then_inc(mix_out, 1)
                    if n == 12:
                        post_stats(L, 0, 0)
                post_stats(L, 0, 1)

                def up(g, t, ready=None):
                    for i in range(2):
                        n = 2 * t + i
                        if t == 0:
                            unit_ready(L, M_AT + i, g)
                        if not isinstance(g, int):
                            pe.wait_ge(up_v, L * 4 * GROUPS + (g - 1) * 4 + n + 1)
                        unit_output(n, (M_AT + i) % SLOTS, t, ready).then_inc(up_out, 1)
                        ready = None

                def down(g, t, banks=4, first=False, between={}):
                    pe.wait_ge(up_lo, L * 4 * GROUPS + g * 4 + 2 * t + 2)
                    for m in range(DC):
                        if t == 0 and m % 4 == 0:
                            unit_ready(L, M_AT + 2 + m // 4, g)
                        before = L * 16 * GROUPS + g * 16 + t * 8 + m
                        if m >= banks or (banks == 4 and not first):
                            pe.wait_ge(down_add, before - banks + 1)
                        elif not first:
                            pe.wait_ge(down_add, before - m)
                        two_tiles(4 + m % banks, (M_AT + 2 + m // 4) % SLOTS, m, t).then_inc(down_out, 1)
                        if m in between:
                            between[m]()

                R = pre_at(L, 0)
                for i in range(2):
                    unit_ready(L, M_AT + i)
                side_by_side([(i, (M_AT + i) % SLOTS) for i in range(2)], 0, pre_ready(R, 0), up_out)
                pre_stats(L, 0, 0)
                side_by_side([(2 + i, (M_AT + i) % SLOTS) for i in range(2)], 1, pre_ready(R, 1), up_out)
                pre_stats(L, 0, 1)
                pe.wait_ge(pre_ln, R * 2 + 2)
                down(0, 0, first=True)
                with pe.Fori(1, GROUPS) as g:
                    up(g, 0)
                    down(g - 1, 1)
                    up(g, 1)
                    down(g, 0)
                down(GROUPS - 1, 1, banks=2, between={4: lambda: post_stats(L, 1, 0)})

                def embed(t, ms):
                    for m in ms:
                        if t == 0 and m % 4 == 0:
                            unit_ready(L, E_AT + m // 4)
                        n = t * 8 + m
                        if n in (8, 9):
                            pe.wait_ge(gate_z, L * 16 + n - 7)
                        elif n >= 4:
                            pe.wait_ge(e_copy, L * 16 + n - 3)
                        two_tiles(m % 4, (E_AT + m // 4) % SLOTS, m, t).then_inc(e_out, 1)

                def gate(n):
                    m, t = GATE_OUTS[n]
                    if t == 0:
                        unit_ready(L, G_AT + m)
                    bank = n % 4 if n >= 4 else n % 2
                    if n < 4:
                        pe.wait_ge(e_copy, L * 16 + 13 + n - 2)
                    elif n < 6:
                        pe.wait_ge(gate_z, L * 16 + n - 1)
                    elif n < 8:
                        pe.wait_ge(e_copy, L * 16 + 9 + n)
                    else:
                        pe.wait_ge(gate_z, L * 16 + n - 3)
                    ready = pre_ready(pre_at(L, 1), t) if n == 2 else None
                    unit_output(bank, (G_AT + m) % SLOTS, t, ready).then_inc(gate_out, 1)

                pe.wait_ge(stage_lo, (L + 1) * STAGES)
                embed(0, range(8))
                post_stats(L, 1, 1)
                for n in range(2):
                    unit_ready(L, G_AT + n)
                    pe.wait_ge(e_copy, L * 16 + 5 + n)
                side_by_side([(n, (G_AT + n) % SLOTS) for n in range(2)], 0, pre_ready(pre_at(L, 1), 0), gate_out)
                pre_stats(L, 1, 0)
                pe.wait_ge(stage_lo, (L + 1) * STAGES + 1)
                embed(1, range(8))
                gate(2)
                pre_stats(L, 1, 1)
                for n in range(3, 16):
                    gate(n)
                    if n == 12:
                        post_stats(L, 2, 0)
                post_stats(L, 2, 1)

        @block.scalar
        def _(act):
            def table_of_exp_and_ln():
                nc.scalar.add_instruction(mybir.InstLoadActFuncSet(
                    name=nc.get_next_instruction_name(), act_func_set_id=6, ins=[], outs=[],
                    engine=mybir.EngineType.Activation))

            def copy(dst, src, **more):
                return nc.scalar.activation(dst, src, ACT.Copy, **more)

            def split_unit(L, w, g=0):
                act.wait_ge(w_in[w % RAW], (L * (UNITS // RAW) + g * (4 // RAW) + w // RAW) * 16 + 16)
                if w >= SLOTS:
                    act.wait_ge(*slot_free(L, w, g))
                copy(wh[:, w % SLOTS, :, :].rearrange("p k m -> p (k m)"), raw[:, w % RAW, :]).then_inc(w_hi, 1)

            def split_stage(L, k, dst):
                act.wait_ge(stage_in, (L * STAGES + k) * 16 + 16)
                copy(dst, stage[:, 0:dst.shape[1]]).then_inc(stage_hi, 1)

            def square(L, e, src):
                k = sum_number(e)
                if is_first(e):
                    dst = sum_of(e)
                else:
                    if L is not None or k >= 2:
                        act.wait_ge(summed, sum_at(L, e) - 2)
                    dst = sq[:, k % 2, :]
                nc.scalar.activation(dst, src, ACT.Square).then_inc(squared, 1)

            def split_head(L, h, a):
                split_stage(L, h, head_unit(a, 0).rearrange("p k m -> p (k m)"))

            def factor(dst, bank, width, stat, ln, r, count, bias=eps, part=slice(None)):
                act.wait_ge(stat, count)
                more = {} if bias is None else {"bias": bias[:, :]}
                nc.scalar.activation(dst, ps[part, bank, :], ACT.Ln, scale=1.0 / width, **more).then_inc(ln, 1)
                act.wait_ge(ln, count)
                nc.scalar.activation(dst, dst, ACT.Exp, scale=-0.5).then_inc(r, 1)

            def pre_factor(L, k, t):
                factor(rpre[:, t, :], 7, D, pre_stat, pre_ln, pre_r, pre_at(L, k) * 2 + t + 1)

            def post_factor(L, k, t):
                factor(accy[:, t, :], 6, D, post_stat, post_ln, post_r, post_at(L, k) * 2 + t + 1)

            def pre_chunk(L, k, t, c):
                g_at = G_FIRST if L is None else G_PRE[k]
                if L is None:
                    act.wait_ge(x_first[2 * t + c // 4], 16)
                else:
                    act.wait_ge(x_new, post_at(L, k) * 16 + t * 8 + c + 1)
                copy(hh[:, c, hs(t)], x[:, t, c, :], scale=gv[:, g_at + c:g_at + c + 1]).then_inc(pre_hi, 1)
                square(L, ("pre", k, t, c), x[:, t, c, :])

            table_of_exp_and_ln()
            act.wait_ge(eps_set, 1)
            for t in range(2):
                for c in range(DC):
                    if t == 0 and c % 4 == 0:
                        split_unit(0, c // 2)
                        split_unit(0, c // 2 + 1)
                    if t == 0 and c == 0:
                        act.wait_ge(const_in, 32)
                    pre_chunk(None, -1, t, c)
            with act.Fori(0, DEPTH) as L:
                factor(rpre[:, 0, :], 7, D, pre_stat, pre_ln, pre_r, pre_at(L, -1) * 2 + 1)

                for n in range(len(IN_OUTS)):
                    u, t = IN_OUTS[n] if n < len(IN_OUTS) else (None, None)
                    kind, j = IN_KIND[u] if u is not None else (None, None)
                    if n == 9:
                        act.wait_ge(x_stored[0], L * 32 + 32)
                    if n == 18:
                        act.wait_ge(x_stored[1], L * 32 + 32)
                        act.wait_ge(pre_lo, pre_at(L, -1) * 16 + 16)
                    if kind == "C":
                        act.wait_ge(in_out, L * 36 + n + 1)
                        if j:
                            act.wait_ge(u_raw, L * 8 + 2 * (j - 1) + t + 1)
                        copy(cc[:, hs(t)], ps[:, n % 4, :]).then_inc(in_act, 1)
                    if kind == "B":
                        act.wait_ge(in_out, L * 36 + n + 1)
                        if j >= 2:
                            act.wait_ge(cv_raw, L * 4 + j - 1)
                        copy(bb[:, j % 2, hs(t)], ps[:, n % 4, :]).then_inc(in_act, 1)
                    if n == 4:
                        factor(rpre[:, 1, :], 7, D, pre_stat, pre_ln, pre_r, pre_at(L, -1) * 2 + 2)
                    if kind == "kr":
                        act.wait_ge(kr_f, L * 2 + t + 1)
                        for a in range(2):
                            copy(kh[NOPE:P, a, hs(t)], kr[NOPE:P, :]).then_inc(kr_hi, 1)
                    for i in range(4):
                        if LF_AT[i] == n:
                            rank = KV_RANK if i % 2 else Q_RANK
                            factor(accy[:, i % 2, :], 6, rank, lr_stat, lr_ln, lr_r, L * 4 + i + 1)
                    for i in range(4):
                        if LSQ_AT[i] == n:
                            if i == 0:
                                act.wait_ge(in_dve, L * 12 + outputs_of(BY_DVE, 13))
                            if i >= 2:
                                act.wait_ge(lr_y, L * 10 + (3, 5)[i - 2])
                            for c in LORA[i % 2]:
                                square(L, ("lora", i, 0, c), zr[:, c, hs(i // 2)])
                    for j in range(CHUNKS - 1):
                        if MULT_AT[j] + 1 == n:
                            for t2 in range(2):
                                act.wait_ge(cv_done, L * 8 + 2 * j + t2 + 1)
                                nc.scalar.activation(cvs[:, t2, :], cv[:, hs(t2)], ACT.Square).then_inc(cv_sq, 1)
                        if CSTAT_AT[j] + 1 == n:
                            for t2 in range(2):
                                factor(cvr[:, t2, :], 4 + t2, 64, cv_stat, cv_ln, cv_r, L * 8 + 2 * j + t2 + 1)
                        if CY_AT[j] + 1 == n:
                            if j:
                                act.wait_ge(mix_stored, L * MIX_STORED + 32 * j)
                            for t2 in range(2):
                                act.wait_ge(cv_y, L * 8 + 2 * j + t2 + 1)
                                copy(cyh[:, hs(t2)], cv[:, hs(t2)]).then_inc(cv_hi, 1)
                    if t == 1 and u + SLOTS < IN_UNITS:
                        split_unit(L, u + SLOTS)
                    if n == HEAD_AT:
                        act.wait_ge(*last_read(L, IN_UNITS - SLOTS))
                        split_head(L, 0, 0)

                def latents(a, b):
                    for c, t in LATENTS[a:b]:
                        copy(hh[:, c, hs(t)], zr[:, c, hs(t)]).then_inc(lr_hi, 1)

                def keys_and_values(h, a, t, bank):
                    H = L * HEADS + h
                    act.wait_ge(kv_out, H * 2 + t + 1)
                    copy(accy[:, t, :], ps[:, bank, :]).then_inc(v_f, 1)
                    copy(kh[0:NOPE, a, hs(t)], ps[0:NOPE, bank, :]).then_inc(k_hi, 1)

                def queries(h, a, t, bank):
                    act.wait_ge(q_f, (L * HEADS + h) * 2 + t + 1)
                    copy(hh[:, HA + a, hs(t)], (tmp, xacc)[t][:, :]).then_inc(q_hi, 1)

                def values_by_token(h, a, t, bank):
                    act.wait_ge(v_out, L * HEADS + h + 1)
                    copy(vh[:, :, 2 * a * V_DIM:(2 * a + 1) * V_DIM],
                         ps[:, bank, :].rearrange("p (c d) -> p c d", c=STEPS)).then_inc(v_hi, 1)

                PIECES = {0: (keys_and_values, 0, 6), 1: (keys_and_values, 1, 6), 3: (values_by_token, 0, 5),
                          4: (queries, 0, 7), 5: (queries, 1, 7)}

                def exponentials(h, s):
                    act.wait_ge(s_neg, step(L, h, s) + 1)
                    nc.scalar.activation(pr[:, s % 2, :], ps[:, 2 * (s % 2):2 * (s % 2) + 2, :].rearrange("p b n -> p (b n)"),
                                         ACT.Exp, bias=nm[:, s % 2:s % 2 + 1], scale=SCALE).then_inc(s_exp, 1)

                def high_of_transposed(h, s, first):
                    G = s // 2
                    for b in range(2):
                        act.wait_ge(t_out, 2 * step(L, h, s) + b + 1)
                        if first and s == 0:
                            act.wait_ge(mix_stored, L * MIX_STORED + 128)
                        if s % 2 == 0 and b == 0 and (G >= 2 or not first):
                            act.wait_ge(pv_out, (L * HEADS + h) * 4 + G - 1)
                        copy(pth[:, G % 2, 4 * b:4 * b + 4, (s % 2) * P:(s % 2 + 1) * P],
                             ps[:, 4 + b, :].rearrange("p (c q) -> p c q", c=4)).then_inc(t_hi, 1)

                def outputs(h, a, t):
                    O = (L * HEADS + h) * 2 + t
                    act.wait_ge(pv_out, 2 * O + 2)
                    act.wait_ge(o_lo, O + 1)
                    nc.scalar.activation(sq[:, 0, :], ps[:, 6 + t, :], ACT.Square).then_inc(o_sq, 1)
                    copy(of[rows(a), :], ps[rows(a), 6 + t, :]).then_inc(o_copy, 1)

                def output_factor(h, a, t):
                    factor(sq[rows(a), 1, :], 6 + t, V_DIM, o_var, o_ln, o_r, (L * HEADS + h) * 2 + t + 1, None, rows(a))

                def high_of_output(h, a, t):
                    O = (L * HEADS + h) * 2 + t
                    act.wait_ge(o_y, O + 1)
                    act.wait_ge(mix_stored, L * MIX_STORED + 128 + (h * 2 + t) * 32)
                    copy(yh[rows(a), :], of[rows(a), :]).then_inc(o_hi, 1)

                def head(h, a, first=False, last=False):
                    for s in range(STEPS):
                        high_of_transposed(h, s, first)
                        if s + 1 < STEPS:
                            exponentials(h, s + 1)
                        elif not last:
                            exponentials(h + 1, 0)
                        if s in PIECES and not last:
                            make, t, bank = PIECES[s]
                            make(h + 1, 1 - a, t, bank)
                        if not first:
                            if s == 0:
                                high_of_output(h - 1, 1 - a, 0)
                            if s == 2:
                                outputs(h - 1, 1 - a, 1)
                            if s == 3:
                                output_factor(h - 1, 1 - a, 1)
                            if s == 4:
                                high_of_output(h - 1, 1 - a, 1)
                        if s == 6:
                            outputs(h, a, 0)
                            if a == 0 and not (isinstance(h, int) and h == HEADS - 2):
                                split_head(L, h + 2, a)
                            elif a == 1 and not last:
                                split_head(L, h + 2, a)
                            if last:
                                split_unit(L, O_AT + 1)
                        if s == 7:
                            output_factor(h, a, 0)
                            if last:
                                split_unit(L, O_AT + 2)
                                split_unit(L, O_AT + 3)
                        if last and s == 5:
                            split_unit(L, O_AT)

                act.wait_ge(in_out, L * 36 + 36)
                act.wait_ge(lr_y, L * 10 + 10)
                latents(0, 10)
                keys_and_values(0, 0, 0, 0)
                keys_and_values(0, 0, 1, 1)
                for t in range(2):
                    act.wait_ge(cv_done, L * 8 + 6 + t + 1)
                    nc.scalar.activation(cvs[:, t, :], cv[:, hs(t)], ACT.Square).then_inc(cv_sq, 1)
                queries(0, 0, 0, 2)
                for t in range(2):
                    factor(cvr[:, t, :], 4 + t, 64, cv_stat, cv_ln, cv_r, L * 8 + 6 + t + 1)
                act.wait_ge(mix_stored, L * MIX_STORED + 96)
                for t in range(2):
                    act.wait_ge(cv_y, L * 8 + 6 + t + 1)
                    copy(cyh[:, hs(t)], cv[:, hs(t)]).then_inc(cv_hi, 1)
                values_by_token(0, 0, 0, 3)
                queries(0, 0, 1, 6)
                split_head(L, 1, 1)
                exponentials(0, 0)
                head(0, 0, first=True)
                head(1, 1)
                with act.Fori(1, PAIRS - 1) as j:
                    head(2 * j, 0)
                    head(2 * j + 1, 1)
                head(HEADS - 2, 0)
                head(HEADS - 1, 1, last=True)
                high_of_output(HEADS - 1, 1, 0)
                outputs(HEADS - 1, 1, 1)
                output_factor(HEADS - 1, 1, 1)
                high_of_output(HEADS - 1, 1, 1)

                for e in OUT_TAIL:
                    if e[0] == "out":
                        m, t = OUT_OUTS[e[1]]
                        act.wait_ge(mix_out, L * 16 + e[1] + 1)
                        if e[1] == 0:
                            act.wait_ge(mix_stored, (L + 1) * MIX_STORED)
                        copy(facc[:, t, m, :], ps[:, e[1] % 4, :]).then_inc(mix_copy, 1)
                        act.wait_ge(mix_copy, L * 16 + e[1] + 1)
                        square(L, ("post", 0, t, m), facc[:, t, m, :])
                        if t == 1:
                            split_unit(L, O_AT + m + SLOTS)
                    elif e[0] == "factor":
                        post_factor(L, 0, e[1])
                    else:
                        pre_chunk(L, *e[1:])
                        if e == ("pre", 0, 1, 3):
                            pre_factor(L, 0, 0)

                def hidden(g, t):
                    for i in range(2):
                        k = L * 4 * GROUPS + g * 4 + 2 * t + i
                        act.wait_ge(up_v, k + 1)
                        nc.scalar.activation(gh[:, i, hs(t)], accy[:, 1, :], ACT.Square).then_inc(up_hi, 1)
                        nc.scalar.activation(accy[:, 0, :], accy[:, 1, :], ACT.Square).then_inc(up_sq, 1)

                def split_two(g, at):
                    for i in range(2):
                        split_unit(L, M_AT + at + i, g)

                hidden(0, 0)
                pre_factor(L, 0, 1)
                hidden(0, 1)
                split_two(1, 0)
                with act.Fori(1, GROUPS) as g:
                    hidden(g, 0)
                    split_two(g, 2)
                    hidden(g, 1)
                    split_two(g + 1, 0)
                def embedding(t, c):
                    act.wait_ge(e_out, L * 16 + t * 8 + c + 1)
                    copy(facc[:, t, c, :], ps[:, c % 4, :]).then_inc(e_copy, 1)

                def gates(e, n):
                    m, t = GATE_OUTS[n]
                    if e == "gate":
                        act.wait_ge(gate_z, L * 16 + n + 1)
                        nc.scalar.activation(gate_of(n), gate_of(n), ACT.Sigmoid).then_inc(gate_s, 1)
                    if e == "use":
                        act.wait_ge(gate_y, L * 16 + n + 1)
                        square(L, ("post", 2, t, m), facc[:, t, m, :])
                    if e == "split" and t == 1:
                        split_unit(L, G_AT + m + SLOTS)

                for e in MLP_TAIL:
                    if e[0] == "p":
                        act.wait_ge(down_out, (L + 1) * 16 * GROUPS - 8 + 8 * e[1])
                        act.wait_ge(stage_in, (L * STAGES + HEADS + e[1]) * 16 + 16)
                        copy(gh[:, :, hs(e[1])], stage[:, :].rearrange("p (k n) -> p k n", k=2)).then_inc(stage_hi, 1)
                    elif e[0] == "sum":
                        t, c = e[1:]
                        act.wait_ge(down_add, (L + 1) * 16 * GROUPS - 16 + 8 * t + c + 1)
                        square(L, ("post", 1, t, c), facc[:, t, c, :])
                    elif e[0] == "unit":
                        split_unit(L, G_AT + e[1])
                    elif e[0] == "factor":
                        post_factor(L, 1, e[1])
                    elif e[0] == "pre_factor":
                        if e[1] == 1:
                            table_of_exp_and_ln()
                        pre_factor(L, 1, e[1])
                    elif e[0] == "embed":
                        embedding(*e[1:])
                    elif e[0] == "pre":
                        pre_chunk(L, *e[1:])
                    else:
                        gates(*e)
                for e in GATE_TAIL:
                    if e[0] in ("gate", "use", "split"):
                        gates(*e)
                    elif e[0] == "factor":
                        table_of_exp_and_ln()
                        post_factor(L, 2, e[1])
                    else:
                        pre_chunk(L, *e[1:])

        @block.vector
        def _(dve):
            V = nc.vector

            def low(dst, whole, high):
                return V.tensor_tensor(dst, whole, high.bitcast(f32), ALU.subtract)

            def split_unit(L, w, g=0):
                dve.wait_ge(w_hi, L * UNITS + g * 4 + w + 1)
                low(wl[:, w % SLOTS, :, :].rearrange("p k m -> p (k m)"), raw[:, w % RAW, :],
                    wh[:, w % SLOTS, :, :].rearrange("p k m -> p (k m)")).then_inc(w_lo, 1)

            def split_stage(L, k, dst, high):
                dve.wait_ge(stage_hi, L * STAGES + k + 1)
                low(dst, stage[:, 0:dst.shape[1]], high).then_inc(stage_lo, 1)

            def split_head(L, h, a):
                split_stage(L, h, head_unit(a, 1).rearrange("p k m -> p (k m)"), head_unit(a, 0).rearrange("p k m -> p (k m)"))

            def pre_low(L, k, t, c):
                g_at = G_FIRST if L is None else G_PRE[k]
                R = 0 if L is None else pre_at(L, k)
                dve.wait_ge(pre_hi, R * 16 + t * 8 + c + 1)
                V.scalar_tensor_tensor(hl[:, c, hs(t)], x[:, t, c, :], gv[:, g_at + c:g_at + c + 1],
                                       hh[:, c, hs(t)].bitcast(f32), ALU.mult, ALU.subtract).then_inc(pre_lo, 1)

            def residual_chunk(L, k, t, c):
                i = post_at(L, k) * 16 + t * 8 + c + 1
                f, xc = facc[:, t, c, :], x[:, t, c, :]
                V.scalar_tensor_tensor(f, f, gv[:, G_POST[k] + c:G_POST[k] + c + 1], accy[:, t, :],
                                       ALU.mult, ALU.mult).then_inc(post_mul, 1)
                dve.wait_ge(post_mul, i)
                V.tensor_tensor(xc, xc, f, ALU.add).then_inc(x_new, 1)
                if c:
                    pre_low(L, k, t, c - 1)
                if c == DC - 1:
                    pre_low(L, k, t, c)

            V.memset(eps[:, :], EPS).then_inc(eps_set, 1)
            V.memset(mx[:, :], 0.0).then_inc(w_lo, RAW)
            V.memset(nm[:, 0:1], 0.0).then_inc(stage_lo, 1)
            V.memset(nm[:, 1:2], 0.0).then_inc(o_lo, 1)
            for t in range(2):
                for c in range(DC):
                    if t == 0 and c % 4 == 0:
                        split_unit(0, c // 2)
                        split_unit(0, c // 2 + 1)
                    if t == 0 and c == 0:
                        dve.wait_ge(const_in, 32)
                    pre_low(None, -1, t, c)
            with dve.Fori(0, DEPTH) as L:

                def conv_taps(j):
                    dve.wait_ge(u_done, L * 8 + 2 * j + 2)
                    if j:
                        dve.wait_ge(cv_lo, L * 8 + 2 * j)
                    w = [gv[:, G_TAP + 3 * j + k:G_TAP + 3 * j + k + 1] for k in range(3)]
                    V.tensor_scalar(cv[:, :], uu[:, 1:SEQ + 1], w[1], None, ALU.mult).then_inc(tap, 1)
                    for i, k in ((1, 0), (2, 2)):
                        dve.wait_ge(tap, L * 12 + 3 * j + i)
                        V.scalar_tensor_tensor(cv[:, :], uu[:, k:SEQ + k], w[k], cv[:, :], ALU.mult, ALU.add).then_inc(tap, 1)

                def conv_gate(j):
                    dve.wait_ge(tap, L * 12 + 3 * j + 3)
                    dve.wait_ge(in_act, L * 16 + outputs_of(BY_ACT, IN_OUTS.index((IN_KIND.index(("B", j)), 1)) + 1))
                    V.tensor_tensor(cv[:, :], cv[:, :], bb[:, j % 2, :], ALU.mult).then_inc(cv_raw, 1)

                def conv_norm(j):
                    for t in range(2):
                        dve.wait_ge(cv_r, L * 8 + 2 * j + t + 1)
                        V.scalar_tensor_tensor(cv[:, hs(t)], cv[:, hs(t)], gv[:, G_CONV + j:G_CONV + j + 1],
                                               cvr[:, t, :], ALU.mult, ALU.mult).then_inc(cv_y, 1)

                def conv_low(j):
                    for t in range(2):
                        dve.wait_ge(cv_hi, L * 8 + 2 * j + t + 1)
                        low(cyl[:, hs(t)], cv[:, hs(t)], cyh[:, hs(t)]).then_inc(cv_lo, 1)

                for n in range(len(IN_OUTS)):
                    u, t = IN_OUTS[n]
                    kind, j = IN_KIND[u]
                    if n in (0, 4):
                        dve.wait_ge(pre_r, pre_at(L, -1) * 2 + t + 1)
                    if n == 8:
                        dve.wait_ge(x_stored[0], L * 32 + 32)
                    if n == 10:
                        dve.wait_ge(pads, L * 2 + 2)
                    if n == 15:
                        dve.wait_ge(gains_in, L * 16 + 16)
                    if n == 19:
                        dve.wait_ge(x_stored[1], L * 32 + 32)
                        dve.wait_ge(squared, square_at(L, SQUARES[0]) - 1)
                    if n == 26:
                        dve.wait_ge(tab_in, L * 16 + 16)
                    if kind not in BY_ACT:
                        dve.wait_ge(in_out, L * 36 + n + 1)
                    src = ps[:, n % 4, :]
                    if kind in ("q", "kv"):
                        V.tensor_tensor(zr[:, j + (QC if kind == "kv" else 0), hs(t)], src, rpre[:, t, :], ALU.mult).then_inc(in_dve, 1)
                    if kind == "u":
                        dve.wait_ge(in_act, L * 16 + outputs_of(BY_ACT, n))
                        V.tensor_tensor(uu[:, 1 + t * HALF:1 + (t + 1) * HALF], src, cc[:, hs(t)], ALU.mult).then_inc(u_raw, 1)
                    if kind == "kr":
                        one, both = slice(NOPE, QK), slice(NOPE, P)
                        if t == 1:
                            dve.wait_ge(kr_lo, L * 4 + 2)
                            dve.wait_ge(kr_hi, L * 4 + 2)
                        V.tensor_tensor(sq[one, 0, :], ps[QK:P, n % 4, :], tab[QK:P, hs(t)], ALU.mult)
                        V.tensor_tensor(kr[one, :], ps[one, n % 4, :], tab[one, hs(t)], ALU.mult).then_inc(kr_cos, 1)
                        dve.wait_ge(kr_cos, L * 2 + t + 1)
                        V.tensor_tensor(kr[QK:P, :], kr[one, :], sq[one, 0, :], ALU.add).then_inc(kr_sum, 1)
                        dve.wait_ge(kr_sum, L * 2 + t + 1)
                        V.tensor_tensor(kr[one, :], kr[one, :], sq[one, 0, :], ALU.add).then_inc(in_dve, 1)
                        dve.wait_ge(in_dve, L * 12 + outputs_of(BY_DVE, n + 1))
                        V.tensor_tensor(kr[both, :], kr[both, :], rpre[both, t, :], ALU.mult).then_inc(kr_f, 1)
                        for a in range(2):
                            dve.wait_ge(kr_hi, L * 4 + 2 * t + a + 1)
                            low(kl[both, a, hs(t)], kr[both, :], kh[both, a, hs(t)]).then_inc(kr_lo, 1)
                    for i in range(4):
                        if LY_AT[i] == n:
                            dve.wait_ge(lr_r, L * 4 + i + 1)
                            for c in LORA[i % 2]:
                                z = zr[:, c, hs(i // 2)]
                                V.scalar_tensor_tensor(z, z, gv[:, G_Q + c:G_Q + c + 1], accy[:, i % 2, :],
                                                       ALU.mult, ALU.mult).then_inc(lr_y, 1)
                    for j in range(CHUNKS - 1):
                        if CLO_AT[j] + 1 == n:
                            conv_low(j)
                        if CY_AT[j] == n:
                            conv_norm(j)
                    for j in range(CHUNKS - 1):
                        if MULT_AT[j] == n:
                            conv_taps(j)
                            conv_gate(j)
                    if t == 1 and u + SLOTS < IN_UNITS:
                        split_unit(L, u + SLOTS)
                    if n == HEAD_AT:
                        split_head(L, 0, 0)

                def latents(a, b):
                    for i in range(a, b):
                        c, t = LATENTS[i]
                        dve.wait_ge(lr_hi, L * 10 + i + 1)
                        low(hl[:, c, hs(t)], zr[:, c, hs(t)], hh[:, c, hs(t)]).then_inc(lr_lo, 1)

                def keys_and_values(h, a, t, bank):
                    dve.wait_ge(k_hi, (L * HEADS + h) * 2 + t + 1)
                    low(kl[0:NOPE, a, hs(t)], ps[0:NOPE, bank, :], kh[0:NOPE, a, hs(t)]).then_inc(k_lo, 1)

                def queries(h, a, t, bank):
                    dve.wait_ge(q_out, (L * HEADS + h) * 2 + t + 1)
                    V.tensor_tensor((tmp, xacc)[t][:, :], ps[:, bank, :], tab[:, hs(t)], ALU.mult).then_inc(q_f, 1)

                def low_of_queries(h, a, t):
                    dve.wait_ge(q_hi, (L * HEADS + h) * 2 + t + 1)
                    low(hl[:, HA + a, hs(t)], (tmp, xacc)[t][:, :], hh[:, HA + a, hs(t)]).then_inc(q_lo, 1)

                def values_by_token(h, a, t, bank):
                    at = (slice(None), slice(None), slice(2 * a * V_DIM, (2 * a + 1) * V_DIM))
                    dve.wait_ge(v_hi, L * HEADS + h + 1)
                    low(vl[at], ps[:, bank, :].rearrange("p (c d) -> p c d", c=STEPS), vh[at]).then_inc(v_lo, 1)

                PIECES = {0: (keys_and_values, 0, 6), 1: (keys_and_values, 1, 6), 3: (values_by_token, 0, 5),
                          4: (queries, 0, 7), 5: (queries, 1, 7)}

                def maxima(h, s):
                    S = step(L, h, s)
                    dve.wait_ge(s_out, S + 1)
                    V.reduce_max(mx[:, s % 2:s % 2 + 1], ps[:, 2 * (s % 2):2 * (s % 2) + 2, :].rearrange("p b n -> p (b n)"),
                                 AX.X).then_inc(s_max, 1)
                    dve.wait_ge(s_max, S + 1)
                    V.tensor_scalar(nm[:, s % 2:s % 2 + 1], mx[:, s % 2:s % 2 + 1], -SCALE, None, ALU.mult).then_inc(s_neg, 1)

                def low_of_transposed(h, s):
                    G = s // 2
                    for b in range(2):
                        dve.wait_ge(t_hi, 2 * step(L, h, s) + b + 1)
                        at = (slice(None), G % 2, slice(4 * b, 4 * b + 4), slice((s % 2) * P, (s % 2 + 1) * P))
                        V.tensor_tensor(ptl[at], ps[:, 4 + b, :].rearrange("p (c q) -> p c q", c=4),
                                        pth[at].bitcast(f32), ALU.subtract).then_inc(t_lo, 1)

                def output(h, a, t, j):
                    dve.wait_ge(o_r, (L * HEADS + h) * 2 + t + 1)
                    V.scalar_tensor_tensor(of[rows(a), :], of[rows(a), :], gatt[rows(a), bass.ds(j, 1)],
                                           sq[rows(a), 1, :], ALU.mult, ALU.mult).then_inc(o_y, 1)

                def low_of_output(h, a, t):
                    dve.wait_ge(o_hi, (L * HEADS + h) * 2 + t + 1)
                    low(yl[rows(a), :], of[rows(a), :], yh[rows(a), :]).then_inc(o_lo, 1)

                def head(j, a, first=False, last=False):
                    h = 2 * j + a
                    before = j if a else j - 1
                    for s in range(STEPS):
                        low_of_transposed(h, s)
                        if s + 2 < STEPS:
                            maxima(h, s + 2)
                        elif not last:
                            maxima(h + 1, s + 2 - STEPS)
                        if s in PIECES and not last:
                            make, t, bank = PIECES[s]
                            make(h + 1, 1 - a, t, bank)
                        if s in (5, 6) and not last:
                            low_of_queries(h + 1, 1 - a, s - 5)
                        if not first:
                            if s == 0:
                                output(h - 1, 1 - a, 0, before)
                            if s == 1:
                                low_of_output(h - 1, 1 - a, 0)
                            if s == 4:
                                output(h - 1, 1 - a, 1, before)
                            if s == 5:
                                low_of_output(h - 1, 1 - a, 1)
                        if s == 6 and not last and not (isinstance(h, int) and h == HEADS - 2):
                            split_head(L, h + 2, a)
                        if last and s == 5:
                            split_unit(L, O_AT)
                        if last and s == 6:
                            split_unit(L, O_AT + 1)
                        if last and s == 7:
                            split_unit(L, O_AT + 2)
                            split_unit(L, O_AT + 3)

                conv_taps(CHUNKS - 1)
                latents(0, 7)
                conv_gate(CHUNKS - 1)
                latents(7, 10)
                keys_and_values(0, 0, 0, 0)
                keys_and_values(0, 0, 1, 1)
                queries(0, 0, 0, 2)
                low_of_queries(0, 0, 0)
                conv_norm(CHUNKS - 1)
                conv_low(CHUNKS - 1)
                values_by_token(0, 0, 0, 3)
                queries(0, 0, 1, 6)
                low_of_queries(0, 0, 1)
                maxima(0, 0)
                maxima(0, 1)
                split_head(L, 1, 1)
                head(0, 0, first=True)
                head(0, 1)
                with dve.Fori(1, PAIRS - 1) as j:
                    head(j, 0)
                    head(j, 1)
                head(PAIRS - 1, 0)
                head(PAIRS - 1, 1, last=True)
                output(HEADS - 1, 1, 0, PAIRS - 1)
                low_of_output(HEADS - 1, 1, 0)
                output(HEADS - 1, 1, 1, PAIRS - 1)
                low_of_output(HEADS - 1, 1, 1)

                for e in OUT_TAIL_DVE:
                    if e[0] == "out":
                        m, t = OUT_OUTS[e[1]]
                        if t == 1:
                            split_unit(L, O_AT + m + SLOTS)
                    elif e[0] == "factor":
                        dve.wait_ge(x_back[e[1]], L * 16 + 16)
                        dve.wait_ge(post_r, post_at(L, 0) * 2 + e[1] + 1)
                    else:
                        residual_chunk(L, *e[1:])

                def hidden(g, t):
                    for i in range(2):
                        k = L * 4 * GROUPS + g * 4 + 2 * t + i
                        dve.wait_ge(up_out, k + 1)
                        V.scalar_tensor_tensor(accy[:, 1, :], ps[:, 2 * t + i, :], 0.0, rpre[:, t, :], ALU.max, ALU.mult).then_inc(up_v, 1)
                        dve.wait_ge(up_sq, k + 1)
                        low(gl[:, i, hs(t)], accy[:, 0, :], gh[:, i, hs(t)]).then_inc(up_lo, 1)

                def add_one(g, t, m, banks):
                    dve.wait_ge(down_out, L * 16 * GROUPS + g * 16 + t * 8 + m + 1)
                    f = facc[:, t, m, :]
                    V.tensor_tensor(f, f, ps[:, 4 + m % banks, :], ALU.add).then_inc(down_add, 1)

                def add(g, t):
                    for m in range(DC):
                        add_one(g, t, m, 4)

                def split_two(g, at):
                    for i in range(2):
                        split_unit(L, M_AT + at + i, g)

                dve.wait_ge(pre_r, pre_at(L, 0) * 2 + 1)
                hidden(0, 0)
                dve.wait_ge(pre_r, pre_at(L, 0) * 2 + 2)
                hidden(0, 1)
                split_two(1, 0)
                for m in range(DC):
                    dve.wait_ge(down_out, L * 16 * GROUPS + m + 1)
                    if m == DC - 1:
                        dve.wait_ge(f_zero, L + 1)
                    V.tensor_copy(facc[:, 0, m, :], ps[:, 4 + m % 4, :]).then_inc(down_add, 1)
                with dve.Fori(1, GROUPS) as g:
                    hidden(g, 0)
                    add(g - 1, 1)
                    split_two(g, 2)
                    hidden(g, 1)
                    for m in range(DC):
                        add_one(g, 0, m, 4)
                        if m in (1, 3):
                            split_unit(L, M_AT + m // 2, g + 1)

                def gates(e, n):
                    m, t = GATE_OUTS[n]
                    if e == "gate":
                        if n in (0, 2):
                            dve.wait_ge(pre_r, pre_at(L, 1) * 2 + t + 1)
                        dve.wait_ge(gate_out, L * 16 + n + 1)
                        if n:
                            dve.wait_ge(gate_y, L * 16 + n)
                        V.tensor_tensor(gate_of(n), ps[:, n % 4 if n >= 4 else n % 2, :], rpre[:, t, :], ALU.mult).then_inc(gate_z, 1)
                    if e == "use":
                        dve.wait_ge(gate_s, L * 16 + n + 1)
                        dve.wait_ge(e_copy, L * 16 + t * 8 + m + 1)
                        f = facc[:, t, m, :]
                        V.tensor_tensor(f, f, gate_of(n), ALU.mult).then_inc(gate_y, 1)
                    if e == "split" and t == 1:
                        split_unit(L, G_AT + m + SLOTS)

                for e in MLP_TAIL_DVE:
                    if e[0] == "p":
                        dve.wait_ge(stage_hi, L * STAGES + HEADS + e[1] + 1)
                        low(gl[:, :, hs(e[1])], stage[:, :].rearrange("p (k n) -> p k n", k=2), gh[:, :, hs(e[1])]).then_inc(stage_lo, 1)
                    elif e[0] == "add":
                        add_one(GROUPS - 1, 1, e[1], 2)
                    elif e[0] == "unit":
                        split_unit(L, G_AT + e[1])
                    elif e[0] == "factor":
                        dve.wait_ge(post_r, post_at(L, 1) * 2 + e[1] + 1)
                    elif e[0] == "pre":
                        residual_chunk(L, *e[1:])
                    else:
                        gates(*e)
                for e in GATE_TAIL_DVE:
                    if e[0] in ("gate", "use", "split"):
                        gates(*e)
                    elif e[0] == "factor":
                        dve.wait_ge(post_r, post_at(L, 2) * 2 + e[1] + 1)
                    else:
                        residual_chunk(L, *e[1:])

        @block.gpsimd
        def _(pool):
            def add_square(L, e):
                acc = sum_of(e)
                pool.wait_ge(squared, square_at(L, e))
                if L is not None or sum_number(e):
                    pool.wait_ge(summed, sum_at(L, e) - 1)
                nc.gpsimd.tensor_tensor(acc, acc, sq[:, sum_number(e) % 2, :], ALU.add).then_inc(summed, 1)

            pool.wait_ge(eps_set, 1)
            for e in AHEAD:
                if not is_first(e):
                    add_square(None, e)
            with pool.Fori(0, DEPTH) as L:
                pool.wait_ge(x_stored[0], L * 32 + 32)
                pool.wait_ge(pre_lo, pre_at(L, -1) * 16 + 8)
                nc.gpsimd.tensor_tensor(uu[:, 0:1], eps[:, :], eps[:, :], ALU.subtract).then_inc(pads, 1)
                nc.gpsimd.tensor_tensor(uu[:, SEQ + 1:SEQ + 2], eps[:, :], eps[:, :], ALU.subtract).then_inc(pads, 1)
                for n in range(len(IN_OUTS)):
                    u, t = IN_OUTS[n]
                    kind, j = IN_KIND[u]
                    if kind == "u":
                        k = L * 8 + 2 * j + t + 1
                        piece = uu[:, 1 + t * HALF:1 + (t + 1) * HALF]
                        pool.wait_ge(u_raw, k)
                        nc.gpsimd.tensor_tensor(piece, piece, rpre[:, t, :], ALU.mult).then_inc(u_once, 1)
                        pool.wait_ge(u_once, k)
                        nc.gpsimd.tensor_tensor(piece, piece, rpre[:, t, :], ALU.mult).then_inc(u_done, 1)
                    for j in range(CHUNKS):
                        if MULT_AT[j] == n:
                            pool.wait_ge(cv_raw, L * 4 + j + 1)
                            for t2 in range(2):
                                nc.gpsimd.tensor_tensor(cv[:, hs(t2)], cv[:, hs(t2)], rpre[:, t2, :], ALU.mult).then_inc(cv_done, 1)
                    for i in range(4):
                        if LSQ_AT[i] == n:
                            for c in LORA[i % 2][1:]:
                                add_square(L, ("lora", i, 0, c))
                pool.wait_ge(lr_lo, L * 10 + 10)
                nc.gpsimd.tensor_tensor(carry[:, :], eps[:, :], eps[:, :], ALU.add)
                nc.gpsimd.memset(vh[:, :, V_DIM:2 * V_DIM].bitcast(f32), 1.0).then_inc(v_ones, 1)
                nc.gpsimd.memset(vl[:, :, V_DIM:2 * V_DIM].bitcast(f32), 0.0).then_inc(v_ones, 1)
                for e in SQUARES:
                    if e[0] == "lora":
                        continue
                    if not is_first(e):
                        add_square(L, e)
                    if e == ("pre", 0, 1, DC - 1):
                        t = 1
                        pool.wait_ge(x_new, post_at(L, 0) * 16 + t * 8 + 8)
                        nc.gpsimd.tensor_tensor(carry[:, :], eps[:, :], eps[:, :], ALU.add)
                        nc.gpsimd.memset(facc[:, t, :, :], 0.0).then_inc(f_zero, 1)


def kernel(**inputs):
    import concourse.bacc as _bacc
    from concourse.bass_utils import run_bass_kernel_spmd as _run

    a = {k: np.ascontiguousarray(v) for k, v in inputs.items()}

    def tiles(w, rows, cols):
        return np.stack([w[:, r:r + P][:, :, cols] for r in rows], axis=2)

    k_all = range(0, D, P)
    swap = np.r_[ROPE // 2:ROPE, 0:ROPE // 2]
    at_kr = Q_RANK + KV_RANK
    at_b = at_kr + ROPE
    starts = {"q": 0, "kv": Q_RANK, "B": at_b, "C": at_b + CONV, "u": at_b + 2 * CONV}
    units = []
    for kind, c in IN_KIND:
        if kind == "kr":
            kr = at_kr + np.arange(ROPE)
            cols = np.concatenate([kr, kr, kr, kr[swap]])
        else:
            cols = starts[kind] + c * P + np.arange(P)
        units.append(tiles(a["w_in"], k_all, cols))
    for m in range(DC):
        units.append(tiles(a["w_out"], k_all, m * P + np.arange(P)))
    for g in range(GROUPS):
        for i in range(2):
            units.append(tiles(a["w_mlp_up"], k_all, (2 * g + i) * P + np.arange(P)))
        for h in range(2):
            units.append(np.concatenate([tiles(a["w_mlp_down"], (2 * g * P, (2 * g + 1) * P), m * P + np.arange(P))
                                         for m in range(4 * h, 4 * h + 4)], axis=2))
    for h in range(2):
        units.append(np.concatenate([tiles(a["w_ple_proj"], (0, P), m * P + np.arange(P))
                                     for m in range(4 * h, 4 * h + 4)], axis=2))
    for m in range(DC):
        units.append(tiles(a["w_ple_gate"], k_all, m * P + np.arange(P)))
    w_units = np.stack(units, axis=1).reshape(DEPTH, UNITS, P, UNIT)
    w_units = np.ascontiguousarray(np.concatenate([w_units, np.roll(w_units, -1, axis=0)[:, :SLOTS]], axis=1))

    heads = []
    for h in range(HEADS):
        nope = h * QK + np.arange(NOPE)
        rope = h * QK + NOPE + np.arange(ROPE)
        q = tiles(a["w_q_b"], range(0, Q_RANK, P), np.concatenate([nope, rope, rope[swap]]))
        kv = tiles(a["w_kv_b"], range(0, KV_RANK, P), h * (NOPE + V_DIM) + np.arange(NOPE + V_DIM))
        heads.append(np.concatenate([q, kv], axis=2))
    w_head = np.ascontiguousarray(np.stack(heads, axis=1).reshape(DEPTH, HEADS, P, HEAD_UNIT))

    def columns(v):
        return v.reshape(DEPTH, -1, P).transpose(0, 2, 1)

    following = [(i + 1) % DEPTH for i in range(DEPTH)]
    taps = a["w_conv"].reshape(DEPTH, 3, CHUNKS, P).transpose(0, 3, 2, 1).reshape(DEPTH, P, 3 * CHUNKS)
    gains = np.ascontiguousarray(np.concatenate(
        [columns(a["g_q_a"]), columns(a["g_kv_a"]), columns(a["g_attn_out"]), columns(a["g_conv_out"]),
         columns(a["g_post_mix"]), columns(a["g_pre_mlp"]), columns(a["g_post_mlp"]), columns(a["g_pre_ple"]),
         columns(a["g_post_ple"]), columns(a["g_pre_mix"][following]), taps, columns(a["g_pre_mix"])], axis=2))
    assert gains.shape[2] == G_ALL

    inv_freq = 1.0 / (np.float32(10000.0) ** (np.arange(0, ROPE, 2, dtype=np.float32) / np.float32(ROPE)))
    angle = inv_freq.astype(np.float32)[:, None] * np.arange(SEQ, dtype=np.float32)[None, :]
    cos, sin = np.cos(angle).astype(np.float32), np.sin(angle).astype(np.float32)
    table = np.concatenate([np.ones((NOPE, SEQ), np.float32), cos, cos, -sin, sin], axis=0)
    consts = np.zeros((P, 5, P), np.float32)
    consts[:, 0] = np.eye(P)
    consts[:, 1] = 1.0
    for i in range(2):
        consts[64 * i:64 * i + 64, 2, 64 * i:64 * i + 64] = 1.0
        consts[64 * i:64 * i + 64, 3 + i, 64 * i:64 * i + 64] = 1.0
        consts[64 * (1 - i), 3 + i, 64 * i:64 * i + 64] = V_DIM * EPS

    arrays = {
        "x_in": np.ascontiguousarray(a["x"].reshape(SEQ, DC, P).transpose(2, 1, 0)),
        "w_units": w_units, "w_head": w_head,
        "p_in": np.ascontiguousarray(a["p"].reshape(DEPTH, 2, HALF, PLE // P, P).transpose(0, 1, 4, 3, 2)
                                     ).reshape(DEPTH, 2, P, UNIT),
        "gains": gains, "table": table, "consts": consts,
    }
    nc = _bacc.Bacc("TRN2", target_bir_lowering=False, num_devices=1)
    args = [nc.dram_tensor(k, v.shape, mybir.dt.from_np(v.dtype), kind="ExternalInput").ap() for k, v in arrays.items()]
    args.append(nc.dram_tensor("out", [P, DC, SEQ], mybir.dt.float32, kind="ExternalOutput").ap())
    encoder(nc, *args)
    r = _run(nc, [arrays], core_ids=[0])
    got = r.results[0]["out"]
    return np.ascontiguousarray(got.transpose(2, 1, 0)).reshape(1, SEQ, D)
```
